# Optimizing a Trainium2 kernel written in Bass

```python
import jax, jax.numpy as jnp
from jax import lax
import numpy as np

D_MODEL = 1024
BATCH = 1
SEQ = 1024
DEPTH = 1
DEC_BATCH = 8
DEC_SEQ = 4
PAST_LEN = 2048
PAGE_SIZE = 128

N_HEADS = 8
QK_NOPE = 64
QK_ROPE = 32
V_HEAD = 64
Q_RANK = 384
KV_RANK = 256
CONV_CH = 512
CONV_WIDTH = 31
D_ATT = N_HEADS * V_HEAD
D_MIX = D_ATT + CONV_CH
D_IN = Q_RANK + KV_RANK + QK_ROPE + 2 * CONV_CH
D_FF = 2816
PLE_DIM = 256
ROPE_BASE = 10000.0
EPS = 1e-6
Q_BLOCK = 128
SCALE = (QK_NOPE + QK_ROPE) ** -0.5
NEG_INF = -1e30

kernel_name = 'hymba_mla_conformer_macaron_ple_step'

def rmsnorm(x, g):
    xf = x.astype(jnp.float32)
    y = xf * lax.rsqrt(jnp.mean(xf * xf, axis=-1, keepdims=True) + EPS)
    return (y * g.astype(jnp.float32)).astype(x.dtype)

def layernorm(x, g, b):
    xf = x.astype(jnp.float32)
    mu = jnp.mean(xf, axis=-1, keepdims=True)
    var = jnp.mean(jnp.square(xf - mu), axis=-1, keepdims=True)
    y = (xf - mu) * lax.rsqrt(var + EPS)
    return (y * g.astype(jnp.float32) + b.astype(jnp.float32)).astype(x.dtype)

def rope(x, pos):
    half = QK_ROPE // 2
    inv = ROPE_BASE ** (-jnp.arange(half, dtype=jnp.float32) / half)
    ang = pos.astype(jnp.float32)[:, None] * inv[None, :]
    ang = ang.reshape(ang.shape[:1] + (1,) * (x.ndim - 3) + ang.shape[1:])
    cos, sin = jnp.cos(ang), jnp.sin(ang)
    x1 = x[..., :half].astype(jnp.float32)
    x2 = x[..., half:].astype(jnp.float32)
    return jnp.concatenate([x1 * cos - x2 * sin, x1 * sin + x2 * cos], axis=-1).astype(x.dtype)

def swiglu(x, wg, wu, wd):
    return (jax.nn.silu(x @ wg) * (x @ wu)) @ wd

def prompt_attention(q_nope, q_pe, ckv, kpe, w_uk, w_uv):
    B, T, H, _ = q_nope.shape
    k_nope = jnp.einsum('bsr,rhn->bshn', ckv, w_uk)
    v = jnp.einsum('bsr,rhv->bshv', ckv, w_uv)
    blk = Q_BLOCK if T % Q_BLOCK == 0 else T
    outs = []
    for i in range(T // blk):
        q0, q1 = i * blk, (i + 1) * blk
        s = (jnp.einsum('bthn,bshn->bhts', q_nope[:, q0:q1], k_nope[:, :q1])
             + jnp.einsum('bthp,bsp->bhts', q_pe[:, q0:q1], kpe[:, :q1]))
        s = s.astype(jnp.float32) * SCALE
        causal = jnp.arange(q0, q1)[:, None] >= jnp.arange(q1)[None, :]
        s = jnp.where(causal, s, NEG_INF)
        pr = jax.nn.softmax(s, axis=-1).astype(v.dtype)
        outs.append(jnp.einsum('bhts,bshv->bthv', pr, v[:, :q1]))
    return jnp.concatenate(outs, axis=1).reshape(B, T, H * V_HEAD)

def sample_attention(q_nope, q_pe, q_pos, ckv_all, kpe_all, w_uk, w_uv):
    B, T, H, _ = q_nope.shape
    q_abs = jnp.einsum('bthn,rhn->bthr', q_nope, w_uk)
    s = (jnp.einsum('bthr,bsr->bhts', q_abs, ckv_all)
         + jnp.einsum('bthp,bsp->bhts', q_pe, kpe_all))
    s = s.astype(jnp.float32) * SCALE
    k_pos = jnp.arange(ckv_all.shape[1])
    s = jnp.where(k_pos[None, :] <= q_pos[:, None], s, NEG_INF)
    pr = jax.nn.softmax(s, axis=-1).astype(ckv_all.dtype)
    o_lat = jnp.einsum('bhts,bsr->bthr', pr, ckv_all)
    return jnp.einsum('bthr,rhv->bthv', o_lat, w_uv).reshape(B, T, H * V_HEAD)

def token_mix(n, prm, q_pos, attend, conv_hist):
    z = n @ prm['w_in']
    o1, o2, o3 = Q_RANK, Q_RANK + KV_RANK, Q_RANK + KV_RANK + QK_ROPE
    cq, ckv_raw, kpe_raw, u = z[..., :o1], z[..., o1:o2], z[..., o2:o3], z[..., o3:]
    q = jnp.einsum('btr,rhd->bthd', rmsnorm(cq, prm['g_q']), prm['w_q_up'])
    q_nope = q[..., :QK_NOPE]
    q_pe = rope(q[..., QK_NOPE:], q_pos)
    ckv = rmsnorm(ckv_raw, prm['g_kv'])
    kpe = rope(kpe_raw, q_pos)
    att = attend(q_nope, q_pe, ckv, kpe)
    v = u[..., :CONV_CH] * jax.nn.sigmoid(u[..., CONV_CH:])
    v_ext = jnp.concatenate([conv_hist, v], axis=1)
    c = lax.conv_general_dilated(v_ext, prm['conv_w'][:, None, :], window_strides=(1,),
                                 padding='VALID', dimension_numbers=('NWC', 'WIO', 'NWC'),
                                 feature_group_count=CONV_CH) + prm['conv_b']
    c = jax.nn.silu(layernorm(c, prm['g_cn'], prm['b_cn']))
    out = jnp.concatenate([att, c], axis=-1) @ prm['w_o']
    return out, ckv, kpe, v_ext[:, -(CONV_WIDTH - 1):]

def layer(h, p, prm, q_pos, attend, conv_hist):
    h = h + 0.5 * swiglu(rmsnorm(h, prm['g_ff1']), prm['w1_gate'], prm['w1_up'], prm['w1_down'])
    mix, ckv, kpe, conv_state = token_mix(rmsnorm(h, prm['g_mix']), prm, q_pos, attend, conv_hist)
    h = h + mix
    h = h + 0.5 * swiglu(rmsnorm(h, prm['g_ff2']), prm['w2_gate'], prm['w2_up'], prm['w2_down'])
    gate = jax.nn.sigmoid(rmsnorm(h, prm['g_ple']) @ prm['w_pg'] + prm['b_pg'])
    h = h + gate * (p @ prm['w_pp'])
    return h, ckv, kpe, conv_state

def setup_inputs(seed: int = 0) -> dict:
    key = jax.random.key(seed)
    ks = iter(jax.random.split(key, 48))
    n_pages = PAST_LEN // PAGE_SIZE
    n_pool = (DEC_BATCH * n_pages * 5) // 4
    f32 = jnp.float32

    def w(shape, fan_in):
        return jax.random.normal(next(ks), shape, f32) * (fan_in ** -0.5)

    def gain(shape):
        return 1.0 + 0.05 * jax.random.normal(next(ks), shape, f32)

    def bias(shape):
        return 0.02 * jax.random.normal(next(ks), shape, f32)

    L = DEPTH
    d = {}
    d['x_prompt'] = jax.random.normal(next(ks), (BATCH, SEQ, D_MODEL), f32)
    d['x_sample'] = jax.random.normal(next(ks), (DEC_BATCH, DEC_SEQ, D_MODEL), f32)
    d['cache_ckv'] = jax.random.normal(next(ks), (L, n_pool, PAGE_SIZE, KV_RANK), f32)
    d['cache_kpe'] = jax.random.normal(next(ks), (L, n_pool, PAGE_SIZE, QK_ROPE), f32)
    d['state_conv'] = jax.random.normal(next(ks), (L, DEC_BATCH, CONV_WIDTH - 1, CONV_CH), f32)
    perm = jax.random.permutation(next(ks), n_pool)
    d['page_table'] = perm[:DEC_BATCH * n_pages].reshape(DEC_BATCH, n_pages).astype(jnp.int32)
    d['p_prompt'] = jax.random.normal(next(ks), (L, BATCH, SEQ, PLE_DIM), f32)
    d['p_sample'] = jax.random.normal(next(ks), (L, DEC_BATCH, DEC_SEQ, PLE_DIM), f32)
    d['g_ff1'] = gain((L, D_MODEL))
    d['w1_gate'] = w((L, D_MODEL, D_FF), D_MODEL)
    d['w1_up'] = w((L, D_MODEL, D_FF), D_MODEL)
    d['w1_down'] = w((L, D_FF, D_MODEL), D_FF)
    d['g_mix'] = gain((L, D_MODEL))
    d['w_in'] = w((L, D_MODEL, D_IN), D_MODEL)
    d['g_q'] = gain((L, Q_RANK))
    d['w_q_up'] = w((L, Q_RANK, N_HEADS, QK_NOPE + QK_ROPE), Q_RANK)
    d['g_kv'] = gain((L, KV_RANK))
    d['w_uk'] = w((L, KV_RANK, N_HEADS, QK_NOPE), KV_RANK)
    d['w_uv'] = w((L, KV_RANK, N_HEADS, V_HEAD), KV_RANK)
    d['conv_w'] = w((L, CONV_WIDTH, CONV_CH), CONV_WIDTH)
    d['conv_b'] = bias((L, CONV_CH))
    d['g_cn'] = gain((L, CONV_CH))
    d['b_cn'] = bias((L, CONV_CH))
    d['w_o'] = w((L, D_MIX, D_MODEL), D_MIX)
    d['g_ff2'] = gain((L, D_MODEL))
    d['w2_gate'] = w((L, D_MODEL, D_FF), D_MODEL)
    d['w2_up'] = w((L, D_MODEL, D_FF), D_MODEL)
    d['w2_down'] = w((L, D_FF, D_MODEL), D_FF)
    d['g_ple'] = gain((L, D_MODEL))
    d['w_pg'] = w((L, D_MODEL, D_MODEL), D_MODEL)
    d['b_pg'] = bias((L, D_MODEL))
    d['w_pp'] = w((L, PLE_DIM, D_MODEL), PLE_DIM)
    d['g_final'] = gain((D_MODEL,))
    return d

def reference(x_prompt, x_sample, cache_ckv, cache_kpe, state_conv, page_table, p_prompt, p_sample,
              g_ff1, w1_gate, w1_up, w1_down, g_mix, w_in, g_q, w_q_up, g_kv, w_uk, w_uv,
              conv_w, conv_b, g_cn, b_cn, w_o, g_ff2, w2_gate, w2_up, w2_down,
              g_ple, w_pg, b_pg, w_pp, g_final):
    b_pr, t_pr = x_prompt.shape[0], x_prompt.shape[1]
    b_dec, t_dec = x_sample.shape[0], x_sample.shape[1]
    past_len = page_table.shape[1] * cache_ckv.shape[2]
    pos_prompt = jnp.arange(t_pr)
    pos_sample = past_len + jnp.arange(t_dec)
    conv_zero = jnp.zeros((b_pr, CONV_WIDTH - 1, CONV_CH), x_prompt.dtype)
    h_p, h_s = x_prompt, x_sample
    ckv_p, kpe_p, conv_p, ckv_s, kpe_s, conv_s = [], [], [], [], [], []
    for l in range(DEPTH):
        prm = dict(g_ff1=g_ff1[l], w1_gate=w1_gate[l], w1_up=w1_up[l], w1_down=w1_down[l],
                   g_mix=g_mix[l], w_in=w_in[l], g_q=g_q[l], w_q_up=w_q_up[l], g_kv=g_kv[l],
                   conv_w=conv_w[l], conv_b=conv_b[l], g_cn=g_cn[l], b_cn=b_cn[l], w_o=w_o[l],
                   g_ff2=g_ff2[l], w2_gate=w2_gate[l], w2_up=w2_up[l], w2_down=w2_down[l],
                   g_ple=g_ple[l], w_pg=w_pg[l], b_pg=b_pg[l], w_pp=w_pp[l])
        wuk, wuv = w_uk[l], w_uv[l]

        def attend_prompt(qn, qp, ckv, kpe):
            return prompt_attention(qn, qp, ckv, kpe, wuk, wuv)

        past_ckv = cache_ckv[l][page_table].reshape(b_dec, past_len, KV_RANK)
        past_kpe = cache_kpe[l][page_table].reshape(b_dec, past_len, QK_ROPE)

        def attend_sample(qn, qp, ckv, kpe):
            ckv_all = jnp.concatenate([past_ckv, ckv], axis=1)
            kpe_all = jnp.concatenate([past_kpe, kpe], axis=1)
            return sample_attention(qn, qp, pos_sample, ckv_all, kpe_all, wuk, wuv)

        h_p, c1, k1, s1 = layer(h_p, p_prompt[l], prm, pos_prompt, attend_prompt, conv_zero)
        h_s, c2, k2, s2 = layer(h_s, p_sample[l], prm, pos_sample, attend_sample, state_conv[l])
        ckv_p.append(c1); kpe_p.append(k1); conv_p.append(s1)
        ckv_s.append(c2); kpe_s.append(k2); conv_s.append(s2)
    y_prompt = rmsnorm(h_p, g_final)
    y_sample = rmsnorm(h_s, g_final)
    return (y_prompt, y_sample, jnp.stack(ckv_p), jnp.stack(kpe_p), jnp.stack(conv_p),
            jnp.stack(ckv_s), jnp.stack(kpe_s), jnp.stack(conv_s))


_drawn_inputs = setup_inputs


def setup_inputs(seed=0):
    import zlib

    import numpy as np

    out = dict(_drawn_inputs(seed))
    spreads = {}
    factors = {'cache_kpe': 4.771,
     'g_ff1': 2.744,
     'g_q': 8.0,
     'conv_b': 4.242,
     'g_cn': 2.779,
     'b_cn': 7.76,
     'g_ff2': 3.355,
     'g_ple': 6.697,
     'b_pg': 8.0}
    for name, (base, spread) in spreads.items():
        noise = np.random.default_rng([zlib.crc32(name.encode()), seed]).standard_normal(out[name].shape)
        drawn = base * np.exp(spread * noise) if base else spread * noise
        out[name] = __import__('jax').numpy.asarray(drawn.astype(out[name].dtype))
    for name, factor in factors.items():
        out[name] = (out[name] * factor).astype(out[name].dtype)
    return out
```

```python
from contextlib import ExitStack

import concourse.bass as bass
from concourse import mybir

P = 128
D_MODEL, SEQ, DEC_B, DEC_T = 1024, 1024, 8, 4
ROWS = SEQ + DEC_B * DEC_T
NRB = 3
RB = ROWS // NRB
KC = D_MODEL // P
D_FF = 2816
GROUPS = D_FF // (2 * P)
Q_RANK, KV_RANK, ROPE, NOPE, VH = 384, 256, 32, 64, 64
QC, VC = Q_RANK // P, KV_RANK // P
HEADS = 8
PAIRS = HEADS // 2
CONV_CH, TAPS = 512, 31
CC = CONV_CH // P
HIST = TAPS - 1
PAGE, N_PAGES = 128, 16
PAST = PAGE * N_PAGES
TH = HEADS * DEC_T
NEW = DEC_B * DEC_T
QB = SEQ // P
SCALE = (NOPE + ROPE) ** -0.5
EPS = 1e-6

RAW = 2
RING = 6
FFN_SLOTS = GROUPS * 6
WIN_TILES = 14
N_FF1 = 0
N_WIN = N_FF1 + FFN_SLOTS
N_WO = N_WIN + WIN_TILES
N_FF2 = N_WO + KC
N_PLE = N_FF2 + FFN_SLOTS
PLE_ORDER = ["pp0", "g0", "p0", "p1", "p2", "g1", "g2", "g3", "pp1", "g4", "g5", "g6", "g7"]
PLE_RING = {"pp0": 4, "g0": 5, "g1": 0, "g2": 1, "g3": 2, "pp1": 3, "g4": 5, "g5": 0, "g6": 1, "g7": 2}
N_ALL = N_PLE + len(PLE_ORDER)
FF2_RING = N_FF2 % RING

G_FF1, G_MIX, G_FF2, G_PLE, G_FIN = (KC * i for i in range(5))
G_Q = 5 * KC
G_KV = G_Q + QC
G_CN = G_KV + VC
B_CN = G_CN + CC
B_CONV = B_CN + CC
B_PG = B_CONV + CC
W_CONV = B_PG + KC
N_GAINS = W_CONV + CC * TAPS

PW_PE = 0
PW_NOPE = PW_PE + QC * 2 * ROPE
PW_UK = PW_NOPE + QC * P
PW_UV = PW_UK + VC * P
PW_UKT = PW_UV + VC * P
PW = PW_UKT + 2 * KV_RANK

DOWN = NRB * KC
T_FF1 = 0
T_WIN = T_FF1 + 6 * GROUPS
T_FF2 = T_WIN + CC * NRB
T_PLE = T_FF2 + 6 * GROUPS
Y_NORM1 = 0
Y_FF1 = Y_NORM1 + NRB
Y_WIN = Y_FF1 + DOWN * GROUPS + NRB
Y_LN = Y_WIN + 6 * NRB + 2 * NRB
Y_WO = Y_LN + 2 * NRB
Y_FF2 = Y_WO + KC * NRB + NRB
Y_PLE = Y_FF2 + DOWN * GROUPS + NRB
Z_PROJ = 12


class Tally:

    def __init__(self, eng, sem):
        self.eng, self.sem, self.n, self.off = eng, sem, 0, 0

    def hit(self, ins):
        ins.then_inc(self.sem, 1)
        self.n += 1

    def sync(self):
        self.eng.wait_ge(self.sem, self.off + self.n)


def program(nc, wstream, pairw, xT, hist, gains, trig, ident_d, tri_d, smask_d, cacheT, cacheN,
            cacheK, wuv_d, ptab_d, yT, ckvT, kpeT, convp, convs):
    f32, f32r, i32 = mybir.dt.float32, mybir.dt.float32r, mybir.dt.int32
    ALU, ACT, AX = mybir.AluOpType, mybir.ActivationFunctionType, mybir.AxisListType
    ctx = ExitStack()

    def scope():
        return ExitStack()

    def sb(st, name, shape, dt=f32):
        return st.enter_context(nc.sbuf_tensor(name, shape, dt))

    ident = sb(ctx, "ident", [P, P])
    ones = sb(ctx, "ones", [P, P])
    gain = sb(ctx, "gain", [P, N_GAINS])
    tri = sb(ctx, "tri", [P, P])
    smask = sb(ctx, "smask", [P, 2, NEW])
    stat = sb(ctx, "stat", [P, 24])
    ptab = sb(ctx, "ptab", [1, DEC_B * N_PAGES], i32)
    h = sb(ctx, "h", [P, KC, ROWS])

    zone_bytes = 50816
    za = scope()
    hid_hi = sb(za, "hid_hi", [P, 2, ROWS], f32r)
    hid_lo = sb(za, "hid_lo", [P, 2, ROWS], f32r)
    sq = sb(za, "sq", [P, KC, RB])
    n32 = sb(za, "n32", [P, KC, RB])
    gact = sb(za, "gact", [P, 2, RB])
    prod = sb(za, "prod", [P, 2, RB])
    red = sb(za, "red", [P, RB])
    rstd = sb(za, "rstd", [P, RB])
    za.close()
    zs = scope()
    PT2 = sb(zs, "PT2", [P, N_PAGES + 1, P])
    ktile = sb(zs, "ktile", [ROPE, 4, 512])
    olat = sb(zs, "olat", [P, KV_RANK])
    ckvnew = sb(zs, "ckvnew", [NEW, KV_RANK])
    olatT = sb(zs, "olatT", [P, VC, 2, P])
    sb(zs, "pad_s1", [P, 56])
    SS = sb(zs, "SS", [P, PAST + NEW])
    wuv = sb(zs, "wuv", [P, VC, HEADS * VH])
    zs.close()
    zl = scope()
    sb(zl, "pad_l1", [P, CC * (HIST + SEQ) + CC * DEC_B * (HIST + DEC_T)])
    lnsq = sb(zl, "lnsq", [P, CC, RB])
    zl.close()
    zb = scope()
    vext = sb(zb, "vext", [P, CC, HIST + SEQ])
    vs = sb(zb, "vs", [P, CC, DEC_B, HIST + DEC_T])
    cq = sb(zb, "cq", [P, QC, ROWS])
    ckv = sb(zb, "ckv", [P, VC, ROWS])
    kpe = sb(zb, "kpe", [ROPE, ROWS])
    sqs = sb(zb, "sqs", [P, QC, RB])
    used = 4 * (CC * (HIST + SEQ) + CC * DEC_B * (HIST + DEC_T) + (QC + VC + 1) * ROWS + QC * RB)
    sb(zb, "pad_b", [P, (zone_bytes - used) // 4])

    zn = scope()
    n_hi = sb(zn, "n_hi", [P, KC, ROWS], f32r)
    n_lo = sb(zn, "n_lo", [P, KC, ROWS], f32r)
    zr = scope()
    raw = [sb(zr, f"raw{i}", [P, 1024]) for i in range(RAW)]
    whi = [sb(zr, f"whi{i}", [P, 1024], f32r) for i in range(RING)]
    wlo = [sb(zr, f"wlo{i}", [P, 1024], f32r) for i in range(RING)]
    zr.close()
    zc = scope()
    qabs = sb(zc, "qabs", [P, VC, DEC_B, TH])
    qspe = sb(zc, "qspe", [ROPE, DEC_B, TH])
    z1 = scope()
    tile = [sb(z1, f"tile{i}", [P, 4, 1024]) for i in range(3)]
    z1.close()
    cs = sb(zc, "cs", [2 * ROPE, 2, ROWS])
    q = sb(zc, "q", [NOPE + ROPE, 2, ROWS])
    k = sb(zc, "k", [NOPE + ROPE, 2, SEQ])
    V = sb(zc, "V", [P, QB, P])
    pw = sb(zc, "pw", [P, PW])
    z2 = scope()
    qraw = sb(z2, "qraw", [2 * ROPE, ROWS])
    qsw = sb(z2, "qsw", [2 * ROPE, ROWS])
    z2.close()
    pr = sb(zc, "pr", [P, 2, 2, SEQ])
    zc.close()
    zn.close()
    zo = scope()
    sb(zo, "pad_o1", [P, CC * ROWS])
    PT = sb(zo, "PT", [P, 2, 2, SEQ])
    sb(zo, "pad_o2", [P, CC * ROWS - 4 * SEQ + CC * ROWS])
    cacc = sb(zo, "cacc", [P, CC, ROWS])
    zo.close()
    zb.close()

    ps = ctx.enter_context(nc.psum_tensor("ps", [P, 8, 512], f32))
    psf = ps[:, :, :].rearrange("p b n -> p (b n)")

    def sem(name):
        return ctx.enter_context(nc.semaphore(name))

    x_in = [sem(f"x_in{r}") for r in range(NRB)]
    const_in = sem("const_in")
    hist_in = sem("hist_in")
    raw_in = [sem(f"raw_in{i}") for i in range(RAW)]
    ready0 = sem("ready0")
    w_hi = sem("w_hi")
    w_split = sem("w_split")
    pair_ready, pair_free = sem("pair_ready"), sem("pair_free")
    one_ready, one_free = sem("one_ready"), sem("one_free")
    act_gate = sem("act_gate")
    hid_high, hid_ready = sem("hid_high"), sem("hid_ready")
    p_high, p_ready = sem("p_high"), sem("p_ready")
    sq_ready, sq_summed = sem("sq_ready"), sem("sq_summed")
    root = sem("root")
    n32_ready, n_high, n_ready = sem("n32_ready"), sem("n_high"), sem("n_ready")
    ple_added = sem("ple_added")
    y_out = sem("y_out")
    lat_sq, lat_red, lat_root, lat_norm = sem("lat_sq"), sem("lat_red"), sem("lat_root"), sem("lat_norm")
    trig_in, pw_in = sem("trig_in"), sem("pw_in")
    kpe_ready = sem("kpe_ready")
    proj_ready, proj_free = sem("proj_ready"), sem("proj_free")
    rope_done = sem("rope_done")
    s_ready, s_max, s_free = sem("s_ready"), sem("s_max"), sem("s_free")
    p_norm = sem("p_norm")
    t4_ready, t4_done, t5_ready, t5_done = sem("t4_ready"), sem("t4_done"), sem("t5_ready"), sem("t5_done")
    av_ready, av_hi, av_lo = sem("av_ready"), sem("av_hi"), sem("av_lo")
    conv_done = sem("conv_done")
    ln_red, ln_cent, ln_sq, ln_root, ln_scaled, ln_act, ln_hi, ln_lo = (
        sem(n) for n in ("ln_red", "ln_cent", "ln_sq", "ln_root", "ln_scaled", "ln_act", "ln_hi", "ln_lo"))
    tile_in = [sem(f"tile_in{i}") for i in range(3)]
    tile_used = sem("tile_used")
    k_in, k_used = sem("k_in"), sem("k_used")
    wuv_in = sem("wuv_in")
    ss_ready, ss_max, ss_exp, ss_norm = sem("ss_ready"), sem("ss_max"), sem("ss_exp"), sem("ss_norm")
    st_ready, st_done = sem("st_ready"), sem("st_done")
    out_state = sem("out_state")
    dve_step, act_step = sem("dve_step"), sem("act_step")

    def rows(r):
        return slice(r * RB, (r + 1) * RB)

    def kap(i):
        return i if i < 4 else 4 + 2 * (i - 4)

    block = ctx.enter_context(nc.Block())

    @block.sync
    def _(sp):
        for r in range(NRB):
            sp.dma_start(h[:, :, rows(r)], xT[:, :, rows(r)]).then_inc(x_in[r], 16)
            if r == 0:
                for s in range(RAW):
                    sp.dma_start(raw[s][:, :], wstream[s]).then_inc(raw_in[s], 16)
                sp.dma_start(gain[:, :], gains).then_inc(const_in, 16)
        sp.dma_start(ident[:, :], ident_d).then_inc(const_in, 16)
        sp.dma_start(tri[:, :], tri_d).then_inc(const_in, 16)
        sp.dma_start(smask[:, :, :], smask_d).then_inc(const_in, 16)
        sp.dma_start(ptab[:, :], ptab_d).then_inc(const_in, 16)
        with sp.Fori(0, (N_WO - RAW) // RAW) as g:
            for s in range(RAW):
                sp.wait_ge(w_split, RAW * g + s + 1)
                sp.dma_start(raw[s][:, :], wstream[RAW * g + s + RAW]).then_inc(raw_in[s], 16)
        sp.wait_ge(pair_ready, T_FF2)
        sp.dma_start(cs[:, :, :], trig).then_inc(trig_in, 16)
        sp.dma_start(pw[:, :], pairw[0]).then_inc(pw_in, 16)
        with sp.Fori(1, PAIRS) as p:
            sp.wait_ge(proj_ready, Z_PROJ * p)
            sp.dma_start(pw[:, :], pairw[p]).then_inc(pw_in, 16)
        sp.wait_ge(const_in, 5 * 16)
        sp.wait_ge(av_ready, PAIRS * QB)
        sp.wait_ge(conv_done, 1)
        n = 0
        for grp in range(2):
            for part in range(2):
                for c4 in range(4):
                    if n >= 3:
                        sp.wait_ge(tile_used, n - 2)
                    if part == 0 and (grp, c4) != (0, 0):
                        sp.wait_ge(k_used, 4 * grp + c4)
                    with sp.Fori(0, 4) as j:
                        for pg in range(4):
                            page = sp.value_load(ptab[0:1, bass.ds((4 * grp + j) * N_PAGES + 4 * c4 + pg, 1)],
                                                 min_val=0, max_val=cacheN.shape[0] - 1)
                            t = tile[n % 3]
                            if part == 0:
                                dst = t[:, j, :].rearrange("p (c s) -> p c s", c=VC)[:, :, pg * P:(pg + 1) * P]
                                sp.dma_start(dst, cacheT[page].rearrange("p (c s) -> p c s", c=VC))\
                                  .then_inc(tile_in[n % 3], 16)
                                sp.dma_start(ktile[:, j, pg * P:(pg + 1) * P], cacheK[page]).then_inc(k_in, 16)
                            else:
                                sp.dma_start(t[:, j, pg * KV_RANK:(pg + 1) * KV_RANK], cacheN[page])\
                                  .then_inc(tile_in[n % 3], 16)
                    n += 1
        sp.wait_ge(ln_lo, NRB)
        sp.dma_start(wuv[:, :, :], wuv_d).then_inc(wuv_in, 16)
        sp.wait_ge(tile_used, 16)
        for s in range(RAW):
            sp.dma_start(raw[(N_WO + s) % RAW][:, :], wstream[N_WO + s]).then_inc(raw_in[(N_WO + s) % RAW], 16)
        left = N_ALL - N_WO - RAW
        with sp.Fori(0, left // RAW) as g:
            for s in range(RAW):
                sp.wait_ge(w_split, RAW * g + (N_WO + s + 1))
                sp.dma_start(raw[s][:, :], wstream[RAW * g + (N_WO + s + RAW)]).then_inc(raw_in[s], 16)
        for n in range(N_WO + RAW + left // RAW * RAW, N_ALL):
            sp.wait_ge(w_split, n - RAW + 1)
            sp.dma_start(raw[n % RAW][:, :], wstream[n]).then_inc(raw_in[n % RAW], 16)

    @block.gpsimd
    def _(pool):
        nc.gpsimd.memset(ones[:, :], 1.0).then_inc(ready0, 1)
        nc.gpsimd.memset(stat[:, 23:24], EPS).then_inc(ready0, 1)
        nc.gpsimd.memset(stat[:, 16:17], 0.0).then_inc(pair_free, 2)
        nc.gpsimd.memset(stat[:, 17:18], 0.0).then_inc(one_free, 4)
        nc.gpsimd.memset(stat[:, 18:19], 0.0).then_inc(proj_free, 4)
        nc.gpsimd.memset(stat[:, 19:20], 0.0).then_inc(s_free, 2)
        nc.gpsimd.memset(stat[:, 20:21], 0.0).then_inc(t4_done, 1)
        nc.gpsimd.memset(stat[:, 21:22], 0.0).then_inc(t5_done, 1)
        nc.gpsimd.memset(stat[:, 22:23], 0.0).then_inc(av_lo, 2)
        pool.wait_ge(n_ready, 2 * NRB)
        pool.wait_ge(one_ready, Y_WIN)
        nc.gpsimd.memset(vext[:, :, 0:HIST], 0.0).then_inc(ready0, 1)
        for c in range(CC):
            pool.dma_start(vs[:, c, :, 0:HIST], hist[:, c]).then_inc(hist_in, 16)
        pool.wait_ge(lat_norm, 2 * NRB)
        pool.dma_start(ckvT, ckv[:, :, :]).then_inc(out_state, 16)
        pool.wait_ge(kpe_ready, 1)
        pool.dma_start(kpeT, kpe[:, :]).then_inc(out_state, 16)
        pool.wait_ge(hist_in, 16 * CC)
        pool.wait_ge(pair_free, 2 + T_FF2)
        pool.dma_start(convp, vext[:, :, SEQ:SEQ + HIST]).then_inc(out_state, 16)
        for c in range(CC):
            pool.dma_start(convs[:, c], vs[:, c, :, DEC_T:DEC_T + HIST]).then_inc(out_state, 16)
        for r in range(NRB):
            pool.wait_ge(n32_ready, 4 * NRB + r + 1)
            pool.dma_start(yT[:, :, rows(r)], n32[:, :, :]).then_inc(y_out, 16)
        pool.wait_ge(y_out, 16 * NRB)
        pool.wait_ge(out_state, 16 * (3 + CC))

    @block.tensor
    def _(pe):
        def split_product(out, w_h, w_l, x_h, x_l, first, last):
            nc.tensor.matmul(out, w_l, x_h, start=first, stop=False)
            nc.tensor.matmul(out, w_h, x_l, start=False, stop=False)
            return nc.tensor.matmul(out, w_h, x_h, start=False, stop=last)

        def contract(out, ring, r, chunks=KC, src=(n_hi, n_lo), cols=0):
            for c in range(chunks):
                w = slice(cols + c * P, cols + (c + 1) * P)
                last = split_product(out, whi[ring][:, w], wlo[ring][:, w], src[0][:, c, rows(r)],
                                     src[1][:, c, rows(r)], c == 0, c == chunks - 1)
            return last

        def row_sum(y, wait_sem, wait_val, src):
            pe.wait_ge(wait_sem, wait_val)
            pe.wait_ge(one_free, y + 1)
            nc.tensor.matmul(ps[:, 4 + y % 4, 0:RB], ones[:, :], src, start=True, stop=True).then_inc(one_ready, 1)

        def tail(y, emit, norm):
            for r in range(NRB):
                y = emit(r, y)
                if r:
                    row_sum(y, sq_summed, NRB * norm + r, red[:, :])
                    y += 1
            row_sum(y, sq_summed, NRB * norm + NRB, red[:, :])

        def ffn(n0, t0, y0, norm, ring0):
            def body(g, last):
                for f in range(2):
                    for r in range(NRB):
                        t = 3 * f + r
                        if r == 0:
                            pe.wait_ge(w_split, 6 * g + (n0 + 2 * f + 1))
                        pe.wait_ge(n_ready, NRB * norm + r + 1)
                        pe.wait_ge(pair_free, 6 * g + (t0 + t + 1))
                        b = 2 * ((t0 + t) % 2)
                        contract(ps[:, b, 0:RB], (ring0 + 2 * f) % RING, r)
                        if r == 0:
                            pe.wait_ge(w_split, 6 * g + (n0 + 2 * f + 2))
                        contract(ps[:, b + 1, 0:RB], (ring0 + 2 * f + 1) % RING, r).then_inc(pair_ready, 1)
                pe.wait_ge(w_split, 6 * g + (n0 + 6))

                def down(r, y):
                    pe.wait_ge(hid_ready, 6 * g + (t0h + 3 + r + 1))
                    for o in range(KC):
                        pe.wait_ge(one_free, DOWN * g + (y + 1))
                        for f in range(2):
                            s = (ring0 + 4 + f) % RING
                            w = slice(o * P, (o + 1) * P)
                            end = split_product(ps[:, 4 + y % 4, 0:RB], whi[s][:, w], wlo[s][:, w],
                                                hid_hi[:, f, rows(r)], hid_lo[:, f, rows(r)], f == 0, f == 1)
                        end.then_inc(one_ready, 1)
                        y += 1
                    return y

                if last:
                    base = y0
                    tail_ffn(base, down, g)
                else:
                    y = y0
                    for r in range(NRB):
                        y = down(r, y)

            def tail_ffn(y, down, g):
                for r in range(NRB):
                    y = down(r, y)
                    if r:
                        row_sum(y + DOWN * g, sq_summed, NRB * (norm + 1) + r, red[:, :])
                        y += 1
                row_sum(y + DOWN * g, sq_summed, NRB * (norm + 1) + NRB, red[:, :])

            t0h = t0 - (CC * NRB if t0 else 0)
            with pe.Fori(0, GROUPS - 1) as g:
                body(g, False)
            body(GROUPS - 1, True)

        pe.wait_ge(ready0, 2)
        for r in range(NRB):
            row_sum(Y_NORM1 + r, sq_summed, r + 1, red[:, :])
        ffn(N_FF1, T_FF1, Y_FF1, 0, 0)

        y = Y_WIN
        for j in range(6):
            pe.wait_ge(w_split, N_WIN + j + 1)
            for r in range(NRB):
                pe.wait_ge(n_ready, NRB + r + 1)
                pe.wait_ge(one_free, y + 1)
                contract(ps[:, 4 + y % 4, 0:RB], j % RING, r).then_inc(one_ready, 1)
                y += 1
        for c in range(CC):
            for r in range(NRB):
                t = T_WIN + c * NRB + r
                pe.wait_ge(w_split, N_WIN + 6 + 2 * c + 2)
                pe.wait_ge(pair_free, t + 1)
                b = 2 * (t % 2)
                contract(ps[:, b, 0:RB], (2 * c) % RING, r)
                contract(ps[:, b + 1, 0:RB], (2 * c + 1) % RING, r).then_inc(pair_ready, 1)
                x = c * NRB + r - 2
                if 0 <= x < 2 * NRB:
                    row_sum(y, lat_red, x + 1, sqs[:, 0, :])
                    y += 1

        pe.wait_ge(const_in, 5 * 16)
        with pe.Fori(0, PAIRS) as p:
            pe.wait_ge(pw_in, 16 * p + 16)

            def proj(z, m, n, kc, col, width, rhs, col0=0):
                out = ps[0:m, 4 + z % 4, col0:col0 + n]
                for c in range(kc):
                    last = nc.tensor.matmul(out, pw[:, col + c * width:col + (c + 1) * width], rhs(c),
                                            start=(c == 0), stop=(c == kc - 1))
                return last

            for z in range(3):
                if z == 2:
                    pe.wait_ge(av_lo, QB * p + 2)
                pe.wait_ge(proj_free, Z_PROJ * p + (z + 1))
                proj(z, 2 * ROPE, RB, QC, PW_PE, 2 * ROPE, lambda c: cq[:, c, rows(z)]).then_inc(proj_ready, 1)
            for z in range(3, 6):
                pe.wait_ge(proj_free, Z_PROJ * p + (z + 1))
                proj(z, P, RB, QC, PW_NOPE, P, lambda c: cq[:, c, rows(z - 3)]).then_inc(proj_ready, 1)
            for z in range(6, 8):
                pe.wait_ge(proj_free, Z_PROJ * p + (z + 1))
                s0 = (z - 6) * 512
                proj(z, P, 512, VC, PW_UK, P, lambda c: ckv[:, c, s0:s0 + 512]).then_inc(proj_ready, 1)
            for z in range(8, 10):
                pe.wait_ge(proj_free, Z_PROJ * p + (z + 1))
                for i in range(4):
                    s0 = ((z - 8) * 4 + i) * P
                    for c in range(VC):
                        last = nc.tensor.matmul(ps[:, 4 + z % 4, i * P:(i + 1) * P], ckv[:, c, s0:s0 + P],
                                                pw[:, PW_UV + c * P:PW_UV + (c + 1) * P],
                                                start=(c == 0), stop=(c == VC - 1))
                last.then_inc(proj_ready, 1)
            pe.wait_ge(proj_free, Z_PROJ * p + (4 + 6))
            for z in range(10, 12):
                pe.wait_ge(proj_free, Z_PROJ * p + (z + 1))
                for c in range(VC):
                    w0 = PW_UKT + (z - 10) * KV_RANK + c * P
                    last = nc.tensor.matmul(ps[:, 4 + z % 4, c * NEW:(c + 1) * NEW], pw[0:NOPE, w0:w0 + P],
                                            q[0:NOPE, z - 10, SEQ:ROWS], start=True, stop=True)
                last.then_inc(proj_ready, 1)
            pe.wait_ge(rope_done, p + 1)
            pe.wait_ge(kpe_ready, 1)

            def scores(i):
                for hh in range(2):
                    pe.wait_ge(s_free, 2 * QB * p + (2 * i + hh + 1))
                    w = (i + 1) * P
                    for c in range(0, w, 512):
                        e = min(w, c + 512)
                        last = nc.tensor.matmul(psf[:, hh * 1024 + c:hh * 1024 + e], q[:, hh, i * P:(i + 1) * P],
                                                k[:, hh, c:e], start=True, stop=True)
                    last.then_inc(s_ready, 1)

            def transposes(i):
                for hh in range(2):
                    pe.wait_ge(p_norm, 2 * QB * p + (2 * i + hh + 1))
                    for c in range(0, i + 1, 4):
                        if i < 4:
                            bank, idx = 4 + hh, kap(i)
                        else:
                            bank, idx = 4 + c // 4, kap(i) + hh
                        ready, done = ((t4_ready, t4_done), (t5_ready, t5_done))[bank - 4]
                        pe.wait_ge(done, 12 * p + (idx + 1))
                        for j in range(c, min(i + 1, c + 4)):
                            last = nc.tensor.transpose(ps[:, bank, (j - c) * P:(j - c + 1) * P],
                                                       pr[:, i % 2, hh, j * P:(j + 1) * P], ident[:, :])
                        last.then_inc(ready, 1)

            def values(i):
                pe.wait_ge(t4_done, 12 * p + (1 + kap(i + 1)))
                pe.wait_ge(t5_done, 12 * p + (1 + kap(i + 1)))
                pe.wait_ge(av_lo, QB * p + (i + 1))
                for j in range(i + 1):
                    for hh in range(2):
                        last = nc.tensor.matmul(ps[VH * hh:VH * (hh + 1), 6 + i % 2, 0:P],
                                                V[:, j, VH * hh:VH * (hh + 1)], PT[:, i % 2, hh, j * P:(j + 1) * P],
                                                start=(j == 0), stop=(j == i))
                last.then_inc(av_ready, 1)

            scores(0)
            pe.wait_ge(proj_free, Z_PROJ * p + (4 + Z_PROJ))
            for i in range(QB):
                if i + 1 < QB:
                    scores(i + 1)
                transposes(i)
                values(i)

        pe.wait_ge(av_lo, PAIRS * QB + 2)
        y = Y_LN
        for r in range(NRB):
            for m in range(2):
                row_sum(y, ln_red, 2 * r + m + 1, sqs[:, 0, :])
                y += 1

        pe.wait_ge(one_free, Y_WO + 4)
        for c in range(VC):
            last = nc.tensor.transpose(ps[0:NEW, 5, c * P:(c + 1) * P], ckv[:, c, SEQ:ROWS], ident[:, :])
        last.then_inc(st_ready, 1)
        st = 1
        n = 0
        for grp in range(2):
            if grp:
                pe.wait_ge(ss_exp, grp)
            for c4 in range(4):
                pe.wait_ge(tile_in[n % 3], 256 * (n // 3 + 1))
                pe.wait_ge(k_in, 256 * (4 * grp + c4 + 1))
                for c in range(VC):
                    for j in range(4):
                        last = nc.tensor.matmul(ps[TH * j:TH * (j + 1), c4, :], qabs[:, c, 4 * grp + j, :],
                                                tile[n % 3][:, j, c * 512:(c + 1) * 512],
                                                start=(c == 0), stop=False)
                last.then_inc(tile_used, 1)
                for j in range(4):
                    last = nc.tensor.matmul(ps[TH * j:TH * (j + 1), c4, :], qspe[:, 4 * grp + j, :],
                                            ktile[:, j, :], start=False, stop=True)
                last.then_inc(k_used, 1)
                n += 1
            for c in range(VC):
                for j in range(4):
                    nc.tensor.matmul(ps[TH * j:TH * (j + 1), 4, 0:NEW], qabs[:, c, 4 * grp + j, :],
                                     ckv[:, c, SEQ:ROWS], start=(c == 0), stop=False)
            for j in range(4):
                last = nc.tensor.matmul(ps[TH * j:TH * (j + 1), 4, 0:NEW], qspe[:, 4 * grp + j, :],
                                        kpe[:, SEQ:ROWS], start=False, stop=True)
            last.then_inc(ss_ready, 1)
            pe.wait_ge(ss_norm, grp + 1)
            for c in range(0, N_PAGES + 1, 4):
                pe.wait_ge(st_done, st)
                for j in range(c, min(c + 4, N_PAGES)):
                    last = nc.tensor.transpose(ps[:, 5 + st % 2, (j - c) * P:(j - c + 1) * P],
                                               SS[:, j * P:(j + 1) * P], ident[:, :])
                if c == N_PAGES:
                    last = nc.tensor.transpose(ps[0:NEW, 5 + st % 2, 0:P], SS[:, PAST:PAST + NEW], ident[:, :])
                last.then_inc(st_ready, 1)
                st += 1
            pe.wait_ge(st_done, st)
            for c4 in range(4):
                pe.wait_ge(tile_in[n % 3], 256 * (n // 3 + 1))
                for pg in range(4):
                    for j in range(4):
                        last = nc.tensor.matmul(ps[TH * j:TH * (j + 1), 7, 0:KV_RANK],
                                                PT2[:, 4 * c4 + pg, TH * j:TH * (j + 1)],
                                                tile[n % 3][:, j, pg * KV_RANK:(pg + 1) * KV_RANK],
                                                start=(c4 == 0 and pg == 0), stop=False)
                last.then_inc(tile_used, 1)
                n += 1
            for j in range(4):
                last = nc.tensor.matmul(ps[TH * j:TH * (j + 1), 7, 0:KV_RANK], PT2[0:NEW, N_PAGES, TH * j:TH * (j + 1)],
                                        ckvnew[:, :], start=False, stop=True)
            last.then_inc(st_ready, 1)
            st += 1
            pe.wait_ge(st_done, st)
            for c in range(VC):
                last = nc.tensor.transpose(ps[:, 5, c * P:(c + 1) * P], olat[:, c * P:(c + 1) * P], ident[:, :])
            last.then_inc(st_ready, 1)
            st += 1
        pe.wait_ge(st_done, st)
        pe.wait_ge(wuv_in, 16)
        for hd in range(HEADS):
            o = VH * (hd % 2)
            for c in range(VC):
                last = nc.tensor.matmul(
                    ps[o:o + VH, 6, (hd // 2) * NEW:(hd // 2 + 1) * NEW], wuv[:, c, hd * VH:(hd + 1) * VH],
                    olatT[:, c].rearrange("p g (j h t) -> p (g j) h t", j=4, h=HEADS)[:, :, hd, :],
                    start=(c == 0), stop=(c == VC - 1))
        last.then_inc(av_ready, 1)

        pe.wait_ge(ln_lo, NRB)
        pe.wait_ge(av_lo, 2 + PAIRS * QB + 1)

        def wo(o):
            def emit(r, y):
                pe.wait_ge(one_free, y + 1)
                contract(ps[:, 4 + y % 4, 0:RB], (N_WO + o) % RING, r).then_inc(one_ready, 1)
                return y + 1
            return emit

        y = Y_WO
        for o in range(KC):
            pe.wait_ge(w_split, N_WO + o + 1)
            if o < KC - 1:
                for r in range(NRB):
                    y = wo(o)(r, y)
        tail(y, wo(KC - 1), 2)

        ffn(N_FF2, T_FF2, Y_FF2, 2, FF2_RING)

        def ple(o):
            def emit(r, y):
                t = T_PLE + NRB * o + r
                pe.wait_ge(pair_free, t + 1)
                pe.wait_ge(n_ready, NRB * 3 + r + 1)
                b = 2 * (t % 2)
                contract(ps[:, b, 0:RB], PLE_RING[f"g{o}"], r)
                pe.wait_ge(p_ready, r + 1)
                pe.wait_ge(w_split, N_PLE + PLE_ORDER.index(f"pp{o // 4}") + 1)
                contract(ps[:, b + 1, 0:RB], PLE_RING[f"pp{o // 4}"], r, VC, (hid_hi, hid_lo),
                         (o % 4) * VC * P).then_inc(pair_ready, 1)
                return y
            return emit

        for o in range(KC):
            pe.wait_ge(w_split, N_PLE + PLE_ORDER.index(f"g{o}") + 1)
            if o < KC - 1:
                for r in range(NRB):
                    ple(o)(r, 0)
        tail(Y_PLE, ple(KC - 1), 4)

    @block.scalar
    def _(act):
        step = Tally(act, act_step)

        def high(n, ring, idx=None, add=0):
            act.wait_ge(raw_in[n % RAW], 16 * (n // RAW + 1) + 8 * add)
            nc.scalar.activation(whi[ring][:, :], raw[n % RAW][:, :], ACT.Copy).then_inc(w_hi, 1)

        def squares(norm, r, sem_, val, src=h, dst=sq, ready=sq_ready, summed=sq_summed):
            act.wait_ge(sem_, val)
            kk = NRB * norm + r
            if kk:
                act.wait_ge(summed, kk)
            nc.scalar.activation(dst[:, :, :], src[:, :, rows(r)], ACT.Square).then_inc(ready, 1)

        def norm_high(norm, r):
            act.wait_ge(n32_ready, NRB * norm + r + 1)
            nc.scalar.activation(n_hi[:, :, rows(r)], n32[:, :, :], ACT.Copy).then_inc(n_high, 1)

        def norm_root(norm, r, y):
            act.wait_ge(one_ready, y + 1)
            if norm == 4 and r:
                act.wait_ge(n32_ready, NRB * norm + r)
            nc.scalar.activation(rstd[:, :], ps[:, 4 + y % 4, 0:RB], ACT.Sqrt, scale=1.0 / D_MODEL,
                                 bias=stat[:, 23:24]).then_inc(root, 1)
            if norm < 4:
                norm_high(norm, r)

        def norm_tail(norm, done, ys, before=lambda r: None):
            before(0)
            squares(norm, 0, *done(0))
            before(1)
            squares(norm, 1, *done(1))
            norm_root(norm, 0, ys[0])
            before(2)
            squares(norm, 2, *done(2))
            norm_root(norm, 1, ys[1])
            norm_root(norm, 2, ys[2])

        def ffn(n0, t0, y0, norm, ring0, nexts):
            t0h = t0 - (CC * NRB if t0 else 0)

            def body(g, last):
                for f in range(2):
                    for r in range(NRB):
                        t = 3 * f + r
                        act.wait_ge(pair_ready, 6 * g + (t0 + t + 1))
                        act.wait_ge(pair_free, 6 * g + (t0 + t + 1))
                        nc.scalar.activation(gact[:, t % 2, :], ps[:, 2 * ((t0 + t) % 2), 0:RB], ACT.Silu)\
                            .then_inc(act_gate, 1)
                        act.wait_ge(pair_free, 6 * g + (t0 + t + 3))
                        nc.scalar.activation(hid_hi[:, f, rows(r)], prod[:, t % 2, :], ACT.Copy)\
                            .then_inc(hid_high, 1)
                    if f == 0:
                        act.wait_ge(one_ready, DOWN * g + y0)
                        for s in (4, 5):
                            high(n0 + s, (ring0 + s) % RING, add=6 * g)
                if last:
                    for n, ring in nexts:
                        high(n, ring)
                else:
                    for s in range(6, 10):
                        high(n0 + s, (ring0 + s) % RING, add=6 * g)

            with act.Fori(0, GROUPS - 1) as g:
                body(g, False)
            body(GROUPS - 1, True)
            y = y0 + DOWN * (GROUPS - 1)
            ends = [y + KC, y + 2 * KC, y + 3 * KC + 1]
            norm_tail(norm + 1, lambda r: (one_free, 4 + ends[r]), [y + 2 * KC, y + 3 * KC + 1, y + 3 * KC + 2])

        act.wait_ge(ready0, 2)
        norm_tail(0, lambda r: (x_in[r], 16), [Y_NORM1 + r for r in range(NRB)])
        for n in range(4):
            high(N_FF1 + n, n)
        ffn(N_FF1, T_FF1, Y_FF1, 0, 0, [(N_WIN + j, j) for j in range(4)])

        act.wait_ge(one_ready, Y_WIN)
        for j in (4, 5):
            high(N_WIN + j, j)

        def lat_squares(m, r):
            n_src, c = ((cq, QC), (ckv, VC))[m]
            act.wait_ge(one_free, 4 + Y_WIN + NRB * (QC if m == 0 else QC + VC))
            if NRB * m + r:
                act.wait_ge(lat_norm, NRB * m + r)
            nc.scalar.activation(sqs[:, 0:c, :], n_src[:, :, rows(r)], ACT.Square).then_inc(lat_sq, 1)

        def gate(c, r):
            t = T_WIN + c * NRB + r
            act.wait_ge(pair_ready, t + 1)
            b = 2 * (t % 2) + 1
            if r < NRB - 1:
                nc.scalar.activation(vext[:, c, HIST + r * RB:HIST + (r + 1) * RB], ps[:, b, 0:RB], ACT.Sigmoid)\
                    .then_inc(act_gate, 1)
            else:
                nc.scalar.activation(vext[:, c, HIST + r * RB:HIST + SEQ], ps[:, b, 0:SEQ - r * RB], ACT.Sigmoid)
                nc.scalar.activation(vs[:, c, :, HIST:HIST + DEC_T],
                                     ps[:, b, SEQ - r * RB:RB].rearrange("p (b t) -> p b t", b=DEC_B), ACT.Sigmoid)\
                    .then_inc(act_gate, 1)

        def lat_root_(x):
            m, r = divmod(x, NRB)
            y = Y_WIN + 6 * NRB + x
            act.wait_ge(one_ready, y + 1)
            nc.scalar.activation(sqs[:, 1, :], ps[:, 4 + y % 4, 0:RB], ACT.Sqrt, scale=1.0 / (P * (QC, VC)[m]),
                                 bias=stat[:, 23:24]).then_inc(lat_root, 1)

        for j in range(6, 12):
            act.wait_ge(one_ready, Y_WIN + NRB * (j - 5))
            high(N_WIN + j, j % RING)
        lat_squares(0, 0)
        for x in range(CC * NRB):
            gate(*divmod(x, NRB))
            if x == 2:
                for j in (12, 13):
                    high(N_WIN + j, j % RING)
            if 0 <= x - 2 < 2 * NRB:
                lat_root_(x - 2)
                if x - 1 < 2 * NRB:
                    lat_squares(*divmod(x - 1, NRB))

        with act.Fori(0, PAIRS) as p:
            def evac(z, dsts):
                act.wait_ge(proj_ready, Z_PROJ * p + (z + 1))
                for d, s in dsts:
                    last = nc.scalar.activation(d, s, ACT.Copy)
                last.then_inc(proj_free, 1)

            for z in range(3):
                evac(z, [(qraw[:, rows(z)], ps[0:2 * ROPE, 4 + z % 4, 0:RB])])
            for z in range(3, 6):
                evac(z, [(q[0:NOPE, hh, rows(z - 3)], ps[NOPE * hh:NOPE * (hh + 1), 4 + z % 4, 0:RB])
                         for hh in range(2)])
            for z in range(6, 8):
                s0 = (z - 6) * 512
                evac(z, [(k[0:NOPE, hh, s0:s0 + 512], ps[NOPE * hh:NOPE * (hh + 1), 4 + z % 4, :])
                         for hh in range(2)])
            for z in range(8, 10):
                evac(z, [(V[:, (z - 8) * 4:(z - 7) * 4, :], ps[:, 4 + z % 4, :].rearrange("p (s v) -> p s v", s=4))])
            for z in range(10, 12):
                evac(z, [(qabs[:, c, :, bass.ds(8 * p + 4 * (z - 10), 4)],
                          ps[:, 4 + z % 4, c * NEW:(c + 1) * NEW].rearrange("p (b t) -> p b t", b=DEC_B))
                         for c in range(VC)])

            def untile(i):
                for x in range(1 if i < 4 else 2):
                    act.wait_ge(t4_ready, 12 * p + (kap(i) + x + 1))
                    n = min(i + 1, 4) * P
                    nc.scalar.activation(PT[:, i % 2, x, 0:n], ps[:, 4, 0:n], ACT.Copy).then_inc(t4_done, 1)

            def high_av(i):
                act.wait_ge(av_ready, QB * p + (i + 1))
                nc.scalar.activation(n_hi[:, p, i * P:(i + 1) * P], ps[:, 6 + i % 2, 0:P], ACT.Copy).then_inc(av_hi, 1)

            for i in range(QB):
                if i:
                    untile(i - 1)
                for hh in range(2):
                    u = 2 * i + hh
                    act.wait_ge(s_max, 2 * QB * p + (u + 1))
                    w = (i + 1) * P
                    nc.scalar.activation(pr[:, i % 2, hh, 0:w], psf[:, 1024 * hh:1024 * hh + w], ACT.Exp,
                                         bias=stat[:, 4 + u % 4:5 + u % 4], scale=SCALE,
                                         accum_out=stat[:, 8 + u % 4:9 + u % 4]).then_inc(s_free, 1)
                if i:
                    high_av(i - 1)
            untile(QB - 1)
            high_av(QB - 1)

        for r in range(NRB):
            act.wait_ge(ln_cent, r + 1)
            nc.scalar.activation(lnsq[:, :, :], cacc[:, :, rows(r)], ACT.Square).then_inc(ln_sq, 1)
            y = Y_LN + 2 * r + 1
            act.wait_ge(one_ready, y + 1)
            nc.scalar.activation(sqs[:, 2, :], ps[:, 4 + y % 4, 0:RB], ACT.Sqrt, scale=1.0 / CONV_CH,
                                 bias=stat[:, 23:24]).then_inc(ln_root, 1)
            act.wait_ge(ln_scaled, r + 1)
            for c in range(CC):
                nc.scalar.activation(cacc[:, c, rows(r)], cacc[:, c, rows(r)], ACT.Silu,
                                     scale=gain[:, G_CN + c:G_CN + c + 1], bias=gain[:, B_CN + c:B_CN + c + 1])\
                    .then_inc(ln_act, 1)
            act.wait_ge(ln_act, CC * (r + 1))
            nc.scalar.activation(n_hi[:, CC:KC, rows(r)], cacc[:, :, rows(r)], ACT.Copy).then_inc(ln_hi, 1)

        for grp in range(2):
            act.wait_ge(ss_max, grp + 1)
            if grp:
                act.wait_ge(st_done, 1 + 5)
            nc.scalar.activation(SS[:, 0:PAST], psf[:, 0:PAST], ACT.Exp, bias=stat[:, 1:2], scale=SCALE,
                                 accum_out=stat[:, 2:3])
            nc.scalar.activation(SS[:, PAST:PAST + NEW], ps[:, 4, 0:NEW], ACT.Exp, bias=stat[:, 1:2], scale=SCALE,
                                 accum_out=stat[:, 3:4]).then_inc(ss_exp, 1)
        act.wait_ge(av_ready, PAIRS * QB + 1)
        nc.scalar.activation(n_hi[:, 0:PAIRS, SEQ:ROWS], ps[:, 6, 0:PAIRS * NEW].rearrange("p (a n) -> p a n", a=PAIRS),
                             ACT.Copy).then_inc(av_hi, 1)

        for o in range(KC):
            if o >= RING:
                act.wait_ge(one_ready, Y_WO + NRB * (o - RING + 1))
            high(N_WO + o, (N_WO + o) % RING)
        for s in range(4):
            act.wait_ge(one_ready, Y_WO + NRB * (s + 3))
            high(N_FF2 + s, (FF2_RING + s) % RING)
        y = Y_WO + NRB * (KC - 1)
        wo_end = [y + 1, y + 2, y + 4]
        norm_tail(2, lambda r: (one_free, 4 + wo_end[r]), [y + 1 + 1, y + 4, y + 5])
        ffn(N_FF2, T_FF2, Y_FF2, 2, FF2_RING, [(N_PLE, PLE_RING["pp0"]), (N_PLE + 1, PLE_RING["g0"])])

        for r in range(NRB):
            n = N_PLE + 2 + r
            act.wait_ge(raw_in[n % RAW], 16 * (n // RAW + 1))
            act.wait_ge(one_ready, Y_PLE)
            nc.scalar.activation(hid_hi[:, :, rows(r)], raw[n % RAW][:, 0:VC * RB].rearrange("p (c n) -> p c n", c=VC),
                                 ACT.Copy).then_inc(w_hi, 1)
        after = {"g1": 0, "g2": 0, "g3": 0, "pp1": 0, "g4": 1, "g5": 2, "g6": 3, "g7": 4}
        highs = [x for x in PLE_ORDER if x in after]

        def high_ple(x):
            if after[x]:
                act.wait_ge(pair_ready, T_PLE + NRB * after[x])
            high(N_PLE + PLE_ORDER.index(x), PLE_RING[x])

        for x in highs[:4]:
            high_ple(x)
        def ple_gate(o, r):
            t = T_PLE + NRB * o + r
            act.wait_ge(pair_ready, t + 1)
            act.wait_ge(pair_free, t + 1)
            nc.scalar.activation(gact[:, t % 2, :], ps[:, 2 * (t % 2), 0:RB], ACT.Sigmoid,
                                 bias=gain[:, B_PG + o:B_PG + o + 1]).then_inc(act_gate, 1)

        for o in range(KC - 1):
            for r in range(NRB):
                ple_gate(o, r)
            if o < 4:
                high_ple(highs[4 + o])
        norm_tail(4, lambda r: (ple_added, NRB * (KC - 1) + r + 1), [Y_PLE + r for r in range(NRB)],
                  lambda r: ple_gate(KC - 1, r))

    @block.vector
    def _(ve):
        step = Tally(ve, dve_step)

        def low(n, ring, add=0):
            ve.wait_ge(w_hi, n + 1 + add)
            nc.vector.tensor_tensor(wlo[ring][:, :], raw[n % RAW][:, :], whi[ring][:, :].bitcast(f32), ALU.subtract)\
                .then_inc(w_split, 1)

        def norm_sum(norm, r, y):
            ve.wait_ge(sq_ready, NRB * norm + r + 1)
            if y is not None:
                ve.wait_ge(one_ready, y + 1)
            nc.vector.tensor_reduce(red[:, :], sq[:, :, :].rearrange("p c n -> p n c"), AX.X, ALU.add)\
                .then_inc(sq_summed, 1)

        def norm_apply(norm, r, y, g0):
            ve.wait_ge(root, NRB * norm + r + 1)
            nc.vector.reciprocal(rstd[:, :], rstd[:, :]).then_inc(one_free, 1)
            if norm == 4 and r:
                ve.wait_ge(y_out, 16 * r)
            ve.wait_ge(one_free, 4 + y + 1)
            for c in range(KC):
                last = nc.vector.scalar_tensor_tensor(out=n32[:, c, :], in0=h[:, c, rows(r)],
                                                      scalar=gain[:, g0 + c:g0 + c + 1], in1=rstd[:, :],
                                                      op0=ALU.mult, op1=ALU.mult)
            last.then_inc(n32_ready, 1)
            if norm < 4:
                ve.wait_ge(n_high, NRB * norm + r + 1)
                nc.vector.tensor_tensor(n_lo[:, :, rows(r)], n32[:, :, :], n_hi[:, :, rows(r)].bitcast(f32),
                                        ALU.subtract).then_inc(n_ready, 1)

        def norm_tail(norm, g0, update, ys):
            update(0)
            norm_sum(norm, 0, None)
            update(1)
            norm_sum(norm, 1, ys[0])
            norm_apply(norm, 0, ys[0], g0)
            update(2)
            norm_sum(norm, 2, ys[1])
            norm_apply(norm, 1, ys[1], g0)
            norm_apply(norm, 2, ys[2], g0)

        def add_tile(o, r, y, factor, base=0):
            ve.wait_ge(one_ready, base + (y + 1))
            nc.vector.scalar_tensor_tensor(out=h[:, o, rows(r)], in0=ps[:, 4 + y % 4, 0:RB], scalar=factor,
                                           in1=h[:, o, rows(r)], op0=ALU.mult, op1=ALU.add).then_inc(one_free, 1)

        def ffn(n0, t0, y0, norm, ring0, nexts, g_next):
            t0h = t0 - (CC * NRB if t0 else 0)

            def body(g, last):
                for f in range(2):
                    for r in range(NRB):
                        t = 3 * f + r
                        ve.wait_ge(act_gate, 6 * g + (t0 + t + 1))
                        nc.vector.tensor_tensor(prod[:, t % 2, :], gact[:, t % 2, :],
                                                ps[:, 2 * ((t0 + t) % 2) + 1, 0:RB], ALU.mult).then_inc(pair_free, 1)
                        ve.wait_ge(hid_high, 6 * g + (t0h + t + 1))
                        nc.vector.tensor_tensor(hid_lo[:, f, rows(r)], prod[:, t % 2, :],
                                                hid_hi[:, f, rows(r)].bitcast(f32), ALU.subtract)\
                            .then_inc(hid_ready, 1)
                    if f == 0:
                        for s in (4, 5):
                            low(n0 + s, (ring0 + s) % RING, 6 * g)
                if last:
                    for n, ring in nexts:
                        low(n, ring)
                    yl = y0 + DOWN * (GROUPS - 1)
                    start = [yl, yl + KC, yl + 2 * KC + 1]

                    def update(r):
                        for o in range(KC):
                            add_tile(o, r, start[r] + o, 0.5)

                    norm_tail(norm + 1, g_next, update, [yl + 2 * KC, yl + 3 * KC + 1, yl + 3 * KC + 2])
                else:
                    for s in range(6, 10):
                        low(n0 + s, (ring0 + s) % RING, 6 * g)
                    for r in range(NRB):
                        for o in range(KC):
                            add_tile(o, r, y0 + KC * r + o, 0.5, DOWN * g)

            with ve.Fori(0, GROUPS - 1) as g:
                body(g, False)
            body(GROUPS - 1, True)

        ve.wait_ge(const_in, 5 * 16)
        norm_tail(0, G_FF1, lambda r: None, [Y_NORM1, Y_NORM1 + 1, Y_NORM1 + 2])
        for n in range(4):
            low(N_FF1 + n, n)
        ffn(N_FF1, T_FF1, Y_FF1, 0, 0, [(N_WIN + j, j) for j in range(4)], G_MIX)

        for j in (4, 5):
            low(N_WIN + j, j)
        y = Y_WIN

        def take(j, r):
            yy = Y_WIN + NRB * j + r
            ve.wait_ge(one_ready, yy + 1)
            dst = (cq[:, j, rows(r)] if j < QC else ckv[:, j - QC, rows(r)] if j < QC + VC else kpe[:, rows(r)])
            src = ps[:, 4 + yy % 4, 0:RB] if j < QC + VC else ps[0:ROPE, 4 + yy % 4, 0:RB]
            nc.vector.tensor_copy(dst, src).then_inc(one_free, 1)

        def lat_sum(m, r):
            ve.wait_ge(lat_sq, NRB * m + r + 1)
            for x in range(1, (QC, VC)[m]):
                last = nc.vector.tensor_tensor(sqs[:, 0, :], sqs[:, 0, :], sqs[:, x, :], ALU.add)
                if x < (QC, VC)[m] - 1:
                    step.hit(last)
                    step.sync()
            last.then_inc(lat_red, 1)

        def lat_apply(m, r):
            src, c, g0 = ((cq, QC, G_Q), (ckv, VC, G_KV))[m]
            yy = Y_WIN + 6 * NRB + NRB * m + r
            ve.wait_ge(lat_root, NRB * m + r + 1)
            nc.vector.reciprocal(sqs[:, 1, :], sqs[:, 1, :]).then_inc(one_free, 1)
            ve.wait_ge(one_free, 4 + yy + 1)
            for x in range(c):
                last = nc.vector.scalar_tensor_tensor(out=src[:, x, rows(r)], in0=src[:, x, rows(r)],
                                                      scalar=gain[:, g0 + x:g0 + x + 1], in1=sqs[:, 1, :],
                                                      op0=ALU.mult, op1=ALU.mult)
            last.then_inc(lat_norm, 1)

        def glu(c, r):
            t = T_WIN + c * NRB + r
            ve.wait_ge(act_gate, t + 1)
            b = 2 * (t % 2)
            if r < NRB - 1:
                v = vext[:, c, HIST + r * RB:HIST + (r + 1) * RB]
                nc.vector.tensor_tensor(v, v, ps[:, b, 0:RB], ALU.mult).then_inc(pair_free, 1)
            else:
                v = vext[:, c, HIST + r * RB:HIST + SEQ]
                nc.vector.tensor_tensor(v, v, ps[:, b, 0:SEQ - r * RB], ALU.mult)
                v = vs[:, c, :, HIST:HIST + DEC_T]
                nc.vector.tensor_tensor(v, v, ps[:, b, SEQ - r * RB:RB].rearrange("p (b t) -> p b t", b=DEC_B),
                                        ALU.mult).then_inc(pair_free, 1)

        for j in range(6, 12):
            for r in range(NRB):
                take(j - 6, r)
            low(N_WIN + j, j % RING)
        lat_sum(0, 0)
        for x in range(CC * NRB):
            glu(*divmod(x, NRB))
            if x == 2:
                for j in (12, 13):
                    low(N_WIN + j, j % RING)
            if 0 <= x - 2 < 2 * NRB:
                lat_apply(*divmod(x - 2, NRB))
                if x - 1 < 2 * NRB:
                    lat_sum(*divmod(x - 1, NRB))

        swap = [(i + ROPE // 2) % ROPE for i in range(ROPE)]
        ksw = sqs[0:ROPE, :, :].rearrange("p c n -> p (c n)")
        ve.wait_ge(trig_in, 16)
        ve.wait_ge(lat_norm, 2 * NRB)
        step.hit(nc.vector.stream_shuffle(ksw, kpe[:, :], swap))
        step.sync()
        step.hit(nc.vector.tensor_tensor(kpe[:, :], kpe[:, :], cs[0:ROPE, 0, :], ALU.mult))
        step.hit(nc.vector.tensor_tensor(ksw, ksw, cs[0:ROPE, 1, :], ALU.mult))
        step.sync()
        step.hit(nc.vector.tensor_tensor(kpe[:, :], kpe[:, :], ksw, ALU.add))
        step.sync()
        nc.vector.tensor_copy(k[NOPE:NOPE + ROPE, 0, :], kpe[:, 0:SEQ])
        nc.vector.tensor_copy(k[NOPE:NOPE + ROPE, 1, :], kpe[:, 0:SEQ]).then_inc(kpe_ready, 1)
        ve.wait_ge(ready0, 3)
        ve.wait_ge(hist_in, 16 * CC)

        per_pair = 3 + 2 + 2 * TAPS + 16 * 3
        done_before = step.n
        with ve.Fori(0, PAIRS) as p:
            step.off = per_pair * p
            ve.wait_ge(proj_free, Z_PROJ * p + (4 + 3))
            nc.vector.memset(stat[:, 22:23], 0.0)
            step.hit(nc.vector.stream_shuffle(qsw[:, :], qraw[:, :], swap))
            step.sync()
            step.hit(nc.vector.tensor_tensor(qraw[:, :], qraw[:, :], cs[:, 0, :], ALU.mult))
            step.hit(nc.vector.tensor_tensor(qsw[:, :], qsw[:, :], cs[:, 1, :], ALU.mult))
            step.sync()
            nc.vector.tensor_tensor(q[NOPE:NOPE + ROPE, 0, :], qraw[0:ROPE, :], qsw[0:ROPE, :], ALU.add)
            nc.vector.tensor_tensor(q[NOPE:NOPE + ROPE, 1, :], qraw[ROPE:2 * ROPE, :], qsw[ROPE:2 * ROPE, :],
                                    ALU.add).then_inc(rope_done, 1)
            ve.wait_ge(rope_done, p + 1)
            for hh in range(2):
                step.hit(nc.vector.tensor_copy(qspe[:, :, bass.ds(8 * p + 4 * hh, 4)],
                                               q[NOPE:NOPE + ROPE, hh, SEQ:ROWS].rearrange("p (b t) -> p b t", b=DEC_B)))

            def tap(x):
                w = gain[:, bass.ds(p * TAPS + (W_CONV + x), 1)]
                out_s = cacc[:, p, SEQ:ROWS].rearrange("p (b t) -> p b t", b=DEC_B)
                if x == 0:
                    b = gain[:, bass.ds(p + B_CONV, 1)]
                    step.hit(nc.vector.tensor_scalar(cacc[:, p, 0:SEQ], vext[:, p, 0:SEQ], w, b, ALU.mult, ALU.add))
                    step.hit(nc.vector.tensor_scalar(out_s, vs[:, p, :, 0:DEC_T], w, b, ALU.mult, ALU.add))
                else:
                    step.sync()
                    step.hit(nc.vector.scalar_tensor_tensor(out=cacc[:, p, 0:SEQ], in0=vext[:, p, x:x + SEQ],
                                                            scalar=w, in1=cacc[:, p, 0:SEQ], op0=ALU.mult, op1=ALU.add))
                    step.hit(nc.vector.scalar_tensor_tensor(out=out_s, in0=vs[:, p, :, x:x + DEC_T], scalar=w,
                                                            in1=out_s, op0=ALU.mult, op1=ALU.add))

            def untile(i):
                for x in range(1 if i < 4 else 2):
                    ve.wait_ge(t5_ready, 12 * p + (kap(i) + x + 1))
                    if i < 4:
                        nc.vector.tensor_copy(PT[:, i % 2, 1, 0:(i + 1) * P], ps[:, 5, 0:(i + 1) * P])\
                            .then_inc(t5_done, 1)
                    else:
                        nc.vector.tensor_copy(PT[:, i % 2, x, 512:(i + 1) * P], ps[:, 5, 0:(i - 3) * P])\
                            .then_inc(t5_done, 1)

            def low_av(i):
                ve.wait_ge(av_hi, QB * p + (i + 1))
                nc.vector.tensor_tensor(n_lo[:, p, i * P:(i + 1) * P], ps[:, 6 + i % 2, 0:P],
                                        n_hi[:, p, i * P:(i + 1) * P].bitcast(f32), ALU.subtract).then_inc(av_lo, 1)

            for i in range(QB):
                for hh in range(2):
                    u = 2 * i + hh
                    ve.wait_ge(s_ready, 2 * QB * p + (u + 1))
                    diag = psf[:, 1024 * hh + i * P:1024 * hh + (i + 1) * P]
                    step.hit(nc.vector.tensor_tensor(diag, diag, tri[:, :], ALU.add))
                    step.sync()
                    step.hit(nc.vector.reduce_max(stat[:, u % 4:u % 4 + 1], psf[:, 1024 * hh:1024 * hh + (i + 1) * P], AX.X))
                    step.sync()
                    nc.vector.tensor_scalar(stat[:, 4 + u % 4:5 + u % 4], stat[:, u % 4:u % 4 + 1], -SCALE, None,
                                            ALU.mult).then_inc(s_max, 1)
                if i:
                    untile(i - 1)
                for x in range(4 * i, min(4 * i + 4, TAPS)):
                    tap(x)
                for hh in range(2):
                    u = 2 * i + hh
                    ve.wait_ge(s_free, 2 * QB * p + (2 + u + 1))
                    step.hit(nc.vector.reciprocal(stat[:, 12 + u % 4:13 + u % 4], stat[:, 8 + u % 4:9 + u % 4]))
                    step.sync()
                    w = (i + 1) * P
                    nc.vector.tensor_scalar(pr[:, i % 2, hh, 0:w], pr[:, i % 2, hh, 0:w],
                                            stat[:, 12 + u % 4:13 + u % 4], None, ALU.mult).then_inc(p_norm, 1)
                if i:
                    low_av(i - 1)
            untile(QB - 1)
            low_av(QB - 1)
            assert step.n - done_before == per_pair, (step.n - done_before, per_pair)
        step.off = 0
        step.n = done_before + per_pair * PAIRS
        step.sync()
        ve.wait_ge(out_state, 16 * (3 + CC))
        nc.vector.tensor_copy(stat[:, 0:1], stat[:, 4:5]).then_inc(conv_done, 1)

        for r in range(NRB):
            c = cacc[:, :, rows(r)]
            for m in range(2):
                y = Y_LN + 2 * r + m
                if m == 0:
                    src = c
                    if r:
                        ve.wait_ge(ln_lo, r)
                else:
                    ve.wait_ge(ln_sq, r + 1)
                    src = lnsq[:, :, :]
                nc.vector.tensor_reduce(sqs[:, 0, :], src.rearrange("p c n -> p n c"), AX.X, ALU.add).then_inc(ln_red, 1)
                ve.wait_ge(one_ready, y + 1)
                if m == 0:
                    nc.vector.tensor_scalar(sqs[:, 1, :], ps[:, 4 + y % 4, 0:RB], 1.0 / CONV_CH, None, ALU.mult)\
                        .then_inc(one_free, 1)
                    ve.wait_ge(one_free, 4 + y + 1)
                    nc.vector.tensor_tensor(c, c, sqs[:, 1:2, :].broadcast_to([P, CC, RB]), ALU.subtract)\
                        .then_inc(ln_cent, 1)
                else:
                    ve.wait_ge(ln_root, r + 1)
                    nc.vector.reciprocal(sqs[:, 2, :], sqs[:, 2, :]).then_inc(one_free, 1)
                    ve.wait_ge(one_free, 4 + y + 1)
                    nc.vector.tensor_tensor(c, c, sqs[:, 2:3, :].broadcast_to([P, CC, RB]), ALU.mult)\
                        .then_inc(ln_scaled, 1)
            ve.wait_ge(ln_hi, r + 1)
            nc.vector.tensor_tensor(n_lo[:, CC:KC, rows(r)], c, n_hi[:, CC:KC, rows(r)].bitcast(f32), ALU.subtract)\
                .then_inc(ln_lo, 1)

        ve.wait_ge(st_ready, 1)
        nc.vector.tensor_copy(ckvnew[:, :], ps[0:NEW, 5, 0:KV_RANK]).then_inc(st_done, 1)
        st = 1
        for grp in range(2):
            ve.wait_ge(ss_ready, grp + 1)
            step.hit(nc.vector.tensor_tensor(ps[:, 4, 0:NEW], ps[:, 4, 0:NEW], smask[:, grp, :], ALU.add))
            step.hit(nc.vector.reduce_max(stat[:, 4:5], psf[:, 0:PAST], AX.X))
            step.sync()
            step.hit(nc.vector.reduce_max(stat[:, 5:6], ps[:, 4, 0:NEW], AX.X))
            step.sync()
            step.hit(nc.vector.tensor_tensor(stat[:, 6:7], stat[:, 4:5], stat[:, 5:6], ALU.max))
            step.sync()
            nc.vector.tensor_scalar(stat[:, 1:2], stat[:, 6:7], -SCALE, None, ALU.mult).then_inc(ss_max, 1)
            ve.wait_ge(ss_exp, grp + 1)
            step.hit(nc.vector.tensor_tensor(stat[:, 7:8], stat[:, 2:3], stat[:, 3:4], ALU.add))
            step.sync()
            step.hit(nc.vector.reciprocal(stat[:, 8:9], stat[:, 7:8]))
            step.sync()
            nc.vector.tensor_scalar(SS[:, :], SS[:, :], stat[:, 8:9], None, ALU.mult).then_inc(ss_norm, 1)
            for c in range(0, N_PAGES + 1, 4):
                st += 1
                ve.wait_ge(st_ready, st)
                if c < N_PAGES:
                    nc.vector.tensor_copy(PT2[:, c:c + 4, :],
                                          ps[:, 5 + (st - 1) % 2, :].rearrange("p (a n) -> p a n", a=4)).then_inc(st_done, 1)
                else:
                    nc.vector.tensor_copy(PT2[0:NEW, N_PAGES, :], ps[0:NEW, 5 + (st - 1) % 2, 0:P]).then_inc(st_done, 1)
            st += 1
            ve.wait_ge(st_ready, st)
            nc.vector.tensor_copy(olat[:, :], ps[:, 7, 0:KV_RANK]).then_inc(st_done, 1)
            st += 1
            ve.wait_ge(st_ready, st)
            nc.vector.tensor_copy(olatT[:, :, grp, :], ps[:, 5, 0:KV_RANK].rearrange("p (c n) -> p c n", c=VC))\
                .then_inc(st_done, 1)
        ve.wait_ge(av_hi, PAIRS * QB + 1)
        nc.vector.tensor_tensor(n_lo[:, 0:PAIRS, SEQ:ROWS], ps[:, 6, 0:PAIRS * NEW].rearrange("p (a n) -> p a n", a=PAIRS),
                                n_hi[:, 0:PAIRS, SEQ:ROWS].bitcast(f32), ALU.subtract).then_inc(av_lo, 1)

        for o in range(RING):
            low(N_WO + o, (N_WO + o) % RING)
        for o in range(KC - 1):
            for r in range(NRB):
                add_tile(o, r, Y_WO + NRB * o + r, 1.0)
            if o + RING < KC:
                low(N_WO + o + RING, (N_WO + o) % RING)
            elif o + RING < KC + 4:
                low(N_WO + o + RING, (N_WO + o) % RING)
        yl = Y_WO + NRB * (KC - 1)
        wo_y = [yl, yl + 1, yl + 3]
        norm_tail(2, G_FF2, lambda r: add_tile(KC - 1, r, wo_y[r], 1.0), [yl + 2, yl + 4, yl + 5])
        ffn(N_FF2, T_FF2, Y_FF2, 2, FF2_RING, [(N_PLE, PLE_RING["pp0"]), (N_PLE + 1, PLE_RING["g0"])], G_PLE)

        for r in range(NRB):
            n = N_PLE + 2 + r
            ve.wait_ge(w_hi, n + 1)
            step.hit(nc.vector.tensor_tensor(hid_lo[:, :, rows(r)],
                                             raw[n % RAW][:, 0:VC * RB].rearrange("p (c n) -> p c n", c=VC),
                                             hid_hi[:, :, rows(r)].bitcast(f32), ALU.subtract))
            step.sync()
            nc.vector.tensor_copy(stat[:, 0:1], stat[:, 4:5]).then_inc(p_ready, 1)
            nc.vector.tensor_copy(stat[:, 1:2], stat[:, 4:5]).then_inc(w_split, 1)
        lows = [x for x in PLE_ORDER[5:]]
        for x in lows[:4]:
            low(N_PLE + PLE_ORDER.index(x), PLE_RING[x])

        def embed(o, r):
            t = T_PLE + NRB * o + r
            ve.wait_ge(act_gate, t + 1)
            nc.vector.tensor_tensor(prod[:, t % 2, :], gact[:, t % 2, :], ps[:, 2 * (t % 2) + 1, 0:RB], ALU.mult)\
                .then_inc(pair_free, 1)
            ve.wait_ge(pair_free, 2 + t + 1)
            nc.vector.tensor_tensor(h[:, o, rows(r)], h[:, o, rows(r)], prod[:, t % 2, :], ALU.add)\
                .then_inc(ple_added, 1)

        for o in range(KC - 1):
            for r in range(NRB):
                embed(o, r)
            if o < 4:
                low(N_PLE + PLE_ORDER.index(lows[4 + o]), PLE_RING[lows[4 + o]])
        norm_tail(4, G_FIN, lambda r: embed(KC - 1, r), [Y_PLE, Y_PLE + 1, Y_PLE + 2])

    ctx.close()


def kernel(x_prompt, x_sample, cache_ckv, cache_kpe, state_conv, page_table, p_prompt, p_sample,
           g_ff1, w1_gate, w1_up, w1_down, g_mix, w_in, g_q, w_q_up, g_kv, w_uk, w_uv,
           conv_w, conv_b, g_cn, b_cn, w_o, g_ff2, w2_gate, w2_up, w2_down,
           g_ple, w_pg, b_pg, w_pp, g_final):
    import numpy as np
    import concourse.bacc as bacc
    from concourse.bass_utils import run_bass_kernel_spmd

    f = np.float32

    def A(x):
        return np.asarray(x)

    def by_chunk(v):
        return A(v).reshape(-1, P).T

    def cols(w):
        w = A(w)
        kk, nn = w.shape[0] // P, w.shape[1] // P
        return w.reshape(kk, P, nn, P).transpose(2, 1, 0, 3).reshape(nn, P, kk * P)

    def ffn_slots(wg, wu, wd):
        g, u, d = cols(wg[0]), cols(wu[0]), A(wd[0]).reshape(-1, P, D_MODEL)
        s = np.stack([g[0::2], u[0::2], g[1::2], u[1::2], d[0::2], d[1::2]], axis=1)
        return s.reshape(-1, P, 1024)

    wi = A(w_in[0])
    o3 = Q_RANK + KV_RANK + ROPE
    lat = np.concatenate([wi[:, :o3], np.zeros((D_MODEL, 6 * P - o3), f)], axis=1)
    ca, cb = cols(wi[:, o3:o3 + CONV_CH]), cols(wi[:, o3 + CONV_CH:])
    win = np.concatenate([cols(lat), np.stack([ca, cb], axis=1).reshape(-1, P, 1024)])
    pT = np.concatenate([A(p_prompt[0, 0]), A(p_sample[0]).reshape(NEW, -1)]).T
    pT = pT.reshape(VC, P, NRB, RB).transpose(2, 1, 0, 3).reshape(NRB, P, VC * RB)
    pT = np.concatenate([pT, np.zeros((NRB, P, 1024 - VC * RB), f)], axis=2)
    wg, wp = cols(w_pg[0]), cols(w_pp[0])
    wp = wp.reshape(2, 4, P, VC * P).transpose(0, 2, 1, 3).reshape(2, P, 1024)
    named = {f"g{i}": wg[i] for i in range(KC)}
    named.update({f"p{i}": pT[i] for i in range(NRB)})
    named.update({f"pp{i}": wp[i] for i in range(2)})
    stream = np.concatenate([ffn_slots(w1_gate, w1_up, w1_down), win, cols(w_o[0]),
                             ffn_slots(w2_gate, w2_up, w2_down), np.stack([named[x] for x in PLE_ORDER])])

    wq = A(w_q_up[0]).reshape(QC, P, PAIRS, 2, NOPE + ROPE)
    pe = wq[..., NOPE:].transpose(2, 1, 0, 3, 4).reshape(PAIRS, P, -1)
    nope = wq[..., :NOPE].transpose(2, 1, 0, 3, 4).reshape(PAIRS, P, -1)
    uk = A(w_uk[0]).reshape(VC, P, PAIRS, 2 * NOPE).transpose(2, 1, 0, 3).reshape(PAIRS, P, -1)
    uv = A(w_uv[0]).reshape(VC, P, PAIRS, 2 * VH).transpose(2, 1, 0, 3).reshape(PAIRS, P, -1)
    ukT = A(w_uk[0]).reshape(KV_RANK, PAIRS, 2, NOPE).transpose(1, 3, 2, 0).reshape(PAIRS, NOPE, -1)
    ukT = np.concatenate([ukT, np.zeros((PAIRS, P - NOPE, ukT.shape[2]), f)], axis=1)
    pairw = np.concatenate([pe, nope, uk, uv, ukT], axis=2)

    xT = np.concatenate([A(x_prompt[0]), A(x_sample).reshape(NEW, -1)]).T
    xT = xT.reshape(KC, P, ROWS).transpose(1, 0, 2)
    hist = A(state_conv[0]).transpose(2, 0, 1).reshape(CC, P, DEC_B, HIST).transpose(1, 0, 2, 3)
    cw = A(conv_w[0]).T.reshape(CC, P, TAPS).transpose(1, 0, 2).reshape(P, -1)
    gains = np.concatenate([by_chunk(g_ff1), by_chunk(g_mix), by_chunk(g_ff2), by_chunk(g_ple), by_chunk(g_final),
                            by_chunk(g_q), by_chunk(g_kv), by_chunk(g_cn), by_chunk(b_cn), by_chunk(conv_b),
                            by_chunk(b_pg), cw], axis=1)

    half = ROPE // 2
    inv = (f(10000.0) ** (-np.arange(half, dtype=f) / f(half))).astype(f)
    pos = np.concatenate([np.arange(SEQ), np.tile(PAST + np.arange(DEC_T), DEC_B)]).astype(f)
    ang = (pos[:, None] * inv[None, :]).astype(f).T
    cos, sin = np.cos(ang), np.sin(ang)
    trig = np.stack([np.tile(np.concatenate([cos, cos]), (2, 1)), np.tile(np.concatenate([-sin, sin]), (2, 1))], axis=1)
    tri = np.where(np.arange(P)[:, None] >= np.arange(P)[None, :], 0.0, -1e30).astype(f)
    row = np.arange(P)
    smask = np.full((P, 2, NEW), -1e30, f)
    for grp in range(2):
        for c in range(NEW):
            ok = (4 * grp + row // TH == c // DEC_T) & (row % DEC_T >= c % DEC_T)
            smask[ok, grp, c] = 0.0

    cn = A(cache_ckv[0])
    ct = cn.transpose(0, 2, 1).reshape(-1, VC, P, PAGE).transpose(0, 2, 1, 3).reshape(-1, P, VC * PAGE)
    ck = A(cache_kpe[0]).transpose(0, 2, 1)
    wuv = A(w_uv[0]).reshape(VC, P, -1).transpose(1, 0, 2)

    ins = dict(wstream=stream, pairw=pairw, xT=xT, hist=hist, gains=gains, trig=trig.astype(f),
               ident=np.eye(P, dtype=f), tri=tri, smask=smask, cacheT=ct, cacheN=cn, cacheK=ck, wuv=wuv,
               ptab=A(page_table).reshape(1, -1))
    outs = dict(yT=(P, KC, ROWS), ckvT=(P, VC, ROWS), kpeT=(ROPE, ROWS), convp=(P, CC, HIST),
                convs=(P, CC, DEC_B, HIST))
    nc = bacc.Bacc("TRN2", target_bir_lowering=False, num_devices=1)
    arrays, args = {}, []
    for name, a in ins.items():
        a = np.ascontiguousarray(a)
        arrays[f"in_{name}"] = a
        args.append(nc.dram_tensor(f"in_{name}", a.shape, mybir.dt.from_np(a.dtype), kind="ExternalInput").ap())
    for name, shape in outs.items():
        args.append(nc.dram_tensor(f"out_{name}", shape, mybir.dt.float32, kind="ExternalOutput").ap())
    program(nc, *args)
    r = run_bass_kernel_spmd(nc, [arrays], core_ids=[0]).results[0]

    def rowsT(a):
        return a.transpose(2, 1, 0).reshape(ROWS, -1)

    y, c_, kp = rowsT(r["out_yT"]), rowsT(r["out_ckvT"]), r["out_kpeT"].T
    cp = r["out_convp"].transpose(2, 1, 0).reshape(1, 1, HIST, CONV_CH)
    cs_ = r["out_convs"].transpose(2, 3, 1, 0).reshape(1, DEC_B, HIST, CONV_CH)
    return (y[:SEQ].reshape(1, SEQ, D_MODEL), y[SEQ:].reshape(DEC_B, DEC_T, D_MODEL),
            c_[:SEQ].reshape(1, 1, SEQ, KV_RANK), kp[:SEQ].reshape(1, 1, SEQ, ROPE), cp,
            c_[SEQ:].reshape(1, DEC_B, DEC_T, KV_RANK), kp[SEQ:].reshape(1, DEC_B, DEC_T, ROPE), cs_)
```

```python
from contextlib import ExitStack

import concourse.bass as bass
from concourse import mybir

P = 128
D_MODEL, SEQ, DEC_B, DEC_T = 1024, 1024, 8, 4
ROWS = SEQ + DEC_B * DEC_T
NRB = 3
RB = ROWS // NRB
KC = D_MODEL // P
D_FF = 2816
GROUPS = D_FF // (2 * P)
Q_RANK, KV_RANK, ROPE, NOPE, VH = 384, 256, 32, 64, 64
QC, VC = Q_RANK // P, KV_RANK // P
HEADS = 8
PAIRS = HEADS // 2
CONV_CH, TAPS = 512, 31
CC = CONV_CH // P
HIST = TAPS - 1
PAGE, N_PAGES = 128, 16
PAST = PAGE * N_PAGES
TH = HEADS * DEC_T
NEW = DEC_B * DEC_T
QB = SEQ // P
SCALE = (NOPE + ROPE) ** -0.5
EPS = 1e-6

RAW = 2
RING = 6
FFN_SLOTS = GROUPS * 6
WIN_TILES = 14
N_FF1 = 0
N_WIN = N_FF1 + FFN_SLOTS
N_WO = N_WIN + WIN_TILES
N_FF2 = N_WO + KC
N_PLE = N_FF2 + FFN_SLOTS
PLE_ORDER = ["pp0", "g0", "p0", "p1", "p2", "g1", "g2", "g3", "pp1", "g4", "g5", "g6", "g7"]
PLE_RING = {"pp0": 4, "g0": 5, "g1": 0, "g2": 1, "g3": 2, "pp1": 3, "g4": 5, "g5": 0, "g6": 1, "g7": 2}
N_ALL = N_PLE + len(PLE_ORDER)
FF2_RING = N_FF2 % RING

G_FF1, G_MIX, G_FF2, G_PLE, G_FIN = (KC * i for i in range(5))
G_Q = 5 * KC
G_KV = G_Q + QC
G_CN = G_KV + VC
B_CN = G_CN + CC
B_CONV = B_CN + CC
B_PG = B_CONV + CC
W_CONV = B_PG + KC
N_GAINS = W_CONV + CC * TAPS

PW_PE = 0
PW_NOPE = PW_PE + QC * 2 * ROPE
PW_UK = PW_NOPE + QC * P
PW_UV = PW_UK + VC * P
PW_UKT = PW_UV + VC * P
PW = PW_UKT + 2 * KV_RANK

DOWN = NRB * KC
T_FF1 = 0
T_WIN = T_FF1 + 6 * GROUPS
T_FF2 = T_WIN + CC * NRB
T_PLE = T_FF2 + 6 * GROUPS
Y_NORM1 = 0
Y_FF1 = Y_NORM1 + NRB
Y_WIN = Y_FF1 + DOWN * GROUPS + 2
WIN_SINGLES = ([(0, 0), (1, 0), (2, 0), "sum", (3, 0)] + [(j, r) for r in (1, 2) for j in range(4)]
               + [(j, r) for j in (4, 5) for r in range(NRB)])
Y_LAT = Y_WIN + len(WIN_SINGLES)
Y_LN = Y_LAT + 2 * NRB
Y_WO = Y_LN + 2 * NRB
WO_ORDER = ([(o, r) for o in (0, 1) for r in range(NRB)] + [(o, 0) for o in range(2, 8)]
            + [(2, 1), (3, 1), (4, 1), "sum0", (5, 1), (6, 1), (7, 1), (2, 2), (3, 2), (4, 2), "sum1",
               (5, 2), (6, 2), (7, 2)])
Y_FF2 = Y_WO + len(WO_ORDER) + 1
Y_PLE = Y_FF2 + DOWN * GROUPS + NRB
PLE_TILES = [(4 * half + i, r) for half in range(2) for r in range(NRB) for i in range(4)]
C96 = 3
K96 = (KV_RANK + ROPE) // C96
TOK = 256
TILES = PAST // TOK
PPT = TOK // PAGE
T_BUFS, N_BUFS = 3, 2
LOOP_TAPS = QB
Z_PROJ = 12


class Tally:

    def __init__(self, eng, sem):
        self.eng, self.sem, self.n, self.off = eng, sem, 0, 0

    def hit(self, ins):
        ins.then_inc(self.sem, 1)
        self.n += 1

    def sync(self):
        self.eng.wait_ge(self.sem, self.off + self.n)


def program(nc, wstream, pairw, xT, hist, gains, trig, ident_d, tri_d, smask_d, cacheT, cacheN,
            wuv_d, ptab_d, yT, ckvT, kpeT, convp, convs):
    f32, f32r, i32 = mybir.dt.float32, mybir.dt.float32r, mybir.dt.int32
    ALU, ACT, AX = mybir.AluOpType, mybir.ActivationFunctionType, mybir.AxisListType
    ctx = ExitStack()

    def scope():
        return ExitStack()

    def sb(st, name, shape, dt=f32):
        return st.enter_context(nc.sbuf_tensor(name, shape, dt))

    ident = sb(ctx, "ident", [P, P])
    ones = sb(ctx, "ones", [P, P])
    gain = sb(ctx, "gain", [P, N_GAINS])
    tri = sb(ctx, "tri", [P, P])
    smask = sb(ctx, "smask", [P, 2, NEW])
    stat = sb(ctx, "stat", [P, 24])
    ptab = sb(ctx, "ptab", [1, DEC_B * N_PAGES], i32)
    h = sb(ctx, "h", [P, KC, ROWS])

    zone_bytes = 50816
    za = scope()
    hid_hi = sb(za, "hid_hi", [P, 2, ROWS], f32r)
    hid_lo = sb(za, "hid_lo", [P, 2, ROWS], f32r)
    sq = sb(za, "sq", [P, KC, RB])
    n32 = sb(za, "n32", [P, KC, RB])
    gact = sb(za, "gact", [P, 2, RB])
    prod = sb(za, "prod", [P, 2, RB])
    red = sb(za, "red", [P, RB])
    rstd = sb(za, "rstd", [P, RB])
    za.close()
    zs = scope()
    SS = sb(zs, "SS", [P, PAST + NEW])
    wuv = sb(zs, "wuv", [P, VC, HEADS * VH])
    zs.close()
    zl = scope()
    lnsq = sb(zl, "lnsq", [P, CC, RB])
    zl.close()
    zb = scope()
    cq = sb(zb, "cq", [P, QC, ROWS])
    ckv = sb(zb, "ckv", [P, VC, ROWS])
    kpe = sb(zb, "kpe", [ROPE, ROWS])
    sqs = sb(zb, "sqs", [P, QC, RB])
    vext = sb(zb, "vext", [P, CC, HIST + SEQ])
    vs = sb(zb, "vs", [P, CC, DEC_B, HIST + DEC_T])
    used = 4 * (CC * (HIST + SEQ) + CC * DEC_B * (HIST + DEC_T) + (QC + VC + 1) * ROWS + QC * RB)
    sb(zb, "pad_b", [P, (zone_bytes - used) // 4])

    zn = scope()
    n_hi = sb(zn, "n_hi", [P, KC, ROWS], f32r)
    n_lo = sb(zn, "n_lo", [P, KC, ROWS], f32r)
    zr = scope()
    raw = [sb(zr, f"raw{i}", [P, 1024]) for i in range(RAW)]
    whi = [sb(zr, f"whi{i}", [P, 1024], f32r) for i in range(RING)]
    wlo = [sb(zr, f"wlo{i}", [P, 1024], f32r) for i in range(RING)]
    zr.close()
    zc = scope()
    qabs = sb(zc, "qabs", [K96, C96, DEC_B, TH])
    newT = sb(zc, "newT", [K96, C96, NEW])
    z1 = scope()
    ttile = [sb(z1, f"ttile{i}", [K96, 4, C96, TOK]) for i in range(T_BUFS)]
    ntile = [sb(z1, f"ntile{i}", [P, 4, PPT, KV_RANK]) for i in range(N_BUFS)]
    z1.close()
    cs = sb(zc, "cs", [2 * ROPE, 2, ROWS])
    q = sb(zc, "q", [NOPE + ROPE, 2, ROWS])
    k = sb(zc, "k", [NOPE + ROPE, 2, SEQ])
    V = sb(zc, "V", [P, QB, P])
    pw = sb(zc, "pw", [P, PW])
    z2 = scope()
    qraw = sb(z2, "qraw", [2 * ROPE, ROWS])
    qsw = sb(z2, "qsw", [2 * ROPE, ROWS])
    z2.close()
    pr = sb(zc, "pr", [P, 2, 2, SEQ])
    zc.close()
    zn.close()
    zo = scope()
    sb(zo, "pad_o1", [P, CC * ROWS])
    z3 = scope()
    PT2 = sb(z3, "PT2", [P, N_PAGES + 1, P])
    olat = sb(z3, "olat", [P, KV_RANK])
    ckvnew = sb(z3, "ckvnew", [NEW, KV_RANK])
    olatT = sb(z3, "olatT", [P, VC, 2, P])
    z3.close()
    PT = sb(zo, "PT", [P, 2, 2, SEQ])
    sb(zo, "pad_o2", [P, CC * ROWS - 4 * SEQ + CC * ROWS])
    cacc = sb(zo, "cacc", [P, CC, ROWS])
    zo.close()
    zb.close()

    ps = ctx.enter_context(nc.psum_tensor("ps", [P, 8, 512], f32))
    psf = ps[:, :, :].rearrange("p b n -> p (b n)")

    def sem(name):
        return ctx.enter_context(nc.semaphore(name))

    x_in = [sem(f"x_in{r}") for r in range(NRB)]
    const_in = sem("const_in")
    hist_in = sem("hist_in")
    raw_in = [sem(f"raw_in{i}") for i in range(RAW)]
    ready0 = sem("ready0")
    w_hi = sem("w_hi")
    w_split = sem("w_split")
    pair_ready, pair_free = sem("pair_ready"), sem("pair_free")
    one_ready, one_free = sem("one_ready"), sem("one_free")
    act_gate = sem("act_gate")
    hid_high, hid_ready = sem("hid_high"), sem("hid_ready")
    p_ready = sem("p_ready")
    sq_ready, sq_summed = sem("sq_ready"), sem("sq_summed")
    root = sem("root")
    n32_ready, n_high, n_ready = sem("n32_ready"), sem("n_high"), sem("n_ready")
    ple_added = sem("ple_added")
    y_out = sem("y_out")
    lat_sq, lat_red, lat_root, lat_norm = sem("lat_sq"), sem("lat_red"), sem("lat_root"), sem("lat_norm")
    trig_in, pw_in = sem("trig_in"), sem("pw_in")
    kpe_ready = sem("kpe_ready")
    proj_ready, proj_free = sem("proj_ready"), sem("proj_free")
    rope_done = sem("rope_done")
    s_ready, s_max, s_free = sem("s_ready"), sem("s_max"), sem("s_free")
    p_norm = sem("p_norm")
    t4_ready, t4_done, t5_ready, t5_done = sem("t4_ready"), sem("t4_done"), sem("t5_ready"), sem("t5_done")
    av_ready, av_hi, av_lo = sem("av_ready"), sem("av_hi"), sem("av_lo")
    ln_red, ln_cent, ln_sq, ln_root, ln_scaled, ln_act, ln_hi, ln_lo = (
        sem(n) for n in ("ln_red", "ln_cent", "ln_sq", "ln_root", "ln_scaled", "ln_act", "ln_hi", "ln_lo"))
    t_in = [sem(f"t_in{i}") for i in range(T_BUFS)]
    n_in = [sem(f"n_in{i}") for i in range(N_BUFS)]
    t_used, n_used = sem("t_used"), sem("n_used")
    wuv_in = sem("wuv_in")
    ss_ready, ss_max, ss_exp, ss_norm = sem("ss_ready"), sem("ss_max"), sem("ss_exp"), sem("ss_norm")
    st_ready, st_done = sem("st_ready"), sem("st_done")
    out_state = sem("out_state")
    dve_step, act_step = sem("dve_step"), sem("act_step")

    def rows(r):
        return slice(r * RB, (r + 1) * RB)

    def kap(i):
        return i if i < 4 else 4 + 2 * (i - 4)

    def load_tile(eng, kind, n, j0):
        bufs, nb, used, arrived, src = ((ttile, T_BUFS, t_used, t_in, cacheT) if kind == "T"
                                        else (ntile, N_BUFS, n_used, n_in, cacheN))
        if n >= nb:
            eng.wait_ge(used, n - nb + 1)
        grp, c = divmod(n, TILES)
        with eng.Fori(j0, j0 + 2) as j:
            for pg in range(PPT):
                at = j * N_PAGES + (4 * grp * N_PAGES + PPT * c + pg)
                page = eng.value_load(ptab[0:1, bass.ds(at, 1)], min_val=0, max_val=cacheN.shape[0] - 1)
                dst = (bufs[n % nb][:, j, :, pg * PAGE:(pg + 1) * PAGE] if kind == "T" else bufs[n % nb][:, j, pg, :])
                eng.dma_start(dst, src[page]).then_inc(arrived[n % nb], 16)

    block = ctx.enter_context(nc.Block())

    @block.sync
    def _(sp):
        for r in range(NRB):
            sp.dma_start(h[:, :, rows(r)], xT[:, :, rows(r)]).then_inc(x_in[r], 16)
            if r == 0:
                for s in range(RAW):
                    sp.dma_start(raw[s][:, :], wstream[s]).then_inc(raw_in[s], 16)
                sp.dma_start(gain[:, :], gains).then_inc(const_in, 16)
        sp.dma_start(ident[:, :], ident_d).then_inc(const_in, 16)
        sp.dma_start(tri[:, :], tri_d).then_inc(const_in, 16)
        sp.dma_start(smask[:, :, :], smask_d).then_inc(const_in, 16)
        sp.dma_start(ptab[:, :], ptab_d).then_inc(const_in, 16)
        with sp.Fori(0, (N_WO - RAW) // RAW) as g:
            for s in range(RAW):
                sp.wait_ge(w_split, RAW * g + s + 1)
                sp.dma_start(raw[s][:, :], wstream[RAW * g + s + RAW]).then_inc(raw_in[s], 16)
        sp.wait_ge(pair_ready, T_FF2)
        sp.dma_start(cs[:, :, :], trig).then_inc(trig_in, 16)
        sp.dma_start(pw[:, :], pairw[0]).then_inc(pw_in, 16)
        with sp.Fori(1, PAIRS) as p:
            sp.wait_ge(proj_ready, Z_PROJ * p)
            sp.dma_start(pw[:, :], pairw[p]).then_inc(pw_in, 16)
        sp.wait_ge(const_in, 5 * 16)
        sp.wait_ge(av_ready, PAIRS * QB)
        for n in range(TILES):
            load_tile(sp, "T", n, 0)
        sp.dma_start(wuv[:, :, :], wuv_d).then_inc(wuv_in, 16)
        for n in range(TILES):
            load_tile(sp, "N", n, 0)
            if 2 <= n < 2 + T_BUFS:
                load_tile(sp, "T", TILES + n - 2, 0)
        for n in range(TILES + T_BUFS, 2 * TILES):
            load_tile(sp, "T", n, 0)
        for n in range(TILES, 2 * TILES):
            load_tile(sp, "N", n, 0)
        sp.wait_ge(n_used, 2 * TILES)
        for s in range(RAW):
            sp.dma_start(raw[(N_WO + s) % RAW][:, :], wstream[N_WO + s]).then_inc(raw_in[(N_WO + s) % RAW], 16)
        left = N_ALL - N_WO - RAW
        with sp.Fori(0, left // RAW) as g:
            for s in range(RAW):
                sp.wait_ge(w_split, RAW * g + (N_WO + s + 1))
                sp.dma_start(raw[s][:, :], wstream[RAW * g + (N_WO + s + RAW)]).then_inc(raw_in[s], 16)
        for n in range(N_WO + RAW + left // RAW * RAW, N_ALL):
            sp.wait_ge(w_split, n - RAW + 1)
            sp.dma_start(raw[n % RAW][:, :], wstream[n]).then_inc(raw_in[n % RAW], 16)

    @block.gpsimd
    def _(pool):
        nc.gpsimd.memset(ones[:, :], 1.0).then_inc(ready0, 1)
        nc.gpsimd.memset(stat[:, 23:24], EPS).then_inc(ready0, 1)
        nc.gpsimd.memset(stat[:, 16:17], 0.0).then_inc(pair_free, 2)
        nc.gpsimd.memset(stat[:, 17:18], 0.0).then_inc(one_free, 4)
        nc.gpsimd.memset(stat[:, 18:19], 0.0).then_inc(proj_free, 4)
        nc.gpsimd.memset(stat[:, 19:20], 0.0).then_inc(s_free, 2)
        nc.gpsimd.memset(stat[:, 20:21], 0.0).then_inc(t4_done, 1)
        nc.gpsimd.memset(stat[:, 21:22], 0.0).then_inc(t5_done, 1)
        nc.gpsimd.memset(stat[:, 22:23], 0.0).then_inc(av_lo, 2)
        pool.wait_ge(n_ready, 2 * NRB)
        nc.gpsimd.memset(vext[:, :, 0:HIST], 0.0).then_inc(ready0, 1)
        for c in range(CC):
            pool.dma_start(vs[:, c, :, 0:HIST], hist[:, c]).then_inc(hist_in, 16)
        pool.wait_ge(lat_norm, 2 * NRB)
        pool.dma_start(ckvT, ckv[:, :, :]).then_inc(out_state, 16)
        pool.wait_ge(kpe_ready, 1)
        pool.dma_start(kpeT, kpe[:, :]).then_inc(out_state, 16)
        pool.wait_ge(hist_in, 16 * CC)
        pool.wait_ge(pair_free, 2 + T_FF2)
        pool.dma_start(convp, vext[:, :, SEQ:SEQ + HIST]).then_inc(out_state, 16)
        for c in range(CC):
            pool.dma_start(convs[:, c], vs[:, c, :, DEC_T:DEC_T + HIST]).then_inc(out_state, 16)
        for r in range(NRB):
            pool.wait_ge(n32_ready, 4 * NRB + r + 1)
            pool.dma_start(yT[:, :, rows(r)], n32[:, :, :]).then_inc(y_out, 16)
        pool.wait_ge(y_out, 16 * NRB)
        pool.wait_ge(out_state, 16 * (3 + CC))

    @block.tensor
    def _(pe):
        def split_product(out, w_h, w_l, x_h, x_l, first, last):
            nc.tensor.matmul(out, w_l, x_h, start=first, stop=False)
            nc.tensor.matmul(out, w_h, x_l, start=False, stop=False)
            return nc.tensor.matmul(out, w_h, x_h, start=False, stop=last)

        def contract(out, ring, r, chunks=KC, src=(n_hi, n_lo), cols=0):
            for c in range(chunks):
                w = slice(cols + c * P, cols + (c + 1) * P)
                last = split_product(out, whi[ring][:, w], wlo[ring][:, w], src[0][:, c, rows(r)],
                                     src[1][:, c, rows(r)], c == 0, c == chunks - 1)
            return last

        def row_sum(y, wait_sem, wait_val, src):
            pe.wait_ge(wait_sem, wait_val)
            pe.wait_ge(one_free, y + 1)
            nc.tensor.matmul(ps[:, 4 + y % 4, 0:RB], ones[:, :], src, start=True, stop=True).then_inc(one_ready, 1)

        def norm_sum(norm, r, y):
            row_sum(y, sq_summed, NRB * norm + r + 1, red[:, :])

        def ffn(n0, t0, y0, norm, ring0):
            t0h = t0 - (CC * NRB if t0 else 0)

            def body(g, first, last):
                def hidden(t):
                    r, f = divmod(t, 2)
                    pe.wait_ge(w_split, 6 * g + (n0 + 2 * f + 1))
                    pe.wait_ge(n_ready, NRB * norm + r + 1)
                    pe.wait_ge(pair_free, 6 * g + (t0 + t + 1))
                    b = 2 * ((t0 + t) % 2)
                    contract(ps[:, b, 0:RB], (ring0 + 2 * f) % RING, r)
                    pe.wait_ge(w_split, 6 * g + (n0 + 2 * f + 2))
                    contract(ps[:, b + 1, 0:RB], (ring0 + 2 * f + 1) % RING, r).then_inc(pair_ready, 1)

                def down_part(o, r, f, y):
                    s = (ring0 + 4 + f) % RING
                    w = slice(o * P, (o + 1) * P)
                    return split_product(ps[:, 4 + y % 4, 0:RB], whi[s][:, w], wlo[s][:, w],
                                         hid_hi[:, f, rows(r)], hid_lo[:, f, rows(r)], f == 0, f == 1)

                def down(r):
                    y = y0 + KC * r + (r if last else 0)
                    pe.wait_ge(w_split, 6 * g + (n0 + 6))
                    o0 = 0
                    if r == NRB - 1:
                        pe.wait_ge(hid_ready, 6 * g + (t0h + 2 * r + 1))
                        for o in range(4):
                            pe.wait_ge(one_free, DOWN * g + (y + o + 1))
                            down_part(o, r, 0, y + o)
                        pe.wait_ge(hid_ready, 6 * g + (t0h + 2 * r + 2))
                        for o in range(4):
                            down_part(o, r, 1, y + o).then_inc(one_ready, 1)
                        o0 = 4
                    pe.wait_ge(hid_ready, 6 * g + (t0h + 2 * r + 2))
                    for o in range(o0, KC):
                        pe.wait_ge(one_free, DOWN * g + (y + o + 1))
                        down_part(o, r, 0, y + o)
                        down_part(o, r, 1, y + o).then_inc(one_ready, 1)

                yl = y0 + DOWN * g
                hidden(0)
                hidden(1)
                if first:
                    norm_sum(norm, 2, y0 - 1)
                hidden(2)
                down(0)
                hidden(3)
                if last:
                    norm_sum(norm + 1, 0, yl + KC)
                hidden(4)
                down(1)
                hidden(5)
                if last:
                    norm_sum(norm + 1, 1, yl + 2 * KC + 1)
                down(2)

            body(0, True, False)
            with pe.Fori(1, GROUPS - 1) as g:
                body(g, False, False)
            body(GROUPS - 1, False, True)

        pe.wait_ge(ready0, 2)
        norm_sum(0, 0, Y_NORM1)
        norm_sum(0, 1, Y_NORM1 + 1)
        ffn(N_FF1, T_FF1, Y_FF1, 0, 0)

        for i, tile in enumerate(WIN_SINGLES):
            y = Y_WIN + i
            if tile == "sum":
                norm_sum(1, 2, y)
                continue
            j, r = tile
            pe.wait_ge(w_split, N_WIN + j + 1)
            pe.wait_ge(n_ready, NRB + r + 1)
            pe.wait_ge(one_free, y + 1)
            contract(ps[:, 4 + y % 4, 0:RB], j % RING, r).then_inc(one_ready, 1)
        y = Y_LAT
        for c in range(CC):
            for r in range(NRB):
                t = T_WIN + c * NRB + r
                pe.wait_ge(w_split, N_WIN + 6 + 2 * c + 2)
                pe.wait_ge(pair_free, t + 1)
                b = 2 * (t % 2)
                contract(ps[:, b, 0:RB], (2 * c) % RING, r)
                contract(ps[:, b + 1, 0:RB], (2 * c + 1) % RING, r).then_inc(pair_ready, 1)
                x = c * NRB + r - 2
                if 0 <= x < 2 * NRB:
                    row_sum(y, lat_red, x + 1, sqs[:, 0, :])
                    y += 1

        pe.wait_ge(const_in, 5 * 16)
        with pe.Fori(0, PAIRS) as p:
            pe.wait_ge(pw_in, 16 * p + 16)

            def proj(z, m, n, kc, col, width, rhs, col0=0):
                out = ps[0:m, 4 + z % 4, col0:col0 + n]
                for c in range(kc):
                    last = nc.tensor.matmul(out, pw[:, col + c * width:col + (c + 1) * width], rhs(c),
                                            start=(c == 0), stop=(c == kc - 1))
                return last

            for z in range(3):
                if z == 2:
                    pe.wait_ge(av_lo, QB * p + 2)
                pe.wait_ge(proj_free, Z_PROJ * p + (z + 1))
                proj(z, 2 * ROPE, RB, QC, PW_PE, 2 * ROPE, lambda c: cq[:, c, rows(z)]).then_inc(proj_ready, 1)
            for z in range(3, 6):
                pe.wait_ge(proj_free, Z_PROJ * p + (z + 1))
                proj(z, P, RB, QC, PW_NOPE, P, lambda c: cq[:, c, rows(z - 3)]).then_inc(proj_ready, 1)
            for z in range(6, 8):
                pe.wait_ge(proj_free, Z_PROJ * p + (z + 1))
                s0 = (z - 6) * 512
                proj(z, P, 512, VC, PW_UK, P, lambda c: ckv[:, c, s0:s0 + 512]).then_inc(proj_ready, 1)
            for z in range(8, 10):
                pe.wait_ge(proj_free, Z_PROJ * p + (z + 1))
                for i in range(4):
                    s0 = ((z - 8) * 4 + i) * P
                    for c in range(VC):
                        last = nc.tensor.matmul(ps[:, 4 + z % 4, i * P:(i + 1) * P], ckv[:, c, s0:s0 + P],
                                                pw[:, PW_UV + c * P:PW_UV + (c + 1) * P],
                                                start=(c == 0), stop=(c == VC - 1))
                last.then_inc(proj_ready, 1)
            pe.wait_ge(proj_free, Z_PROJ * p + (4 + 6))
            for z in range(10, 12):
                pe.wait_ge(proj_free, Z_PROJ * p + (z + 1))
                for c in range(C96):
                    m = min(K96, KV_RANK - c * K96)
                    w0 = PW_UKT + (z - 10) * KV_RANK + c * K96
                    last = nc.tensor.matmul(ps[0:m, 4 + z % 4, c * NEW:(c + 1) * NEW], pw[0:NOPE, w0:w0 + m],
                                            q[0:NOPE, z - 10, SEQ:ROWS], start=True, stop=True)
                last.then_inc(proj_ready, 1)
            pe.wait_ge(rope_done, p + 1)
            pe.wait_ge(kpe_ready, 1)

            def scores(i):
                for hh in range(2):
                    pe.wait_ge(s_free, 2 * QB * p + (2 * i + hh + 1))
                    w = (i + 1) * P
                    for c in range(0, w, 512):
                        e = min(w, c + 512)
                        last = nc.tensor.matmul(psf[:, hh * 1024 + c:hh * 1024 + e], q[:, hh, i * P:(i + 1) * P],
                                                k[:, hh, c:e], start=True, stop=True)
                    last.then_inc(s_ready, 1)

            def transposes(i):
                for hh in range(2):
                    pe.wait_ge(p_norm, 2 * QB * p + (2 * i + hh + 1))
                    for c in range(0, i + 1, 4):
                        if i < 4:
                            bank, idx = 4 + hh, kap(i)
                        else:
                            bank, idx = 4 + c // 4, kap(i) + hh
                        ready, done = ((t4_ready, t4_done), (t5_ready, t5_done))[bank - 4]
                        pe.wait_ge(done, 12 * p + (idx + 1))
                        for j in range(c, min(i + 1, c + 4)):
                            last = nc.tensor.transpose(ps[:, bank, (j - c) * P:(j - c + 1) * P],
                                                       pr[:, i % 2, hh, j * P:(j + 1) * P], ident[:, :])
                        last.then_inc(ready, 1)

            def values(i):
                pe.wait_ge(t4_done, 12 * p + (1 + kap(i + 1)))
                pe.wait_ge(t5_done, 12 * p + (1 + kap(i + 1)))
                pe.wait_ge(av_lo, QB * p + (i + 1))
                for j in range(i + 1):
                    for hh in range(2):
                        last = nc.tensor.matmul(ps[VH * hh:VH * (hh + 1), 6 + i % 2, 0:P],
                                                V[:, j, VH * hh:VH * (hh + 1)], PT[:, i % 2, hh, j * P:(j + 1) * P],
                                                start=(j == 0), stop=(j == i))
                last.then_inc(av_ready, 1)

            scores(0)
            pe.wait_ge(proj_free, Z_PROJ * p + (4 + Z_PROJ))
            for i in range(QB):
                if i + 1 < QB:
                    scores(i + 1)
                transposes(i)
                values(i)

        pe.wait_ge(av_lo, PAIRS * QB + 2)
        for c in range(VC):
            last = nc.tensor.transpose(ps[0:NEW, 5, c * P:(c + 1) * P], ckv[:, c, SEQ:ROWS], ident[:, :])
        last.then_inc(st_ready, 1)
        st = 1
        for grp in range(2):
            if grp:
                pe.wait_ge(ss_exp, grp)
            for c8 in range(TILES + 1):
                n = TILES * grp + c8
                if c8 < TILES:
                    pe.wait_ge(t_in[n % T_BUFS], 64 * 2 * (n // T_BUFS + 1))
                for c in range(C96):
                    for j in range(4):
                        if c8 < TILES:
                            out = psf[TH * j:TH * (j + 1), c8 * TOK:(c8 + 1) * TOK]
                            src = ttile[n % T_BUFS][:, j, c, :]
                        else:
                            out = psf[TH * j:TH * (j + 1), PAST:PAST + NEW]
                            src = newT[:, c, :]
                        last = nc.tensor.matmul(out, qabs[:, c, 4 * grp + j, :], src, start=(c == 0),
                                                stop=(c == C96 - 1))
                last.then_inc(t_used if c8 < TILES else ss_ready, 1)
            pe.wait_ge(ss_norm, grp + 1)
            for c in range(0, N_PAGES + 1, 4):
                pe.wait_ge(st_done, st)
                for j in range(c, min(c + 4, N_PAGES)):
                    last = nc.tensor.transpose(ps[:, 5 + st % 2, (j - c) * P:(j - c + 1) * P],
                                               SS[:, j * P:(j + 1) * P], ident[:, :])
                if c == N_PAGES:
                    last = nc.tensor.transpose(ps[0:NEW, 5 + st % 2, 0:P], SS[:, PAST:PAST + NEW], ident[:, :])
                last.then_inc(st_ready, 1)
                st += 1
            pe.wait_ge(st_done, st)
            for c8 in range(TILES):
                n = TILES * grp + c8
                pe.wait_ge(n_in[n % N_BUFS], 64 * 2 * (n // N_BUFS + 1))
                for pg in range(PPT):
                    for j in range(4):
                        last = nc.tensor.matmul(ps[TH * j:TH * (j + 1), 7, 0:KV_RANK],
                                                PT2[:, PPT * c8 + pg, TH * j:TH * (j + 1)],
                                                ntile[n % N_BUFS][:, j, pg, :],
                                                start=(c8 == 0 and pg == 0), stop=False)
                last.then_inc(n_used, 1)
            for j in range(4):
                last = nc.tensor.matmul(ps[TH * j:TH * (j + 1), 7, 0:KV_RANK], PT2[0:NEW, N_PAGES, TH * j:TH * (j + 1)],
                                        ckvnew[:, :], start=False, stop=True)
            last.then_inc(st_ready, 1)
            st += 1
            pe.wait_ge(st_done, st)
            for c in range(VC):
                last = nc.tensor.transpose(ps[:, 5, c * P:(c + 1) * P], olat[:, c * P:(c + 1) * P], ident[:, :])
            last.then_inc(st_ready, 1)
            st += 1
        pe.wait_ge(st_done, st)
        pe.wait_ge(wuv_in, 16)
        for hd in range(HEADS):
            o = VH * (hd % 2)
            for c in range(VC):
                last = nc.tensor.matmul(
                    ps[o:o + VH, 6, (hd // 2) * NEW:(hd // 2 + 1) * NEW], wuv[:, c, hd * VH:(hd + 1) * VH],
                    olatT[:, c].rearrange("p g (j h t) -> p (g j) h t", j=4, h=HEADS)[:, :, hd, :],
                    start=(c == 0), stop=(c == VC - 1))
        last.then_inc(av_ready, 1)

        pe.wait_ge(av_lo, 2 + PAIRS * QB + 1)
        y = Y_LN
        for r in range(NRB):
            for m in range(2):
                row_sum(y, ln_red, 2 * r + m + 1, sqs[:, 0, :])
                y += 1

        for i, tile in enumerate(WO_ORDER):
            y = Y_WO + i
            if tile in ("sum0", "sum1"):
                norm_sum(2, int(tile[-1]), y)
                continue
            o, r = tile
            pe.wait_ge(ln_lo, r + 1)
            pe.wait_ge(w_split, N_WO + o + 1)
            pe.wait_ge(one_free, y + 1)
            contract(ps[:, 4 + y % 4, 0:RB], (N_WO + o) % RING, r).then_inc(one_ready, 1)

        ffn(N_FF2, T_FF2, Y_FF2, 2, FF2_RING)

        for i, (o, r) in enumerate(PLE_TILES):
            t = T_PLE + i
            pe.wait_ge(w_split, N_PLE + PLE_ORDER.index(f"g{o}") + 1)
            pe.wait_ge(pair_free, t + 1)
            pe.wait_ge(n_ready, NRB * 3 + r + 1)
            b = 2 * (t % 2)
            contract(ps[:, b, 0:RB], PLE_RING[f"g{o}"], r)
            pe.wait_ge(p_ready, r + 1)
            pe.wait_ge(w_split, N_PLE + PLE_ORDER.index(f"pp{o // 4}") + 1)
            contract(ps[:, b + 1, 0:RB], PLE_RING[f"pp{o // 4}"], r, VC, (hid_hi, hid_lo),
                     (o % 4) * VC * P).then_inc(pair_ready, 1)
            if i == 2:
                norm_sum(3, 2, Y_PLE - 1)
            if i in (17, 21):
                norm_sum(4, (i - 17) // 4, Y_PLE + (i - 17) // 4)
        norm_sum(4, 2, Y_PLE + 2)

    @block.scalar
    def _(act):
        step = Tally(act, act_step)

        def high(n, ring, idx=None, add=0):
            act.wait_ge(raw_in[n % RAW], 16 * (n // RAW + 1) + 8 * add)
            nc.scalar.activation(whi[ring][:, :], raw[n % RAW][:, :], ACT.Copy).then_inc(w_hi, 1)

        def squares(norm, r, sem_, val, src=h, dst=sq, ready=sq_ready, summed=sq_summed):
            act.wait_ge(sem_, val)
            kk = NRB * norm + r
            if kk:
                act.wait_ge(summed, kk)
            nc.scalar.activation(dst[:, :, :], src[:, :, rows(r)], ACT.Square).then_inc(ready, 1)

        def norm_high(norm, r):
            act.wait_ge(n32_ready, NRB * norm + r + 1)
            nc.scalar.activation(n_hi[:, :, rows(r)], n32[:, :, :], ACT.Copy).then_inc(n_high, 1)

        def norm_root(norm, r, y, then_high=True):
            act.wait_ge(one_ready, y + 1)
            if norm == 4 and r:
                act.wait_ge(n32_ready, NRB * norm + r)
            nc.scalar.activation(rstd[:, :], ps[:, 4 + y % 4, 0:RB], ACT.Sqrt, scale=1.0 / D_MODEL,
                                 bias=stat[:, 23:24]).then_inc(root, 1)
            if norm < 4 and then_high:
                norm_high(norm, r)

        def ffn(n0, t0, y0, norm, ring0, nexts):
            def body(g, first, last):
                def hidden(t):
                    r, f = divmod(t, 2)
                    act.wait_ge(pair_ready, 6 * g + (t0 + t + 1))
                    act.wait_ge(pair_free, 6 * g + (t0 + t + 1))
                    nc.scalar.activation(gact[:, t % 2, :], ps[:, 2 * ((t0 + t) % 2), 0:RB], ACT.Silu)\
                        .then_inc(act_gate, 1)
                    act.wait_ge(pair_free, 6 * g + (t0 + t + 3))
                    nc.scalar.activation(hid_hi[:, f, rows(r)], prod[:, t % 2, :], ACT.Copy).then_inc(hid_high, 1)

                def next_high(i):
                    if not last:
                        high(n0 + 6 + i, (ring0 + i) % RING, add=6 * g)
                    elif i < len(nexts):
                        high(*nexts[i])

                yl = y0 + DOWN * g
                hidden(0)
                act.wait_ge(one_ready, DOWN * g + (y0 - first))
                high(n0 + 4, (ring0 + 4) % RING, add=6 * g)
                hidden(1)
                high(n0 + 5, (ring0 + 5) % RING, add=6 * g)
                if first:
                    norm_root(norm, 2, y0 - 1)
                hidden(2)
                if last:
                    squares(norm + 1, 0, one_free, 4 + yl + KC)
                hidden(3)
                if last:
                    norm_root(norm + 1, 0, yl + KC)
                hidden(4)
                next_high(0)
                next_high(1)
                if last:
                    squares(norm + 1, 1, one_free, 4 + yl + 2 * KC + 1)
                hidden(5)
                if last:
                    norm_root(norm + 1, 1, yl + 2 * KC + 1, then_high=False)
                next_high(2)
                next_high(3)
                if last:
                    squares(norm + 1, 2, one_free, 4 + yl + 3 * KC + 2)
                    norm_high(norm + 1, 1)

            body(0, True, False)
            with act.Fori(1, GROUPS - 1) as g:
                body(g, False, False)
            body(GROUPS - 1, False, True)

        act.wait_ge(ready0, 2)
        high(N_FF1, 0)
        high(N_FF1 + 1, 1)
        squares(0, 0, x_in[0], 16)
        squares(0, 1, x_in[1], 16)
        norm_root(0, 0, Y_NORM1)
        high(N_FF1 + 2, 2)
        high(N_FF1 + 3, 3)
        squares(0, 2, x_in[2], 16)
        norm_root(0, 1, Y_NORM1 + 1)
        ffn(N_FF1, T_FF1, Y_FF1, 0, 0, [(N_WIN + j, j) for j in range(4)])

        act.wait_ge(one_ready, Y_WIN)
        for j in (4, 5):
            high(N_WIN + j, j)

        def lat_squares(m, r):
            n_src, c = ((cq, QC), (ckv, VC))[m]
            act.wait_ge(one_free, 4 + Y_WIN + WIN_SINGLES.index((4, 2)) + 1)
            if NRB * m + r:
                act.wait_ge(lat_norm, NRB * m + r)
            nc.scalar.activation(sqs[:, 0:c, :], n_src[:, :, rows(r)], ACT.Square).then_inc(lat_sq, 1)

        def gate(c, r):
            t = T_WIN + c * NRB + r
            act.wait_ge(pair_ready, t + 1)
            b = 2 * (t % 2) + 1
            if r < NRB - 1:
                nc.scalar.activation(vext[:, c, HIST + r * RB:HIST + (r + 1) * RB], ps[:, b, 0:RB], ACT.Sigmoid)\
                    .then_inc(act_gate, 1)
            else:
                nc.scalar.activation(vext[:, c, HIST + r * RB:HIST + SEQ], ps[:, b, 0:SEQ - r * RB], ACT.Sigmoid)
                nc.scalar.activation(vs[:, c, :, HIST:HIST + DEC_T],
                                     ps[:, b, SEQ - r * RB:RB].rearrange("p (b t) -> p b t", b=DEC_B), ACT.Sigmoid)\
                    .then_inc(act_gate, 1)

        def lat_root_(x):
            m, r = divmod(x, NRB)
            y = Y_LAT + x
            act.wait_ge(one_ready, y + 1)
            nc.scalar.activation(sqs[:, 1, :], ps[:, 4 + y % 4, 0:RB], ACT.Sqrt, scale=1.0 / (P * (QC, VC)[m]),
                                 bias=stat[:, 23:24]).then_inc(lat_root, 1)

        norm_root(1, 2, Y_WIN + 3)
        for j in range(6, 12):
            act.wait_ge(one_ready, Y_WIN + WIN_SINGLES.index((j - 6, 2)) + 1)
            high(N_WIN + j, j % RING)
        lat_squares(0, 0)
        for x in range(CC * NRB):
            gate(*divmod(x, NRB))
            if x == 2:
                for j in (12, 13):
                    high(N_WIN + j, j % RING)
            if 0 <= x - 2 < 2 * NRB:
                lat_root_(x - 2)
                if x - 1 < 2 * NRB:
                    lat_squares(*divmod(x - 1, NRB))

        with act.Fori(0, PAIRS) as p:
            def evac(z, dsts):
                act.wait_ge(proj_ready, Z_PROJ * p + (z + 1))
                for d, s in dsts:
                    last = nc.scalar.activation(d, s, ACT.Copy)
                last.then_inc(proj_free, 1)

            for z in range(3):
                evac(z, [(qraw[:, rows(z)], ps[0:2 * ROPE, 4 + z % 4, 0:RB])])
            for z in range(3, 6):
                evac(z, [(q[0:NOPE, hh, rows(z - 3)], ps[NOPE * hh:NOPE * (hh + 1), 4 + z % 4, 0:RB])
                         for hh in range(2)])
            for z in range(6, 8):
                s0 = (z - 6) * 512
                evac(z, [(k[0:NOPE, hh, s0:s0 + 512], ps[NOPE * hh:NOPE * (hh + 1), 4 + z % 4, :])
                         for hh in range(2)])
            for z in range(8, 10):
                evac(z, [(V[:, (z - 8) * 4:(z - 7) * 4, :], ps[:, 4 + z % 4, :].rearrange("p (s v) -> p s v", s=4))])
            for z in range(10, 12):
                evac(z, [(qabs[0:min(K96, KV_RANK - c * K96), c, :, bass.ds(8 * p + 4 * (z - 10), 4)],
                          ps[0:min(K96, KV_RANK - c * K96), 4 + z % 4, c * NEW:(c + 1) * NEW]
                          .rearrange("p (b t) -> p b t", b=DEC_B)) for c in range(C96)])

            def untile(i):
                for x in range(1 if i < 4 else 2):
                    act.wait_ge(t4_ready, 12 * p + (kap(i) + x + 1))
                    n = min(i + 1, 4) * P
                    nc.scalar.activation(PT[:, i % 2, x, 0:n], ps[:, 4, 0:n], ACT.Copy).then_inc(t4_done, 1)

            def high_av(i):
                act.wait_ge(av_ready, QB * p + (i + 1))
                nc.scalar.activation(n_hi[:, p, i * P:(i + 1) * P], ps[:, 6 + i % 2, 0:P], ACT.Copy).then_inc(av_hi, 1)

            for i in range(QB):
                if i:
                    untile(i - 1)
                for hh in range(2):
                    u = 2 * i + hh
                    act.wait_ge(s_max, 2 * QB * p + (u + 1))
                    w = (i + 1) * P
                    nc.scalar.activation(pr[:, i % 2, hh, 0:w], psf[:, 1024 * hh:1024 * hh + w], ACT.Exp,
                                         bias=stat[:, 4 + u % 4:5 + u % 4], scale=SCALE,
                                         accum_out=stat[:, 8 + u % 4:9 + u % 4]).then_inc(s_free, 1)
                if i:
                    high_av(i - 1)
            untile(QB - 1)
            high_av(QB - 1)

        act.wait_ge(const_in, 5 * 16)
        for n in range(TILES):
            load_tile(act, "T", n, 2)
        for n in range(2):
            load_tile(act, "N", n, 2)

        def sample_exp(grp):
            act.wait_ge(ss_max, grp + 1)
            if grp:
                act.wait_ge(st_done, 1 + 5)
            nc.scalar.activation(SS[:, 0:PAST], psf[:, 0:PAST], ACT.Exp, bias=stat[:, 1:2], scale=SCALE,
                                 accum_out=stat[:, 2:3])
            nc.scalar.activation(SS[:, PAST:PAST + NEW], ps[:, 4, 0:NEW], ACT.Exp, bias=stat[:, 1:2], scale=SCALE,
                                 accum_out=stat[:, 3:4]).then_inc(ss_exp, 1)

        sample_exp(0)
        for n in range(2, TILES):
            load_tile(act, "N", n, 2)
            if n < 2 + T_BUFS:
                load_tile(act, "T", TILES + n - 2, 2)
        for n in range(TILES + T_BUFS, 2 * TILES):
            load_tile(act, "T", n, 2)
        for n in range(TILES, TILES + 2):
            load_tile(act, "N", n, 2)
        sample_exp(1)
        for n in range(TILES + 2, 2 * TILES):
            load_tile(act, "N", n, 2)
        act.wait_ge(av_ready, PAIRS * QB + 1)
        nc.scalar.activation(n_hi[:, 0:PAIRS, SEQ:ROWS], ps[:, 6, 0:PAIRS * NEW].rearrange("p (a n) -> p a n", a=PAIRS),
                             ACT.Copy).then_inc(av_hi, 1)

        for r in range(NRB):
            act.wait_ge(ln_cent, r + 1)
            nc.scalar.activation(lnsq[:, :, :], cacc[:, :, rows(r)], ACT.Square).then_inc(ln_sq, 1)
            y = Y_LN + 2 * r + 1
            act.wait_ge(one_ready, y + 1)
            nc.scalar.activation(sqs[:, 2, :], ps[:, 4 + y % 4, 0:RB], ACT.Sqrt, scale=1.0 / CONV_CH,
                                 bias=stat[:, 23:24]).then_inc(ln_root, 1)
            act.wait_ge(ln_scaled, r + 1)
            for c in range(CC):
                nc.scalar.activation(cacc[:, c, rows(r)], cacc[:, c, rows(r)], ACT.Silu,
                                     scale=gain[:, G_CN + c:G_CN + c + 1], bias=gain[:, B_CN + c:B_CN + c + 1])\
                    .then_inc(ln_act, 1)
            act.wait_ge(ln_act, CC * (r + 1))
            nc.scalar.activation(n_hi[:, CC:KC, rows(r)], cacc[:, :, rows(r)], ACT.Copy).then_inc(ln_hi, 1)

        for o in range(KC):
            if o >= RING:
                act.wait_ge(one_ready, Y_WO + NRB * (o - RING + 1))
            high(N_WO + o, (N_WO + o) % RING)

        def wo_y(tile):
            return Y_WO + WO_ORDER.index(tile)

        act.wait_ge(out_state, 16 * (3 + CC))
        squares(2, 0, one_free, 4 + wo_y((7, 0)) + 1)
        norm_root(2, 0, wo_y("sum0"))
        squares(2, 1, one_free, 4 + wo_y((7, 1)) + 1)
        for s in range(4):
            act.wait_ge(one_ready, wo_y((2 + s, 2)) + 1)
            high(N_FF2 + s, (FF2_RING + s) % RING)
            if s == 2:
                norm_root(2, 1, wo_y("sum1"))
        squares(2, 2, one_free, 4 + wo_y((7, 2)) + 1)
        ffn(N_FF2, T_FF2, Y_FF2, 2, FF2_RING, [(N_PLE, PLE_RING["pp0"]), (N_PLE + 1, PLE_RING["g0"])])

        act.wait_ge(one_ready, Y_PLE - 1)
        for r in range(NRB):
            n = N_PLE + 2 + r
            act.wait_ge(raw_in[n % RAW], 16 * (n // RAW + 1))
            nc.scalar.activation(hid_hi[:, :, rows(r)], raw[n % RAW][:, 0:VC * RB].rearrange("p (c n) -> p c n", c=VC),
                                 ACT.Copy).then_inc(w_hi, 1)
        for x in ("g1", "g2", "g3", "pp1"):
            high(N_PLE + PLE_ORDER.index(x), PLE_RING[x])
        for i, (o, r) in enumerate(PLE_TILES):
            t = T_PLE + i
            act.wait_ge(pair_ready, t + 1)
            act.wait_ge(pair_free, t + 1)
            nc.scalar.activation(gact[:, t % 2, :], ps[:, 2 * (t % 2), 0:RB], ACT.Sigmoid,
                                 bias=gain[:, B_PG + o:B_PG + o + 1]).then_inc(act_gate, 1)
            if i == 2:
                norm_root(3, 2, Y_PLE - 1)
            if 8 <= i < 12:
                x = f"g{i - 4}"
                high(N_PLE + PLE_ORDER.index(x), PLE_RING[x])
            if i in (15, 19):
                squares(4, (i - 15) // 4, ple_added, i + 1)
            if i in (17, 21):
                norm_root(4, (i - 17) // 4, Y_PLE + (i - 17) // 4)
        squares(4, 2, ple_added, 24)
        norm_root(4, 2, Y_PLE + 2)

    @block.vector
    def _(ve):
        step = Tally(ve, dve_step)

        def low(n, ring, add=0):
            ve.wait_ge(w_hi, n + 1 + add)
            nc.vector.tensor_tensor(wlo[ring][:, :], raw[n % RAW][:, :], whi[ring][:, :].bitcast(f32), ALU.subtract)\
                .then_inc(w_split, 1)

        def norm_sum(norm, r, y):
            ve.wait_ge(sq_ready, NRB * norm + r + 1)
            if y is not None:
                ve.wait_ge(one_ready, y + 1)
            nc.vector.tensor_reduce(red[:, :], sq[:, :, :].rearrange("p c n -> p n c"), AX.X, ALU.add)\
                .then_inc(sq_summed, 1)

        def norm_recip(norm, r):
            ve.wait_ge(root, NRB * norm + r + 1)
            nc.vector.reciprocal(rstd[:, :], rstd[:, :]).then_inc(one_free, 1)

        def norm_apply(norm, r, y, g0, recip=True):
            if recip:
                norm_recip(norm, r)
            if norm == 4 and r:
                ve.wait_ge(y_out, 16 * r)
            ve.wait_ge(one_free, 4 + y + 1)
            for c in range(KC):
                last = nc.vector.scalar_tensor_tensor(out=n32[:, c, :], in0=h[:, c, rows(r)],
                                                      scalar=gain[:, g0 + c:g0 + c + 1], in1=rstd[:, :],
                                                      op0=ALU.mult, op1=ALU.mult)
            last.then_inc(n32_ready, 1)
            if norm < 4:
                ve.wait_ge(n_high, NRB * norm + r + 1)
                nc.vector.tensor_tensor(n_lo[:, :, rows(r)], n32[:, :, :], n_hi[:, :, rows(r)].bitcast(f32),
                                        ALU.subtract).then_inc(n_ready, 1)

        def add_tile(o, r, y, factor, base=0):
            ve.wait_ge(one_ready, base + (y + 1))
            nc.vector.scalar_tensor_tensor(out=h[:, o, rows(r)], in0=ps[:, 4 + y % 4, 0:RB], scalar=factor,
                                           in1=h[:, o, rows(r)], op0=ALU.mult, op1=ALU.add).then_inc(one_free, 1)

        def ffn(n0, t0, y0, norm, ring0, nexts, g_this, g_next):
            t0h = t0 - (CC * NRB if t0 else 0)

            def body(g, first, last):
                def hidden(t):
                    r, f = divmod(t, 2)
                    ve.wait_ge(act_gate, 6 * g + (t0 + t + 1))
                    nc.vector.tensor_tensor(prod[:, t % 2, :], gact[:, t % 2, :],
                                            ps[:, 2 * ((t0 + t) % 2) + 1, 0:RB], ALU.mult).then_inc(pair_free, 1)
                    ve.wait_ge(hid_high, 6 * g + (t0h + t + 1))
                    nc.vector.tensor_tensor(hid_lo[:, f, rows(r)], prod[:, t % 2, :],
                                            hid_hi[:, f, rows(r)].bitcast(f32), ALU.subtract).then_inc(hid_ready, 1)

                def next_low(i):
                    if not last:
                        low(n0 + 6 + i, (ring0 + i) % RING, 6 * g)
                    elif i < len(nexts):
                        low(*nexts[i])

                def adds(r, lo, hi):
                    for o in range(lo, hi):
                        add_tile(o, r, y0 + KC * r + (r if last else 0) + o, 0.5, DOWN * g)

                yl = y0 + DOWN * g
                hidden(0)
                low(n0 + 4, (ring0 + 4) % RING, 6 * g)
                hidden(1)
                low(n0 + 5, (ring0 + 5) % RING, 6 * g)
                if first:
                    norm_apply(norm, 2, y0 - 1, g_this)
                hidden(2)
                adds(0, 0, KC)
                if last:
                    norm_sum(norm + 1, 0, None)
                hidden(3)
                if last:
                    norm_apply(norm + 1, 0, yl + KC, g_next)
                hidden(4)
                next_low(0)
                adds(1, 0, 4)
                next_low(1)
                adds(1, 4, KC)
                if last:
                    norm_sum(norm + 1, 1, yl + KC)
                hidden(5)
                if last:
                    norm_recip(norm + 1, 1)
                adds(2, 0, 4)
                next_low(2)
                adds(2, 4, KC)
                next_low(3)
                if last:
                    norm_apply(norm + 1, 1, yl + 2 * KC + 1, g_next, recip=False)
                    norm_sum(norm + 1, 2, yl + 2 * KC + 1)

            body(0, True, False)
            with ve.Fori(1, GROUPS - 1) as g:
                body(g, False, False)
            body(GROUPS - 1, False, True)

        low(N_FF1, 0)
        low(N_FF1 + 1, 1)
        norm_sum(0, 0, None)
        ve.wait_ge(const_in, 5 * 16)
        norm_sum(0, 1, Y_NORM1)
        norm_apply(0, 0, Y_NORM1, G_FF1)
        low(N_FF1 + 2, 2)
        low(N_FF1 + 3, 3)
        norm_apply(0, 1, Y_NORM1 + 1, G_FF1)
        norm_sum(0, 2, Y_NORM1 + 1)
        ffn(N_FF1, T_FF1, Y_FF1, 0, 0, [(N_WIN + j, j) for j in range(4)], G_FF1, G_MIX)

        for j in (4, 5):
            low(N_WIN + j, j)

        def take(j, r):
            yy = Y_WIN + WIN_SINGLES.index((j, r))
            ve.wait_ge(one_ready, yy + 1)
            dst = (cq[:, j, rows(r)] if j < QC else ckv[:, j - QC, rows(r)] if j < QC + VC else kpe[:, rows(r)])
            src = ps[:, 4 + yy % 4, 0:RB] if j < QC + VC else ps[0:ROPE, 4 + yy % 4, 0:RB]
            nc.vector.tensor_copy(dst, src).then_inc(one_free, 1)

        def lat_sum(m, r):
            ve.wait_ge(lat_sq, NRB * m + r + 1)
            for x in range(1, (QC, VC)[m]):
                last = nc.vector.tensor_tensor(sqs[:, 0, :], sqs[:, 0, :], sqs[:, x, :], ALU.add)
                if x < (QC, VC)[m] - 1:
                    step.hit(last)
                    step.sync()
            last.then_inc(lat_red, 1)

        def lat_apply(m, r):
            src, c, g0 = ((cq, QC, G_Q), (ckv, VC, G_KV))[m]
            yy = Y_LAT + NRB * m + r
            ve.wait_ge(lat_root, NRB * m + r + 1)
            nc.vector.reciprocal(sqs[:, 1, :], sqs[:, 1, :]).then_inc(one_free, 1)
            ve.wait_ge(one_free, 4 + yy + 1)
            for x in range(c):
                last = nc.vector.scalar_tensor_tensor(out=src[:, x, rows(r)], in0=src[:, x, rows(r)],
                                                      scalar=gain[:, g0 + x:g0 + x + 1], in1=sqs[:, 1, :],
                                                      op0=ALU.mult, op1=ALU.mult)
            last.then_inc(lat_norm, 1)

        def glu(c, r):
            t = T_WIN + c * NRB + r
            ve.wait_ge(act_gate, t + 1)
            b = 2 * (t % 2)
            if r < NRB - 1:
                v = vext[:, c, HIST + r * RB:HIST + (r + 1) * RB]
                nc.vector.tensor_tensor(v, v, ps[:, b, 0:RB], ALU.mult).then_inc(pair_free, 1)
            else:
                v = vext[:, c, HIST + r * RB:HIST + SEQ]
                nc.vector.tensor_tensor(v, v, ps[:, b, 0:SEQ - r * RB], ALU.mult)
                v = vs[:, c, :, HIST:HIST + DEC_T]
                nc.vector.tensor_tensor(v, v, ps[:, b, SEQ - r * RB:RB].rearrange("p (b t) -> p b t", b=DEC_B),
                                        ALU.mult).then_inc(pair_free, 1)

        for tile in WIN_SINGLES:
            if tile == "sum":
                norm_apply(1, 2, Y_WIN + 3, G_MIX)
                continue
            take(*tile)
            if tile[0] == 4:
                low(N_WIN + 6 + tile[1], tile[1])
        for j in range(9, 12):
            low(N_WIN + j, j % RING)
        lat_sum(0, 0)
        for x in range(CC * NRB):
            glu(*divmod(x, NRB))
            if x == 2:
                for j in (12, 13):
                    low(N_WIN + j, j % RING)
            if 0 <= x - 2 < 2 * NRB:
                lat_apply(*divmod(x - 2, NRB))
                if x - 1 < 2 * NRB:
                    lat_sum(*divmod(x - 1, NRB))

        swap = [(i + ROPE // 2) % ROPE for i in range(ROPE)]
        ksw = sqs[0:ROPE, :, :].rearrange("p c n -> p (c n)")
        ve.wait_ge(trig_in, 16)
        ve.wait_ge(lat_norm, 2 * NRB)
        step.hit(nc.vector.stream_shuffle(ksw, kpe[:, :], swap))
        step.sync()
        step.hit(nc.vector.tensor_tensor(kpe[:, :], kpe[:, :], cs[0:ROPE, 0, :], ALU.mult))
        step.hit(nc.vector.tensor_tensor(ksw, ksw, cs[0:ROPE, 1, :], ALU.mult))
        step.sync()
        step.hit(nc.vector.tensor_tensor(kpe[:, :], kpe[:, :], ksw, ALU.add))
        step.sync()
        S0, S1 = ckv[:, 0, SEQ:ROWS], ckv[:, 1, SEQ:ROWS]
        for dst, src in ((newT[:, 0, :], S0[0:K96]), (newT[0:32, 1, :], S0[K96:P]), (newT[32:64, 1, :], S1[0:32]),
                         (newT[64:K96, 1, :], S1[32:64]), (newT[0:64, 2, :], S1[64:P]),
                         (newT[64:K96, 2, :], kpe[:, SEQ:ROWS])):
            nc.vector.tensor_copy(dst, src)
        nc.vector.tensor_copy(k[NOPE:NOPE + ROPE, 0, :], kpe[:, 0:SEQ])
        nc.vector.tensor_copy(k[NOPE:NOPE + ROPE, 1, :], kpe[:, 0:SEQ]).then_inc(kpe_ready, 1)
        ve.wait_ge(ready0, 3)
        ve.wait_ge(hist_in, 16 * CC)

        per_pair = 3 + 2 + 2 * LOOP_TAPS + 16 * 3
        done_before = step.n
        with ve.Fori(0, PAIRS) as p:
            step.off = per_pair * p
            ve.wait_ge(proj_free, Z_PROJ * p + (4 + 3))
            nc.vector.memset(stat[:, 22:23], 0.0)
            step.hit(nc.vector.stream_shuffle(qsw[:, :], qraw[:, :], swap))
            step.sync()
            step.hit(nc.vector.tensor_tensor(qraw[:, :], qraw[:, :], cs[:, 0, :], ALU.mult))
            step.hit(nc.vector.tensor_tensor(qsw[:, :], qsw[:, :], cs[:, 1, :], ALU.mult))
            step.sync()
            nc.vector.tensor_tensor(q[NOPE:NOPE + ROPE, 0, :], qraw[0:ROPE, :], qsw[0:ROPE, :], ALU.add)
            nc.vector.tensor_tensor(q[NOPE:NOPE + ROPE, 1, :], qraw[ROPE:2 * ROPE, :], qsw[ROPE:2 * ROPE, :],
                                    ALU.add).then_inc(rope_done, 1)
            ve.wait_ge(rope_done, p + 1)
            for hh in range(2):
                step.hit(nc.vector.tensor_copy(qabs[NOPE:K96, 2, :, bass.ds(8 * p + 4 * hh, 4)],
                                               q[NOPE:NOPE + ROPE, hh, SEQ:ROWS].rearrange("p (b t) -> p b t", b=DEC_B)))

            def tap(x):
                w = gain[:, bass.ds(p * TAPS + (W_CONV + x), 1)]
                out_s = cacc[:, p, SEQ:ROWS].rearrange("p (b t) -> p b t", b=DEC_B)
                if x == 0:
                    b = gain[:, bass.ds(p + B_CONV, 1)]
                    step.hit(nc.vector.tensor_scalar(cacc[:, p, 0:SEQ], vext[:, p, 0:SEQ], w, b, ALU.mult, ALU.add))
                    step.hit(nc.vector.tensor_scalar(out_s, vs[:, p, :, 0:DEC_T], w, b, ALU.mult, ALU.add))
                else:
                    step.sync()
                    step.hit(nc.vector.scalar_tensor_tensor(out=cacc[:, p, 0:SEQ], in0=vext[:, p, x:x + SEQ],
                                                            scalar=w, in1=cacc[:, p, 0:SEQ], op0=ALU.mult, op1=ALU.add))
                    step.hit(nc.vector.scalar_tensor_tensor(out=out_s, in0=vs[:, p, :, x:x + DEC_T], scalar=w,
                                                            in1=out_s, op0=ALU.mult, op1=ALU.add))

            def untile(i):
                for x in range(1 if i < 4 else 2):
                    ve.wait_ge(t5_ready, 12 * p + (kap(i) + x + 1))
                    if i < 4:
                        nc.vector.tensor_copy(PT[:, i % 2, 1, 0:(i + 1) * P], ps[:, 5, 0:(i + 1) * P])\
                            .then_inc(t5_done, 1)
                    else:
                        nc.vector.tensor_copy(PT[:, i % 2, x, 512:(i + 1) * P], ps[:, 5, 0:(i - 3) * P])\
                            .then_inc(t5_done, 1)

            def low_av(i):
                ve.wait_ge(av_hi, QB * p + (i + 1))
                nc.vector.tensor_tensor(n_lo[:, p, i * P:(i + 1) * P], ps[:, 6 + i % 2, 0:P],
                                        n_hi[:, p, i * P:(i + 1) * P].bitcast(f32), ALU.subtract).then_inc(av_lo, 1)

            for i in range(QB):
                for hh in range(2):
                    u = 2 * i + hh
                    ve.wait_ge(s_ready, 2 * QB * p + (u + 1))
                    diag = psf[:, 1024 * hh + i * P:1024 * hh + (i + 1) * P]
                    step.hit(nc.vector.tensor_tensor(diag, diag, tri[:, :], ALU.add))
                    step.sync()
                    step.hit(nc.vector.reduce_max(stat[:, u % 4:u % 4 + 1], psf[:, 1024 * hh:1024 * hh + (i + 1) * P], AX.X))
                    step.sync()
                    nc.vector.tensor_scalar(stat[:, 4 + u % 4:5 + u % 4], stat[:, u % 4:u % 4 + 1], -SCALE, None,
                                            ALU.mult).then_inc(s_max, 1)
                if i:
                    untile(i - 1)
                tap(i)
                for hh in range(2):
                    u = 2 * i + hh
                    ve.wait_ge(s_free, 2 * QB * p + (2 + u + 1))
                    step.hit(nc.vector.reciprocal(stat[:, 12 + u % 4:13 + u % 4], stat[:, 8 + u % 4:9 + u % 4]))
                    step.sync()
                    w = (i + 1) * P
                    nc.vector.tensor_scalar(pr[:, i % 2, hh, 0:w], pr[:, i % 2, hh, 0:w],
                                            stat[:, 12 + u % 4:13 + u % 4], None, ALU.mult).then_inc(p_norm, 1)
                if i:
                    low_av(i - 1)
            untile(QB - 1)
            low_av(QB - 1)
            assert step.n - done_before == per_pair, (step.n - done_before, per_pair)
        step.off = 0
        step.n = done_before + per_pair * PAIRS
        step.sync()

        taps = [(c, x) for x in range(LOOP_TAPS, TAPS) for c in range(CC)]
        written = [0] * CC

        def convolve(n):
            for c, x in taps[:n]:
                w = gain[:, W_CONV + c * TAPS + x:W_CONV + c * TAPS + x + 1]
                if written[c]:
                    ve.wait_ge(dve_step, written[c])
                step.hit(nc.vector.scalar_tensor_tensor(out=cacc[:, c, 0:SEQ], in0=vext[:, c, x:x + SEQ], scalar=w,
                                                        in1=cacc[:, c, 0:SEQ], op0=ALU.mult, op1=ALU.add))
                out_s = cacc[:, c, SEQ:ROWS].rearrange("p (b t) -> p b t", b=DEC_B)
                step.hit(nc.vector.scalar_tensor_tensor(out=out_s, in0=vs[:, c, :, x:x + DEC_T], scalar=w,
                                                        in1=out_s, op0=ALU.mult, op1=ALU.add))
                written[c] = step.n
            del taps[:n]

        ve.wait_ge(st_ready, 1)
        nc.vector.tensor_copy(ckvnew[:, :], ps[0:NEW, 5, 0:KV_RANK]).then_inc(st_done, 1)
        st = 1
        for grp in range(2):
            convolve(26 if grp == 0 else 20)
            ve.wait_ge(ss_ready, grp + 1)
            step.hit(nc.vector.tensor_tensor(ps[:, 4, 0:NEW], ps[:, 4, 0:NEW], smask[:, grp, :], ALU.add))
            step.hit(nc.vector.reduce_max(stat[:, 4:5], psf[:, 0:PAST], AX.X))
            step.sync()
            step.hit(nc.vector.reduce_max(stat[:, 5:6], ps[:, 4, 0:NEW], AX.X))
            step.sync()
            step.hit(nc.vector.tensor_tensor(stat[:, 6:7], stat[:, 4:5], stat[:, 5:6], ALU.max))
            step.sync()
            nc.vector.tensor_scalar(stat[:, 1:2], stat[:, 6:7], -SCALE, None, ALU.mult).then_inc(ss_max, 1)
            ve.wait_ge(ss_exp, grp + 1)
            step.hit(nc.vector.tensor_tensor(stat[:, 7:8], stat[:, 2:3], stat[:, 3:4], ALU.add))
            step.sync()
            step.hit(nc.vector.reciprocal(stat[:, 8:9], stat[:, 7:8]))
            step.sync()
            nc.vector.tensor_scalar(SS[:, :], SS[:, :], stat[:, 8:9], None, ALU.mult).then_inc(ss_norm, 1)
            for c in range(0, N_PAGES + 1, 4):
                st += 1
                ve.wait_ge(st_ready, st)
                if c < N_PAGES:
                    nc.vector.tensor_copy(PT2[:, c:c + 4, :],
                                          ps[:, 5 + (st - 1) % 2, :].rearrange("p (a n) -> p a n", a=4)).then_inc(st_done, 1)
                else:
                    nc.vector.tensor_copy(PT2[0:NEW, N_PAGES, :], ps[0:NEW, 5 + (st - 1) % 2, 0:P]).then_inc(st_done, 1)
            st += 1
            convolve(22 if grp == 0 else len(taps))
            ve.wait_ge(st_ready, st)
            nc.vector.tensor_copy(olat[:, :], ps[:, 7, 0:KV_RANK]).then_inc(st_done, 1)
            st += 1
            ve.wait_ge(st_ready, st)
            nc.vector.tensor_copy(olatT[:, :, grp, :], ps[:, 5, 0:KV_RANK].rearrange("p (c n) -> p c n", c=VC))\
                .then_inc(st_done, 1)
        ve.wait_ge(av_hi, PAIRS * QB + 1)
        nc.vector.tensor_tensor(n_lo[:, 0:PAIRS, SEQ:ROWS], ps[:, 6, 0:PAIRS * NEW].rearrange("p (a n) -> p a n", a=PAIRS),
                                n_hi[:, 0:PAIRS, SEQ:ROWS].bitcast(f32), ALU.subtract).then_inc(av_lo, 1)

        step.sync()
        for r in range(NRB):
            c = cacc[:, :, rows(r)]
            for m in range(2):
                y = Y_LN + 2 * r + m
                if m == 0:
                    src = c
                    if r:
                        ve.wait_ge(ln_lo, r)
                else:
                    ve.wait_ge(ln_sq, r + 1)
                    src = lnsq[:, :, :]
                nc.vector.tensor_reduce(sqs[:, 0, :], src.rearrange("p c n -> p n c"), AX.X, ALU.add).then_inc(ln_red, 1)
                ve.wait_ge(one_ready, y + 1)
                if m == 0:
                    nc.vector.tensor_scalar(sqs[:, 1, :], ps[:, 4 + y % 4, 0:RB], 1.0 / CONV_CH, None, ALU.mult)\
                        .then_inc(one_free, 1)
                    ve.wait_ge(one_free, 4 + y + 1)
                    nc.vector.tensor_tensor(c, c, sqs[:, 1:2, :].broadcast_to([P, CC, RB]), ALU.subtract)\
                        .then_inc(ln_cent, 1)
                else:
                    ve.wait_ge(ln_root, r + 1)
                    nc.vector.reciprocal(sqs[:, 2, :], sqs[:, 2, :]).then_inc(one_free, 1)
                    ve.wait_ge(one_free, 4 + y + 1)
                    nc.vector.tensor_tensor(c, c, sqs[:, 2:3, :].broadcast_to([P, CC, RB]), ALU.mult)\
                        .then_inc(ln_scaled, 1)
            ve.wait_ge(ln_hi, r + 1)
            nc.vector.tensor_tensor(n_lo[:, CC:KC, rows(r)], c, n_hi[:, CC:KC, rows(r)].bitcast(f32), ALU.subtract)\
                .then_inc(ln_lo, 1)

        for o in range(RING):
            low(N_WO + o, (N_WO + o) % RING)

        def wo_y(tile):
            return Y_WO + WO_ORDER.index(tile)

        for tile in WO_ORDER:
            if tile == "sum0":
                norm_apply(2, 0, wo_y("sum0"), G_FF2)
                continue
            if tile == "sum1":
                norm_apply(2, 1, wo_y("sum1"), G_FF2)
                continue
            add_tile(*tile, wo_y(tile), 1.0)
            if tile in ((0, 2), (1, 2)):
                low(N_WO + RING + tile[0], (N_WO + tile[0]) % RING)
            if tile == (7, 0):
                norm_sum(2, 0, None)
            if tile == (7, 1):
                norm_sum(2, 1, wo_y("sum0"))
            if tile in ((3, 2), (4, 2), (5, 2), (6, 2)):
                s = tile[0] - 3
                low(N_FF2 + s, (FF2_RING + s) % RING)
        norm_sum(2, 2, wo_y("sum1"))
        ffn(N_FF2, T_FF2, Y_FF2, 2, FF2_RING, [(N_PLE, PLE_RING["pp0"]), (N_PLE + 1, PLE_RING["g0"])], G_FF2, G_PLE)

        for r in range(NRB):
            n = N_PLE + 2 + r
            ve.wait_ge(w_hi, n + 1)
            nc.vector.tensor_tensor(hid_lo[:, :, rows(r)], raw[n % RAW][:, 0:VC * RB].rearrange("p (c n) -> p c n", c=VC),
                                    hid_hi[:, :, rows(r)].bitcast(f32), ALU.subtract).then_inc(w_split, 1)
            ve.wait_ge(w_split, n + 1)
            nc.vector.memset(stat[:, 22:23], 0.0).then_inc(p_ready, 1)
        for x in ("g1", "g2", "g3", "pp1"):
            low(N_PLE + PLE_ORDER.index(x), PLE_RING[x])
        for i, (o, r) in enumerate(PLE_TILES):
            t = T_PLE + i
            ve.wait_ge(act_gate, t + 1)
            nc.vector.tensor_tensor(prod[:, t % 2, :], gact[:, t % 2, :], ps[:, 2 * (t % 2) + 1, 0:RB], ALU.mult)\
                .then_inc(pair_free, 1)
            ve.wait_ge(pair_free, 2 + t + 1)
            nc.vector.tensor_tensor(h[:, o, rows(r)], h[:, o, rows(r)], prod[:, t % 2, :], ALU.add)\
                .then_inc(ple_added, 1)
            if i == 2:
                norm_apply(3, 2, Y_PLE - 1, G_PLE)
            if 8 <= i < 12:
                x = f"g{i - 4}"
                low(N_PLE + PLE_ORDER.index(x), PLE_RING[x])
            if i in (15, 19):
                norm_sum(4, (i - 15) // 4, None if i == 15 else Y_PLE)
            if i in (17, 21):
                norm_apply(4, (i - 17) // 4, Y_PLE + (i - 17) // 4, G_FIN)
        norm_sum(4, 2, Y_PLE + 1)
        norm_apply(4, 2, Y_PLE + 2, G_FIN)

    ctx.close()


def kernel(x_prompt, x_sample, cache_ckv, cache_kpe, state_conv, page_table, p_prompt, p_sample,
           g_ff1, w1_gate, w1_up, w1_down, g_mix, w_in, g_q, w_q_up, g_kv, w_uk, w_uv,
           conv_w, conv_b, g_cn, b_cn, w_o, g_ff2, w2_gate, w2_up, w2_down,
           g_ple, w_pg, b_pg, w_pp, g_final):
    import numpy as np
    import concourse.bacc as bacc
    from concourse.bass_utils import run_bass_kernel_spmd

    f = np.float32

    def A(x):
        return np.asarray(x)

    def by_chunk(v):
        return A(v).reshape(-1, P).T

    def cols(w):
        w = A(w)
        kk, nn = w.shape[0] // P, w.shape[1] // P
        return w.reshape(kk, P, nn, P).transpose(2, 1, 0, 3).reshape(nn, P, kk * P)

    def ffn_slots(wg, wu, wd):
        g, u, d = cols(wg[0]), cols(wu[0]), A(wd[0]).reshape(-1, P, D_MODEL)
        s = np.stack([g[0::2], u[0::2], g[1::2], u[1::2], d[0::2], d[1::2]], axis=1)
        return s.reshape(-1, P, 1024)

    wi = A(w_in[0])
    o3 = Q_RANK + KV_RANK + ROPE
    lat = np.concatenate([wi[:, :o3], np.zeros((D_MODEL, 6 * P - o3), f)], axis=1)
    ca, cb = cols(wi[:, o3:o3 + CONV_CH]), cols(wi[:, o3 + CONV_CH:])
    win = np.concatenate([cols(lat), np.stack([ca, cb], axis=1).reshape(-1, P, 1024)])
    pT = np.concatenate([A(p_prompt[0, 0]), A(p_sample[0]).reshape(NEW, -1)]).T
    pT = pT.reshape(VC, P, NRB, RB).transpose(2, 1, 0, 3).reshape(NRB, P, VC * RB)
    pT = np.concatenate([pT, np.zeros((NRB, P, 1024 - VC * RB), f)], axis=2)
    wg, wp = cols(w_pg[0]), cols(w_pp[0])
    wp = wp.reshape(2, 4, P, VC * P).transpose(0, 2, 1, 3).reshape(2, P, 1024)
    named = {f"g{i}": wg[i] for i in range(KC)}
    named.update({f"p{i}": pT[i] for i in range(NRB)})
    named.update({f"pp{i}": wp[i] for i in range(2)})
    stream = np.concatenate([ffn_slots(w1_gate, w1_up, w1_down), win, cols(w_o[0]),
                             ffn_slots(w2_gate, w2_up, w2_down), np.stack([named[x] for x in PLE_ORDER])])

    wq = A(w_q_up[0]).reshape(QC, P, PAIRS, 2, NOPE + ROPE)
    pe = wq[..., NOPE:].transpose(2, 1, 0, 3, 4).reshape(PAIRS, P, -1)
    nope = wq[..., :NOPE].transpose(2, 1, 0, 3, 4).reshape(PAIRS, P, -1)
    uk = A(w_uk[0]).reshape(VC, P, PAIRS, 2 * NOPE).transpose(2, 1, 0, 3).reshape(PAIRS, P, -1)
    uv = A(w_uv[0]).reshape(VC, P, PAIRS, 2 * VH).transpose(2, 1, 0, 3).reshape(PAIRS, P, -1)
    ukT = A(w_uk[0]).reshape(KV_RANK, PAIRS, 2, NOPE).transpose(1, 3, 2, 0).reshape(PAIRS, NOPE, -1)
    ukT = np.concatenate([ukT, np.zeros((PAIRS, P - NOPE, ukT.shape[2]), f)], axis=1)
    pairw = np.concatenate([pe, nope, uk, uv, ukT], axis=2)

    xT = np.concatenate([A(x_prompt[0]), A(x_sample).reshape(NEW, -1)]).T
    xT = xT.reshape(KC, P, ROWS).transpose(1, 0, 2)
    hist = A(state_conv[0]).transpose(2, 0, 1).reshape(CC, P, DEC_B, HIST).transpose(1, 0, 2, 3)
    cw = A(conv_w[0]).T.reshape(CC, P, TAPS).transpose(1, 0, 2).reshape(P, -1)
    gains = np.concatenate([by_chunk(g_ff1), by_chunk(g_mix), by_chunk(g_ff2), by_chunk(g_ple), by_chunk(g_final),
                            by_chunk(g_q), by_chunk(g_kv), by_chunk(g_cn), by_chunk(b_cn), by_chunk(conv_b),
                            by_chunk(b_pg), cw], axis=1)

    half = ROPE // 2
    inv = (f(10000.0) ** (-np.arange(half, dtype=f) / f(half))).astype(f)
    pos = np.concatenate([np.arange(SEQ), np.tile(PAST + np.arange(DEC_T), DEC_B)]).astype(f)
    ang = (pos[:, None] * inv[None, :]).astype(f).T
    cos, sin = np.cos(ang), np.sin(ang)
    trig = np.stack([np.tile(np.concatenate([cos, cos]), (2, 1)), np.tile(np.concatenate([-sin, sin]), (2, 1))], axis=1)
    tri = np.where(np.arange(P)[:, None] >= np.arange(P)[None, :], 0.0, -1e30).astype(f)
    row = np.arange(P)
    smask = np.full((P, 2, NEW), -1e30, f)
    for grp in range(2):
        for c in range(NEW):
            ok = (4 * grp + row // TH == c // DEC_T) & (row % DEC_T >= c % DEC_T)
            smask[ok, grp, c] = 0.0

    cn = A(cache_ckv[0])
    ct = np.concatenate([cn, A(cache_kpe[0])], axis=2).transpose(0, 2, 1)
    ct = ct.reshape(-1, C96, K96, PAGE).transpose(0, 2, 1, 3)
    wuv = A(w_uv[0]).reshape(VC, P, -1).transpose(1, 0, 2)

    ins = dict(wstream=stream, pairw=pairw, xT=xT, hist=hist, gains=gains, trig=trig.astype(f),
               ident=np.eye(P, dtype=f), tri=tri, smask=smask, cacheT=ct, cacheN=cn, wuv=wuv,
               ptab=A(page_table).reshape(1, -1))
    outs = dict(yT=(P, KC, ROWS), ckvT=(P, VC, ROWS), kpeT=(ROPE, ROWS), convp=(P, CC, HIST),
                convs=(P, CC, DEC_B, HIST))
    nc = bacc.Bacc("TRN2", target_bir_lowering=False, num_devices=1)
    arrays, args = {}, []
    for name, a in ins.items():
        a = np.ascontiguousarray(a)
        arrays[f"in_{name}"] = a
        args.append(nc.dram_tensor(f"in_{name}", a.shape, mybir.dt.from_np(a.dtype), kind="ExternalInput").ap())
    for name, shape in outs.items():
        args.append(nc.dram_tensor(f"out_{name}", shape, mybir.dt.float32, kind="ExternalOutput").ap())
    program(nc, *args)
    r = run_bass_kernel_spmd(nc, [arrays], core_ids=[0]).results[0]

    def rowsT(a):
        return a.transpose(2, 1, 0).reshape(ROWS, -1)

    y, c_, kp = rowsT(r["out_yT"]), rowsT(r["out_ckvT"]), r["out_kpeT"].T
    cp = r["out_convp"].transpose(2, 1, 0).reshape(1, 1, HIST, CONV_CH)
    cs_ = r["out_convs"].transpose(2, 3, 1, 0).reshape(1, DEC_B, HIST, CONV_CH)
    return (y[:SEQ].reshape(1, SEQ, D_MODEL), y[SEQ:].reshape(DEC_B, DEC_T, D_MODEL),
            c_[:SEQ].reshape(1, 1, SEQ, KV_RANK), kp[:SEQ].reshape(1, 1, SEQ, ROPE), cp,
            c_[SEQ:].reshape(1, DEC_B, DEC_T, KV_RANK), kp[SEQ:].reshape(1, DEC_B, DEC_T, ROPE), cs_)
```

```python
from contextlib import ExitStack

import concourse.bass as bass
from concourse import mybir

P = 128
D_MODEL, SEQ, DEC_B, DEC_T = 1024, 1024, 8, 4
ROWS = SEQ + DEC_B * DEC_T
NRB = 3
RB = ROWS // NRB
KC = D_MODEL // P
D_FF = 2816
GROUPS = D_FF // (2 * P)
Q_RANK, KV_RANK, ROPE, NOPE, VH = 384, 256, 32, 64, 64
QC, VC = Q_RANK // P, KV_RANK // P
HEADS = 8
PAIRS = HEADS // 2
CONV_CH, TAPS = 512, 31
CC = CONV_CH // P
HIST = TAPS - 1
PAGE, N_PAGES = 128, 16
PAST = PAGE * N_PAGES
TH = HEADS * DEC_T
NEW = DEC_B * DEC_T
QB = SEQ // P
SCALE = (NOPE + ROPE) ** -0.5
EPS = 1e-6

RAW = 2
RING = 6
FFN_SLOTS = GROUPS * 6
WIN_TILES = 14
N_FF1 = 0
N_WIN = N_FF1 + FFN_SLOTS
N_WO = N_WIN + WIN_TILES
N_FF2 = N_WO + KC
N_PLE = N_FF2 + FFN_SLOTS
PLE_ORDER = ["pp0", "g0", "g1", "g2", "p0", "p1", "p2", "g3", "pp1", "g4", "g5", "g6", "g7"]
PLE_RING = {"pp0": 4, "g0": 5, "g1": 0, "g2": 1, "g3": 2, "pp1": 3, "g4": 5, "g5": 0, "g6": 1, "g7": 2}
N_ALL = N_PLE + len(PLE_ORDER)
FF2_RING = N_FF2 % RING

G_FF1, G_MIX, G_FF2, G_PLE, G_FIN = (KC * i for i in range(5))
G_Q = 5 * KC
G_KV = G_Q + QC
G_CN = G_KV + VC
B_CN = G_CN + CC
B_CONV = B_CN + CC
B_PG = B_CONV + CC
W_CONV = B_PG + KC
N_GAINS = W_CONV + CC * TAPS

PW_PE = 0
PW_NOPE = PW_PE + QC * 2 * ROPE
PW_UK = PW_NOPE + QC * P
PW_UV = PW_UK + VC * P
PW_UKT = PW_UV + VC * P
PW = PW_UKT + 2 * KV_RANK

DOWN = NRB * KC
T_FF1 = 0
T_WIN = T_FF1 + 6 * GROUPS
T_FF2 = T_WIN + CC * NRB
T_PLE = T_FF2 + 6 * GROUPS
Y_NORM1 = 0
Y_FF1 = Y_NORM1 + NRB
Y_WIN = Y_FF1 + DOWN * GROUPS + 2
WIN_SINGLES = ([(0, 0), (1, 0), (2, 0), (3, 0), "sum"] + [(j, r) for r in (1, 2) for j in range(4)]
               + [(j, r) for j in (4, 5) for r in range(NRB)])
Y_LAT = Y_WIN + len(WIN_SINGLES)
Y_WO = Y_LAT + 2 * NRB
WO_ORDER = ([(o, r) for r in range(NRB) for o in (0, 1)] + [(o, 0) for o in range(2, 8)]
            + [(2, 1), (3, 1), (4, 1), "sum0", (5, 1), (6, 1), (7, 1), (2, 2), (3, 2), (4, 2), "sum1",
               (5, 2), (6, 2), (7, 2)])
Y_FF2 = Y_WO + len(WO_ORDER) + 1
Y_PLE = Y_FF2 + DOWN * GROUPS + NRB
PLE_TILES = [(4 * half + i, r) for half in range(2) for r in range(NRB) for i in range(4)]
C96 = 3
K96 = (KV_RANK + ROPE) // C96
TOK = 256
TILES = PAST // TOK
LAST = 2 * TILES - 1
PPT = TOK // PAGE
LAT = KV_RANK + ROPE
BUFS = 4
PAIR_TAPS = 3
POOL_FIRST = 27
Z_PROJ = 12


class Tally:

    def __init__(self, eng, sem):
        self.eng, self.sem, self.n, self.off = eng, sem, 0, 0

    def hit(self, ins):
        ins.then_inc(self.sem, 1)
        self.n += 1

    def sync(self):
        self.eng.wait_ge(self.sem, self.off + self.n)


def program(nc, wstream, pairw, xT, hist, gains, trig, ident_d, tri_d, smask_d, cache,
            wuv_d, ptab_d, yT, ckvT, kpeT, convp, convs):
    f32, f32r, i32 = mybir.dt.float32, mybir.dt.float32r, mybir.dt.int32
    ALU, ACT, AX = mybir.AluOpType, mybir.ActivationFunctionType, mybir.AxisListType
    ctx = ExitStack()

    def scope():
        return ExitStack()

    def sb(st, name, shape, dt=f32):
        return st.enter_context(nc.sbuf_tensor(name, shape, dt))

    ident = sb(ctx, "ident", [P, P])
    ones = sb(ctx, "ones", [P, P])
    gain = sb(ctx, "gain", [P, N_GAINS])
    tri = sb(ctx, "tri", [P, P])
    smask = sb(ctx, "smask", [P, 2, NEW])
    stat = sb(ctx, "stat", [P, 24])
    ptab = sb(ctx, "ptab", [1, DEC_B * N_PAGES], i32)
    h = sb(ctx, "h", [P, KC, ROWS])

    zone_bytes = 50816
    za = scope()
    hid_hi = sb(za, "hid_hi", [P, 2, ROWS], f32r)
    hid_lo = sb(za, "hid_lo", [P, 2, ROWS], f32r)
    sq = sb(za, "sq", [P, KC, RB])
    n32 = sb(za, "n32", [P, KC, RB])
    gact = sb(za, "gact", [P, 2, RB])
    prod = sb(za, "prod", [P, 2, RB])
    red = sb(za, "red", [P, RB])
    rstd = sb(za, "rstd", [P, RB])
    za.close()
    zs = scope()
    ctile = [sb(zs, "ctile0", [P, 4, PPT, LAT])]
    SS = sb(zs, "SS", [P, 2, TOK + NEW])
    zs.close()
    zl = scope()
    lnsq = sb(zl, "lnsq", [P, NRB, CC, RB])
    zl.close()
    zb = scope()
    cq = sb(zb, "cq", [P, QC, ROWS])
    ckv = sb(zb, "ckv", [P, VC, ROWS])
    kpe = sb(zb, "kpe", [ROPE, ROWS])
    sqs = sb(zb, "sqs", [P, QC, RB])
    vext = sb(zb, "vext", [P, CC, HIST + SEQ])
    vs = sb(zb, "vs", [P, CC, DEC_B, HIST + DEC_T])
    used = 4 * (CC * (HIST + SEQ) + CC * DEC_B * (HIST + DEC_T) + (QC + VC + 1) * ROWS + QC * RB)
    sb(zb, "pad_b", [P, (zone_bytes - used) // 4])

    zn = scope()
    n_hi = sb(zn, "n_hi", [P, KC, ROWS], f32r)
    n_lo = sb(zn, "n_lo", [P, KC, ROWS], f32r)
    zr = scope()
    raw = [sb(zr, f"raw{i}", [P, 1024]) for i in range(RAW)]
    whi = [sb(zr, f"whi{i}", [P, 1024], f32r) for i in range(RING)]
    wlo = [sb(zr, f"wlo{i}", [P, 1024], f32r) for i in range(RING)]
    zr.close()
    zc = scope()
    qabs = sb(zc, "qabs", [K96, C96, DEC_B, TH])
    newT = sb(zc, "newT", [K96, C96, NEW])
    z1 = scope()
    ctile.append(sb(z1, "ctile1", [P, 4, PPT, LAT]))
    wuv = sb(z1, "wuv", [P, VC, HEADS * VH])
    z1.close()
    cs = sb(zc, "cs", [2 * ROPE, 2, ROWS])
    pw = sb(zc, "pw", [P, PW])
    z1 = scope()
    ttile = [sb(z1, f"ttile{i}", [K96, 4, C96, TOK]) for i in range(2)]
    ctile.append(sb(z1, "ctile2", [P, 4, PPT, LAT]))
    z1.close()
    q = sb(zc, "q", [NOPE + ROPE, 2, ROWS])
    k = sb(zc, "k", [NOPE + ROPE, 2, SEQ])
    V = sb(zc, "V", [P, QB, P])
    z2 = scope()
    qraw = sb(z2, "qraw", [2 * ROPE, ROWS])
    qsw = sb(z2, "qsw", [2 * ROPE, ROWS])
    z2.close()
    pr = sb(zc, "pr", [P, 2, 2, SEQ])
    zc.close()
    zn.close()
    zo = scope()
    sb(zo, "pad_o1", [P, CC * ROWS])
    z3 = scope()
    PT2 = sb(z3, "PT2", [P, 2, PPT + 1, P])
    ctile.append(sb(z3, "ctile3", [P, 4, PPT, LAT]))
    olat = sb(z3, "olat", [P, KV_RANK])
    ckvnew = sb(z3, "ckvnew", [NEW, KV_RANK])
    olatT = sb(z3, "olatT", [P, VC, 2, P])
    z3.close()
    PT = sb(zo, "PT", [P, 2, 2, SEQ])
    sb(zo, "pad_o2", [P, CC * ROWS - 4 * SEQ + CC * ROWS])
    cacc = sb(zo, "cacc", [P, CC, ROWS])
    zo.close()
    zb.close()

    ps = ctx.enter_context(nc.psum_tensor("ps", [P, 8, 512], f32))
    psf = ps[:, :, :].rearrange("p b n -> p (b n)")

    def sem(name):
        return ctx.enter_context(nc.semaphore(name))

    x_in = [sem(f"x_in{r}") for r in range(NRB)]
    const_in = sem("const_in")
    hist_in = sem("hist_in")
    raw_in = [sem(f"raw_in{i}") for i in range(RAW)]
    ready0 = sem("ready0")
    w_hi = sem("w_hi")
    w_split = sem("w_split")
    pair_ready, pair_free = sem("pair_ready"), sem("pair_free")
    one_ready, one_free = sem("one_ready"), sem("one_free")
    act_gate = sem("act_gate")
    hid_high, hid_ready = sem("hid_high"), sem("hid_ready")
    sq_ready, sq_summed = sem("sq_ready"), sem("sq_summed")
    root = sem("root")
    n32_ready, n_high, n_ready = sem("n32_ready"), sem("n_high"), sem("n_ready")
    ple_added = sem("ple_added")
    y_out = sem("y_out")
    lat_sq, lat_red, lat_root, lat_norm = sem("lat_sq"), sem("lat_red"), sem("lat_root"), sem("lat_norm")
    trig_in, pw_in = sem("trig_in"), sem("pw_in")
    kpe_ready = sem("kpe_ready")
    proj_ready, proj_free = sem("proj_ready"), sem("proj_free")
    rope_done = sem("rope_done")
    s_ready, s_max, s_free = sem("s_ready"), sem("s_max"), sem("s_free")
    p_norm = sem("p_norm")
    t4_ready, t4_done, t5_ready, t5_done = sem("t4_ready"), sem("t4_done"), sem("t5_ready"), sem("t5_done")
    av_ready, av_hi, av_lo = sem("av_ready"), sem("av_hi"), sem("av_lo")
    conv_done = sem("conv_done")
    ln_sum, ln_cent, ln_sq, ln_root, ln_recip, ln_scaled, ln_act, ln_hi, ln_lo = (
        sem(n) for n in ("ln_sum", "ln_cent", "ln_sq", "ln_root", "ln_recip", "ln_scaled", "ln_act", "ln_hi", "ln_lo"))
    c_in = [sem(f"c_in{i}") for i in range(BUFS)]
    c_used = sem("c_used")
    wuv_in = sem("wuv_in")
    lt_ready = sem("lt_ready")
    lt_done = [sem("lt_done0"), sem("lt_done1")]
    ss_ready, ss_max, ss_exp = sem("ss_ready"), sem("ss_max"), sem("ss_exp")
    pt_ready, pt_done = sem("pt_ready"), sem("pt_done")
    acc_done, olat_ready = sem("acc_done"), sem("olat_ready")
    ot_ready, ot_done = sem("ot_ready"), sem("ot_done")
    out_state = sem("out_state")
    dve_step = sem("dve_step")
    pool_tap = sem("pool_tap")

    def rows(r):
        return slice(r * RB, (r + 1) * RB)

    def kap(i):
        return i if i < 4 else 4 + 2 * (i - 4)

    def tap_operands(c, x):
        def by_seq(a):
            return a.rearrange("p (b t) -> p b t", b=DEC_B)

        flat = sqs[:, :, :].rearrange("p c n -> p (c n)")
        return (((cacc[:, c, 0:SEQ], vext[:, c, x:x + SEQ], flat[:, 0:SEQ]),
                 (by_seq(cacc[:, c, SEQ:ROWS]), vs[:, c, :, x:x + DEC_T], by_seq(flat[:, SEQ:ROWS]))),
                gain[:, W_CONV + c * TAPS + x:W_CONV + c * TAPS + x + 1], gain[:, B_CONV + c:B_CONV + c + 1])

    def load_tile(eng, n, seqs):
        if n >= BUFS:
            eng.wait_ge(c_used, n - BUFS + 1)
        grp, c = divmod(n, TILES)
        for j in seqs:
            for pg in range(PPT):
                at = (4 * grp + j) * N_PAGES + PPT * c + pg
                page = eng.value_load(ptab[0:1, at:at + 1], min_val=0, max_val=cache.shape[0] - 1)
                eng.dma_start(ctile[n % BUFS][:, j, pg, :], cache[page]).then_inc(c_in[n % BUFS], 16)

    def latents_out(eng, copy, n, j):
        if n >= 2:
            eng.wait_ge(ss_ready, n - 1)
        x = 4 * n + j
        eng.wait_ge(lt_ready, x + 1)
        b = 2 * (x % 2)
        copy(ttile[n % 2][:, j, :, :].rearrange("p c (g t) -> p g c t", g=PPT),
             ps[0:K96, b:b + 2, 0:C96 * P].rearrange("p g (c t) -> p g c t", c=C96)).then_inc(lt_done[x % 2], 1)

    block = ctx.enter_context(nc.Block())

    @block.sync
    def _(sp):
        for r in range(NRB):
            sp.dma_start(h[:, :, rows(r)], xT[:, :, rows(r)]).then_inc(x_in[r], 16)
            if r == 0:
                for s in range(RAW):
                    sp.dma_start(raw[s][:, :], wstream[s]).then_inc(raw_in[s], 16)
                sp.dma_start(gain[:, :], gains).then_inc(const_in, 16)
        sp.dma_start(ident[:, :], ident_d).then_inc(const_in, 16)
        sp.dma_start(tri[:, :], tri_d).then_inc(const_in, 16)
        sp.dma_start(smask[:, :, :], smask_d).then_inc(const_in, 16)
        sp.dma_start(ptab[:, :], ptab_d).then_inc(const_in, 16)
        with sp.Fori(0, (N_WO - RAW) // RAW) as g:
            for s in range(RAW):
                sp.wait_ge(w_split, RAW * g + s + 1)
                sp.dma_start(raw[s][:, :], wstream[RAW * g + s + RAW]).then_inc(raw_in[s], 16)
        sp.wait_ge(pair_ready, T_FF2)
        sp.dma_start(cs[:, :, :], trig).then_inc(trig_in, 16)
        sp.dma_start(pw[:, :], pairw[0]).then_inc(pw_in, 16)
        sp.wait_ge(lat_norm, 2 * NRB)
        sp.dma_start(ckvT, ckv[:, :, :]).then_inc(out_state, 16)
        sp.wait_ge(hist_in, 16 * CC)
        sp.wait_ge(pair_free, 2 + T_FF2)
        sp.dma_start(convp, vext[:, :, SEQ:SEQ + HIST]).then_inc(out_state, 16)
        for c in range(CC):
            sp.dma_start(convs[:, c], vs[:, c, :, DEC_T:DEC_T + HIST]).then_inc(out_state, 16)
        sp.wait_ge(kpe_ready, 1)
        sp.dma_start(kpeT, kpe[:, :]).then_inc(out_state, 16)
        with sp.Fori(1, PAIRS) as p:
            sp.wait_ge(proj_ready, Z_PROJ * p)
            sp.dma_start(pw[:, :], pairw[p]).then_inc(pw_in, 16)
        sp.wait_ge(const_in, 5 * 16)
        sp.wait_ge(proj_ready, Z_PROJ * PAIRS)
        load_tile(sp, 0, (0, 1, 2, 3))
        sp.wait_ge(rope_done, PAIRS)
        load_tile(sp, 1, (0, 1, 2, 3))
        sp.dma_start(wuv[:, :, :], wuv_d).then_inc(wuv_in, 16)
        sp.wait_ge(av_ready, PAIRS * QB)
        for n in range(2, LAST + 1):
            load_tile(sp, n, (0, 1, 2))
        sp.wait_ge(c_used, LAST + 1)
        for s in range(RAW):
            sp.dma_start(raw[(N_WO + s) % RAW][:, :], wstream[N_WO + s]).then_inc(raw_in[(N_WO + s) % RAW], 16)
        left = N_ALL - N_WO - RAW
        with sp.Fori(0, left // RAW) as g:
            for s in range(RAW):
                sp.wait_ge(w_split, RAW * g + (N_WO + s + 1))
                sp.dma_start(raw[s][:, :], wstream[RAW * g + (N_WO + s + RAW)]).then_inc(raw_in[s], 16)
        for n in range(N_WO + RAW + left // RAW * RAW, N_ALL):
            sp.wait_ge(w_split, n - RAW + 1)
            sp.dma_start(raw[n % RAW][:, :], wstream[n]).then_inc(raw_in[n % RAW], 16)

    @block.gpsimd
    def _(pool):
        nc.gpsimd.memset(ones[:, :], 1.0).then_inc(ready0, 1)
        nc.gpsimd.memset(stat[:, 23:24], EPS).then_inc(ready0, 1)
        nc.gpsimd.memset(stat[:, 16:17], 0.0).then_inc(pair_free, 2)
        nc.gpsimd.memset(stat[:, 17:18], 0.0).then_inc(one_free, 4)
        nc.gpsimd.memset(stat[:, 18:19], 0.0).then_inc(proj_free, 4)
        nc.gpsimd.memset(stat[:, 19:20], 0.0).then_inc(s_free, 2)
        nc.gpsimd.memset(stat[:, 20:21], 0.0).then_inc(t4_done, 1)
        nc.gpsimd.memset(stat[:, 21:22], 0.0).then_inc(t5_done, 1)
        nc.gpsimd.memset(stat[:, 22:23], 0.0).then_inc(av_lo, 2)
        pool.wait_ge(n_ready, 2 * NRB)
        nc.gpsimd.memset(vext[:, :, 0:HIST], 0.0).then_inc(ready0, 1)
        for c in range(CC):
            pool.dma_start(vs[:, c, :, 0:HIST], hist[:, c]).then_inc(hist_in, 16)
        pool.wait_ge(hist_in, 16 * CC)
        pool.wait_ge(pair_free, 2 + T_FF2)
        pool.wait_ge(kpe_ready, 1)
        pool.wait_ge(ready0, 3)
        pool.wait_ge(const_in, 5 * 16)
        done = 0
        for c, x in [(2, x) for x in range(POOL_FIRST)] + [(3, x) for x in range(TAPS)]:
            both, w, b = tap_operands(c, x)
            if x == 0:
                for acc, src, _ in both:
                    last = nc.gpsimd.tensor_scalar(acc, src, w, b, ALU.mult, ALU.add)
                last.then_inc(pool_tap, 1)
                done += 1
                continue
            pool.wait_ge(pool_tap, done)
            for _, src, product in both:
                last = nc.gpsimd.tensor_scalar(product, src, w, None, ALU.mult)
            last.then_inc(pool_tap, 1)
            pool.wait_ge(pool_tap, done + 1)
            for acc, _, product in both:
                last = nc.gpsimd.tensor_tensor(acc, acc, product, ALU.add)
            last.then_inc(pool_tap, 1)
            done += 2
        for r in range(NRB):
            pool.wait_ge(n32_ready, 4 * NRB + r + 1)
            pool.dma_start(yT[:, :, rows(r)], n32[:, :, :]).then_inc(y_out, 16)
        pool.wait_ge(y_out, 16 * NRB)
        pool.wait_ge(out_state, 16 * (3 + CC))

    @block.tensor
    def _(pe):
        def split_product(out, w_h, w_l, x_h, x_l, first, last):
            nc.tensor.matmul(out, w_l, x_h, start=first, stop=False)
            nc.tensor.matmul(out, w_h, x_l, start=False, stop=False)
            return nc.tensor.matmul(out, w_h, x_h, start=False, stop=last)

        def contract(out, ring, r, chunks=KC, src=(n_hi, n_lo), cols=0, part=None):
            for c in part or range(chunks):
                w = slice(cols + c * P, cols + (c + 1) * P)
                last = split_product(out, whi[ring][:, w], wlo[ring][:, w], src[0][:, c, rows(r)],
                                     src[1][:, c, rows(r)], c == 0, c == chunks - 1)
            return last

        def row_sum(y, wait_sem, wait_val, src):
            pe.wait_ge(wait_sem, wait_val)
            pe.wait_ge(one_free, y + 1)
            nc.tensor.matmul(ps[:, 4 + y % 4, 0:RB], ones[:, :], src, start=True, stop=True).then_inc(one_ready, 1)

        def norm_sum(norm, r, y):
            row_sum(y, sq_summed, NRB * norm + r + 1, red[:, :])

        def ffn(n0, t0, y0, norm, ring0):
            t0h = t0 - (CC * NRB if t0 else 0)

            def body(g, first, last):
                def hidden(t, between=None):
                    r, f = divmod(t, 2)
                    pe.wait_ge(w_split, 6 * g + (n0 + 2 * f + 1))
                    pe.wait_ge(n_ready, NRB * norm + r + 1)
                    pe.wait_ge(pair_free, 6 * g + (t0 + t + 1))
                    b = 2 * ((t0 + t) % 2)
                    contract(ps[:, b, 0:RB], (ring0 + 2 * f) % RING, r)
                    if between:
                        between()
                    pe.wait_ge(w_split, 6 * g + (n0 + 2 * f + 2))
                    contract(ps[:, b + 1, 0:RB], (ring0 + 2 * f + 1) % RING, r).then_inc(pair_ready, 1)

                def down_part(o, r, f, y):
                    s = (ring0 + 4 + f) % RING
                    w = slice(o * P, (o + 1) * P)
                    return split_product(ps[:, 4 + y % 4, 0:RB], whi[s][:, w], wlo[s][:, w],
                                         hid_hi[:, f, rows(r)], hid_lo[:, f, rows(r)], f == 0, f == 1)

                def down(r):
                    y = y0 + KC * r + (last and r > 0)
                    pe.wait_ge(w_split, 6 * g + (n0 + 6))
                    o0 = 0
                    if r == NRB - 1:
                        pe.wait_ge(hid_ready, 6 * g + (t0h + 2 * r + 1))
                        for o in range(4):
                            pe.wait_ge(one_free, DOWN * g + (y + o + 1))
                            down_part(o, r, 0, y + o)
                        pe.wait_ge(hid_ready, 6 * g + (t0h + 2 * r + 2))
                        for o in range(4):
                            down_part(o, r, 1, y + o).then_inc(one_ready, 1)
                        o0 = 4
                        if last:
                            norm_sum(norm + 1, 1, yl + 2 * KC + 5)
                            y += 1
                    pe.wait_ge(hid_ready, 6 * g + (t0h + 2 * r + 2))
                    for o in range(o0, KC):
                        pe.wait_ge(one_free, DOWN * g + (y + o + 1))
                        down_part(o, r, 0, y + o)
                        down_part(o, r, 1, y + o).then_inc(one_ready, 1)

                yl = y0 + DOWN * g
                hidden(0)
                hidden(1, (lambda: norm_sum(norm, 2, y0 - 1)) if first else None)
                hidden(2)
                down(0)
                hidden(3)
                if last:
                    norm_sum(norm + 1, 0, yl + KC)
                hidden(4)
                down(1)
                hidden(5)
                down(2)

            body(0, True, False)
            with pe.Fori(1, GROUPS - 1) as g:
                body(g, False, False)
            body(GROUPS - 1, False, True)

        pe.wait_ge(ready0, 2)
        norm_sum(0, 0, Y_NORM1)
        norm_sum(0, 1, Y_NORM1 + 1)
        ffn(N_FF1, T_FF1, Y_FF1, 0, 0)

        for i, tile in enumerate(WIN_SINGLES):
            y = Y_WIN + i
            if tile == "sum":
                norm_sum(1, 2, y)
                continue
            j, r = tile
            pe.wait_ge(w_split, N_WIN + j + 1)
            pe.wait_ge(n_ready, NRB + r + 1)
            pe.wait_ge(one_free, y + 1)
            contract(ps[:, 4 + y % 4, 0:RB], j % RING, r).then_inc(one_ready, 1)
        y = Y_LAT
        for c in range(CC):
            for r in range(NRB):
                t = T_WIN + c * NRB + r
                pe.wait_ge(w_split, N_WIN + 6 + 2 * c + 2)
                pe.wait_ge(pair_free, t + 1)
                b = 2 * (t % 2)
                contract(ps[:, b, 0:RB], (2 * c) % RING, r)
                contract(ps[:, b + 1, 0:RB], (2 * c + 1) % RING, r).then_inc(pair_ready, 1)
                x = c * NRB + r - 2
                if 0 <= x < 2 * NRB:
                    row_sum(y, lat_red, x + 1, sqs[:, 0, :])
                    y += 1

        pe.wait_ge(const_in, 5 * 16)
        with pe.Fori(0, PAIRS) as p:
            pe.wait_ge(pw_in, 16 * p + 16)

            def proj(z, m, n, kc, col, width, rhs, col0=0):
                out = ps[0:m, 4 + z % 4, col0:col0 + n]
                for c in range(kc):
                    last = nc.tensor.matmul(out, pw[:, col + c * width:col + (c + 1) * width], rhs(c),
                                            start=(c == 0), stop=(c == kc - 1))
                return last

            for z in range(3):
                if z == 2:
                    pe.wait_ge(av_lo, QB * p + 2)
                pe.wait_ge(proj_free, Z_PROJ * p + (z + 1))
                proj(z, 2 * ROPE, RB, QC, PW_PE, 2 * ROPE, lambda c: cq[:, c, rows(z)]).then_inc(proj_ready, 1)
            for z in range(3, 6):
                pe.wait_ge(proj_free, Z_PROJ * p + (z + 1))
                proj(z, P, RB, QC, PW_NOPE, P, lambda c: cq[:, c, rows(z - 3)]).then_inc(proj_ready, 1)
            for z in range(6, 8):
                pe.wait_ge(proj_free, Z_PROJ * p + (z + 1))
                s0 = (z - 6) * 512
                proj(z, P, 512, VC, PW_UK, P, lambda c: ckv[:, c, s0:s0 + 512]).then_inc(proj_ready, 1)
            for z in range(8, 10):
                pe.wait_ge(proj_free, Z_PROJ * p + (z + 1))
                for i in range(4):
                    s0 = ((z - 8) * 4 + i) * P
                    for c in range(VC):
                        last = nc.tensor.matmul(ps[:, 4 + z % 4, i * P:(i + 1) * P], ckv[:, c, s0:s0 + P],
                                                pw[:, PW_UV + c * P:PW_UV + (c + 1) * P],
                                                start=(c == 0), stop=(c == VC - 1))
                last.then_inc(proj_ready, 1)
            pe.wait_ge(proj_free, Z_PROJ * p + (4 + 6))
            for z in range(10, 12):
                pe.wait_ge(proj_free, Z_PROJ * p + (z + 1))
                for c in range(C96):
                    m = min(K96, KV_RANK - c * K96)
                    w0 = PW_UKT + (z - 10) * KV_RANK + c * K96
                    last = nc.tensor.matmul(ps[0:m, 4 + z % 4, c * NEW:(c + 1) * NEW], pw[0:NOPE, w0:w0 + m],
                                            q[0:NOPE, z - 10, SEQ:ROWS], start=True, stop=True)
                last.then_inc(proj_ready, 1)
            pe.wait_ge(rope_done, p + 1)
            pe.wait_ge(kpe_ready, 1)

            def scores(i):
                for hh in range(2):
                    pe.wait_ge(s_free, 2 * QB * p + (2 * i + hh + 1))
                    w = (i + 1) * P
                    for c in range(0, w, 512):
                        e = min(w, c + 512)
                        last = nc.tensor.matmul(psf[:, hh * 1024 + c:hh * 1024 + e], q[:, hh, i * P:(i + 1) * P],
                                                k[:, hh, c:e], start=True, stop=True)
                    last.then_inc(s_ready, 1)

            def transposes(i):
                for hh in range(2):
                    pe.wait_ge(p_norm, 2 * QB * p + (2 * i + hh + 1))
                    for c in range(0, i + 1, 4):
                        if i < 4:
                            bank, idx = 4 + hh, kap(i)
                        else:
                            bank, idx = 4 + c // 4, kap(i) + hh
                        ready, done = ((t4_ready, t4_done), (t5_ready, t5_done))[bank - 4]
                        pe.wait_ge(done, 12 * p + (idx + 1))
                        for j in range(c, min(i + 1, c + 4)):
                            last = nc.tensor.transpose(ps[:, bank, (j - c) * P:(j - c + 1) * P],
                                                       pr[:, i % 2, hh, j * P:(j + 1) * P], ident[:, :])
                        last.then_inc(ready, 1)

            def values(i):
                pe.wait_ge(t4_done, 12 * p + (1 + kap(i + 1)))
                pe.wait_ge(t5_done, 12 * p + (1 + kap(i + 1)))
                pe.wait_ge(av_lo, QB * p + (i + 1))
                for j in range(i + 1):
                    for hh in range(2):
                        last = nc.tensor.matmul(ps[VH * hh:VH * (hh + 1), 6 + i % 2, 0:P],
                                                V[:, j, VH * hh:VH * (hh + 1)], PT[:, i % 2, hh, j * P:(j + 1) * P],
                                                start=(j == 0), stop=(j == i))
                last.then_inc(av_ready, 1)

            scores(0)
            pe.wait_ge(proj_free, Z_PROJ * p + (4 + Z_PROJ))
            for i in range(QB):
                if i + 1 < QB:
                    scores(i + 1)
                if i:
                    values(i - 1)
                transposes(i)
            values(QB - 1)

        pe.wait_ge(s_free, 2 * QB * PAIRS + 2)

        def latents_T(n, j):
            x = 4 * n + j
            if x >= 2:
                pe.wait_ge(lt_done[x % 2], x // 2)
            for pg in range(PPT):
                for c in range(C96):
                    last = nc.tensor.transpose(ps[0:K96, 2 * (x % 2) + pg, c * P:(c + 1) * P],
                                               ctile[n % BUFS][:, j, pg, c * K96:(c + 1) * K96], ident[:, :])
            last.then_inc(lt_ready, 1)

        def sample_scores(n, c):
            if c == 0:
                for parity in range(2):
                    pe.wait_ge(lt_done[parity], 2 * (n + 1))
                if n >= 2:
                    pe.wait_ge(ss_exp, n - 1)
            wide = n % TILES == TILES - 1
            for j in range(4):
                w = qabs[:, c, 4 * (n // TILES) + j, :]
                o = slice(TH * j, TH * (j + 1))
                last = nc.tensor.matmul(ps[o, 4 + n % 2, 0:TOK], w, ttile[n % 2][:, j, c, :],
                                        start=(c == 0), stop=(c == C96 - 1))
            if c == C96 - 1 and wide:
                for cc in range(C96):
                    for j in range(4):
                        last = nc.tensor.matmul(ps[TH * j:TH * (j + 1), 4 + n % 2, TOK:TOK + NEW],
                                                qabs[:, cc, 4 * (n // TILES) + j, :], newT[:, cc, :],
                                                start=(cc == 0), stop=(cc == C96 - 1))
            if c == C96 - 1:
                last.then_inc(ss_ready, 1)

        def sample_probs_T(n):
            pe.wait_ge(ss_exp, n + 1)
            if n:
                pe.wait_ge(pt_done, n)
            for pg in range(PPT):
                last = nc.tensor.transpose(ps[:, 6, pg * P:(pg + 1) * P], SS[:, n % 2, pg * P:(pg + 1) * P],
                                           ident[:, :])
            if n % TILES == TILES - 1:
                last = nc.tensor.transpose(ps[0:NEW, 6, TOK:TOK + P], SS[:, n % 2, TOK:TOK + NEW], ident[:, :])
            last.then_inc(pt_ready, 1)

        def sample_values(n):
            pe.wait_ge(pt_done, n + 1)
            if n:
                pe.wait_ge(acc_done, n)
            if n % TILES == 0:
                pe.wait_ge(ot_done, n // TILES + 1)
            wide = n % TILES == TILES - 1
            for pg in range(PPT):
                for j in range(4):
                    last = nc.tensor.matmul(ps[TH * j:TH * (j + 1), 7, 0:KV_RANK], PT2[:, n % 2, pg, TH * j:TH * (j + 1)],
                                            ctile[n % BUFS][:, j, pg, 0:KV_RANK], start=(pg == 0),
                                            stop=(pg == PPT - 1 and not wide))
            if wide:
                for j in range(4):
                    last = nc.tensor.matmul(ps[TH * j:TH * (j + 1), 7, 0:KV_RANK],
                                            PT2[0:NEW, n % 2, PPT, TH * j:TH * (j + 1)], ckvnew[:, :],
                                            start=False, stop=True)
            last.then_inc(c_used, 1)

        def outputs_T(grp):
            pe.wait_ge(olat_ready, grp + 1)
            pe.wait_ge(ot_done, grp + 1)
            for c in range(VC):
                last = nc.tensor.transpose(ps[:, 7, KV_RANK + c * P:KV_RANK + (c + 1) * P], olat[:, c * P:(c + 1) * P],
                                           ident[:, :])
            last.then_inc(ot_ready, 1)

        for n in range(LAST + 3):
            if n <= LAST:
                pe.wait_ge(c_in[n % BUFS], 16 * 4 * PPT * (n // BUFS + 1))
                latents_T(n, 0)
                latents_T(n, 1)
            if n == 0:
                pe.wait_ge(av_lo, PAIRS * QB + 2)
                for c in range(VC):
                    last = nc.tensor.transpose(ps[0:NEW, 7, KV_RANK + c * P:KV_RANK + (c + 1) * P],
                                               ckv[:, c, SEQ:ROWS], ident[:, :])
                last.then_inc(ot_ready, 1)
            for c in range(C96):
                if 1 <= n <= LAST + 1:
                    sample_scores(n - 1, c)
                if c == 0 and n >= 2:
                    sample_probs_T(n - 2)
                if n <= LAST and c < 2:
                    latents_T(n, 2 + c)
                if c == 0 and n == TILES + 2:
                    outputs_T(0)
                if c == 0 and n >= 2:
                    sample_values(n - 2)
        outputs_T(1)
        pe.wait_ge(ot_done, 3)
        pe.wait_ge(wuv_in, 16)
        for hd in range(HEADS):
            o = VH * (hd % 2)
            for c in range(VC):
                last = nc.tensor.matmul(
                    ps[o:o + VH, 6, (hd // 2) * NEW:(hd // 2 + 1) * NEW], wuv[:, c, hd * VH:(hd + 1) * VH],
                    olatT[:, c].rearrange("p g (j h t) -> p (g j) h t", j=4, h=HEADS)[:, :, hd, :],
                    start=(c == 0), stop=(c == VC - 1))
        last.then_inc(av_ready, 1)

        pe.wait_ge(av_lo, 2 + PAIRS * QB + 1)
        def ln_sums(m):
            for r in range(NRB):
                if m:
                    pe.wait_ge(ln_sq, r + 1)
                for c in range(CC):
                    last = nc.tensor.matmul(ps[:, (NRB * m + r) % 4, 0:RB], ones[:, :],
                                            lnsq[:, r, c, :] if m else cacc[:, c, rows(r)],
                                            start=(c == 0), stop=(c == CC - 1))
                last.then_inc(ln_sum, 1)

        def wo_tile(i, part):
            (o, r), y = WO_ORDER[i], Y_WO + i
            if part != "attention":
                pe.wait_ge(ln_lo, r + 1)
            pe.wait_ge(w_split, N_WO + o + 1)
            pe.wait_ge(one_free, y + 1)
            last = contract(ps[:, 4 + y % 4, 0:RB], (N_WO + o) % RING, r,
                            part={"attention": range(0, CC), "convolution": range(CC, KC), "all": None}[part])
            if part != "attention":
                last.then_inc(one_ready, 1)

        pe.wait_ge(conv_done, 1)
        ln_sums(0)
        wo_tile(0, "attention")
        wo_tile(1, "attention")
        ln_sums(1)
        wo_tile(2, "attention")
        wo_tile(3, "attention")

        for i, tile in enumerate(WO_ORDER):
            y = Y_WO + i
            if tile in ("sum0", "sum1"):
                norm_sum(2, int(tile[-1]), y)
                continue
            wo_tile(i, "convolution" if i < 4 else "all")

        ffn(N_FF2, T_FF2, Y_FF2, 2, FF2_RING)

        for i, (o, r) in enumerate(PLE_TILES):
            t = T_PLE + i
            pe.wait_ge(w_split, N_PLE + PLE_ORDER.index(f"g{o}") + 1)
            pe.wait_ge(pair_free, t + 1)
            pe.wait_ge(n_ready, NRB * 3 + r + 1)
            b = 2 * (t % 2)
            contract(ps[:, b, 0:RB], PLE_RING[f"g{o}"], r)
            pe.wait_ge(w_split, N_PLE + PLE_ORDER.index("p0") + r + 1)
            pe.wait_ge(w_split, N_PLE + PLE_ORDER.index(f"pp{o // 4}") + 1)
            contract(ps[:, b + 1, 0:RB], PLE_RING[f"pp{o // 4}"], r, VC, (hid_hi, hid_lo),
                     (o % 4) * VC * P).then_inc(pair_ready, 1)
            if i == 3:
                norm_sum(3, 2, Y_PLE - 1)
            if i in (17, 21):
                norm_sum(4, (i - 17) // 4, Y_PLE + (i - 17) // 4)
        norm_sum(4, 2, Y_PLE + 2)

    @block.scalar
    def _(act):
        def high(n, ring, add=0):
            act.wait_ge(raw_in[n % RAW], 16 * (n // RAW + 1) + 8 * add)
            nc.scalar.activation(whi[ring][:, :], raw[n % RAW][:, :], ACT.Copy).then_inc(w_hi, 1)

        def squares(norm, r, sem_, val):
            act.wait_ge(sem_, val)
            kk = NRB * norm + r
            if kk:
                act.wait_ge(sq_summed, kk)
            nc.scalar.activation(sq[:, :, :], h[:, :, rows(r)], ACT.Square).then_inc(sq_ready, 1)

        def norm_high(norm, r):
            act.wait_ge(n32_ready, NRB * norm + r + 1)
            nc.scalar.activation(n_hi[:, :, rows(r)], n32[:, :, :], ACT.Copy).then_inc(n_high, 1)

        def norm_root(norm, r, y, then_high=True):
            act.wait_ge(one_ready, y + 1)
            if norm == 4 and r:
                act.wait_ge(n32_ready, NRB * norm + r)
            nc.scalar.activation(rstd[:, :], ps[:, 4 + y % 4, 0:RB], ACT.Sqrt, scale=1.0 / D_MODEL,
                                 bias=stat[:, 23:24]).then_inc(root, 1)
            if norm < 4 and then_high:
                norm_high(norm, r)

        def ffn(n0, t0, y0, norm, ring0, nexts):
            def body(g, first, last):
                def hidden_high(t):
                    r, f = divmod(t, 2)
                    act.wait_ge(pair_free, 6 * g + (t0 + t + 3))
                    nc.scalar.activation(hid_hi[:, f, rows(r)], prod[:, t % 2, :], ACT.Copy).then_inc(hid_high, 1)

                def hidden(t):
                    act.wait_ge(pair_ready, 6 * g + (t0 + t + 1))
                    act.wait_ge(pair_free, 6 * g + (t0 + t + 1))
                    nc.scalar.activation(gact[:, t % 2, :], ps[:, 2 * ((t0 + t) % 2), 0:RB], ACT.Silu)\
                        .then_inc(act_gate, 1)
                    hidden_high(t)

                def next_high(i):
                    if not last:
                        high(n0 + 6 + i, (ring0 + i) % RING, add=6 * g)
                    elif i < len(nexts):
                        high(*nexts[i])

                yl = y0 + DOWN * g
                hidden(0)
                act.wait_ge(one_ready, DOWN * g + (y0 - first))
                high(n0 + 4, (ring0 + 4) % RING, add=6 * g)
                if first:
                    high(n0 + 5, (ring0 + 5) % RING)
                    norm_root(norm, 2, y0 - 1, then_high=False)
                hidden(1)
                if first:
                    norm_high(norm, 2)
                else:
                    high(n0 + 5, (ring0 + 5) % RING, add=6 * g)
                hidden(2)
                if last:
                    squares(norm + 1, 0, one_free, 4 + yl + KC)
                hidden(3)
                if last:
                    norm_root(norm + 1, 0, yl + KC, then_high=False)
                hidden(4)
                if last:
                    norm_high(norm + 1, 0)
                next_high(0)
                next_high(1)
                if last:
                    squares(norm + 1, 1, one_free, 4 + yl + 2 * KC + 1)
                hidden(5)
                if last:
                    norm_root(norm + 1, 1, yl + 2 * KC + 5, then_high=False)
                next_high(2)
                next_high(3)

            body(0, True, False)
            with act.Fori(1, GROUPS - 1) as g:
                body(g, False, False)
            body(GROUPS - 1, False, True)

        act.wait_ge(ready0, 2)
        squares(0, 0, x_in[0], 16)
        high(N_FF1, 0)
        high(N_FF1 + 1, 1)
        norm_root(0, 0, Y_NORM1, then_high=False)
        squares(0, 1, x_in[1], 16)
        norm_high(0, 0)
        high(N_FF1 + 2, 2)
        high(N_FF1 + 3, 3)
        norm_root(0, 1, Y_NORM1 + 1)
        squares(0, 2, x_in[2], 16)
        ffn(N_FF1, T_FF1, Y_FF1, 0, 0, [(N_WIN + j, j) for j in range(4)])

        squares(1, 2, one_free, 4 + Y_WIN)
        norm_high(1, 1)
        for j in (4, 5):
            high(N_WIN + j, j)

        def lat_squares(m, r):
            n_src, c = ((cq, QC), (ckv, VC))[m]
            act.wait_ge(one_free, 4 + Y_WIN + WIN_SINGLES.index((4, 2)) + 1)
            if NRB * m + r:
                act.wait_ge(lat_norm, NRB * m + r)
            nc.scalar.activation(sqs[:, 0:c, :], n_src[:, :, rows(r)], ACT.Square).then_inc(lat_sq, 1)

        def gate(c, r):
            t = T_WIN + c * NRB + r
            act.wait_ge(pair_ready, t + 1)
            b = 2 * (t % 2) + 1
            if r < NRB - 1:
                nc.scalar.activation(vext[:, c, HIST + r * RB:HIST + (r + 1) * RB], ps[:, b, 0:RB], ACT.Sigmoid)\
                    .then_inc(act_gate, 1)
            else:
                nc.scalar.activation(vext[:, c, HIST + r * RB:HIST + SEQ], ps[:, b, 0:SEQ - r * RB], ACT.Sigmoid)
                nc.scalar.activation(vs[:, c, :, HIST:HIST + DEC_T],
                                     ps[:, b, SEQ - r * RB:RB].rearrange("p (b t) -> p b t", b=DEC_B), ACT.Sigmoid)\
                    .then_inc(act_gate, 1)

        def lat_root_(x):
            m, r = divmod(x, NRB)
            y = Y_LAT + x
            act.wait_ge(one_ready, y + 1)
            nc.scalar.activation(sqs[:, 1, :], ps[:, 4 + y % 4, 0:RB], ACT.Sqrt, scale=1.0 / (P * (QC, VC)[m]),
                                 bias=stat[:, 23:24]).then_inc(lat_root, 1)

        norm_root(1, 2, Y_WIN + 4)
        for j in range(6, 12):
            act.wait_ge(one_ready, Y_WIN + WIN_SINGLES.index((j - 6, 2)) + 1)
            high(N_WIN + j, j % RING)
        lat_squares(0, 0)
        for x in range(CC * NRB):
            gate(*divmod(x, NRB))
            if x == 2:
                for j in (12, 13):
                    high(N_WIN + j, j % RING)
            if 0 <= x - 2 < 2 * NRB:
                lat_root_(x - 2)
                if x - 1 < 2 * NRB:
                    lat_squares(*divmod(x - 1, NRB))

        with act.Fori(0, PAIRS) as p:
            def evac(z, dsts):
                act.wait_ge(proj_ready, Z_PROJ * p + (z + 1))
                for d, s in dsts:
                    last = nc.scalar.activation(d, s, ACT.Copy, scale=SCALE if z < 6 else 1.0)
                last.then_inc(proj_free, 1)

            for z in range(3):
                evac(z, [(qraw[:, rows(z)], ps[0:2 * ROPE, 4 + z % 4, 0:RB])])
            for z in range(3, 6):
                evac(z, [(q[0:NOPE, hh, rows(z - 3)], ps[NOPE * hh:NOPE * (hh + 1), 4 + z % 4, 0:RB])
                         for hh in range(2)])
            for z in range(6, 8):
                s0 = (z - 6) * 512
                evac(z, [(k[0:NOPE, hh, s0:s0 + 512], ps[NOPE * hh:NOPE * (hh + 1), 4 + z % 4, :])
                         for hh in range(2)])
            for z in range(8, 10):
                evac(z, [(V[:, (z - 8) * 4:(z - 7) * 4, :], ps[:, 4 + z % 4, :].rearrange("p (s v) -> p s v", s=4))])
            for z in range(10, 12):
                evac(z, [(qabs[0:min(K96, KV_RANK - c * K96), c, :, bass.ds(8 * p + 4 * (z - 10), 4)],
                          ps[0:min(K96, KV_RANK - c * K96), 4 + z % 4, c * NEW:(c + 1) * NEW]
                          .rearrange("p (b t) -> p b t", b=DEC_B)) for c in range(C96)])

            def untile(i):
                for x in range(1 if i < 4 else 2):
                    act.wait_ge(t4_ready, 12 * p + (kap(i) + x + 1))
                    n = min(i + 1, 4) * P
                    nc.scalar.activation(PT[:, i % 2, x, 0:n], ps[:, 4, 0:n], ACT.Copy).then_inc(t4_done, 1)

            def high_av(i):
                act.wait_ge(av_ready, QB * p + (i + 1))
                nc.scalar.activation(n_hi[:, p, i * P:(i + 1) * P], ps[:, 6 + i % 2, 0:P], ACT.Copy).then_inc(av_hi, 1)

            for i in range(QB):
                if i:
                    untile(i - 1)
                for hh in range(2):
                    u = 2 * i + hh
                    act.wait_ge(s_max, 2 * QB * p + (u + 1))
                    w = (i + 1) * P
                    nc.scalar.activation(pr[:, i % 2, hh, 0:w], psf[:, 1024 * hh:1024 * hh + w], ACT.Exp,
                                         bias=stat[:, 4 + u % 4:5 + u % 4],
                                         accum_out=stat[:, 8 + u % 4:9 + u % 4]).then_inc(s_free, 1)
                if i >= 2:
                    high_av(i - 2)
            untile(QB - 1)
            high_av(QB - 2)
            high_av(QB - 1)

        act.wait_ge(const_in, 5 * 16)

        def probs_out(n):
            act.wait_ge(pt_ready, n + 1)
            if n >= 2:
                act.wait_ge(c_used, n - 1)
            if n % TILES == TILES - 1:
                nc.scalar.activation(PT2[0:NEW, n % 2, PPT, :], ps[0:NEW, 6, TOK:TOK + P], ACT.Copy)
            nc.scalar.activation(PT2[:, n % 2, 0:PPT, :], ps[:, 6, 0:TOK].rearrange("p (g t) -> p g t", g=PPT), ACT.Copy)\
                .then_inc(pt_done, 1)

        def sample_exp(n):
            act.wait_ge(ss_max, n + 1)
            if n >= 2:
                act.wait_ge(pt_ready, n - 1)
                act.wait_ge(acc_done, n - 1)
            m, e, neg = n % 2, (n - 1) % 2, stat[:, n % 2:1 + n % 2]
            if n % TILES:
                nc.scalar.activation(stat[:, 4 + m:5 + m], stat[:, e:e + 1], ACT.Exp, bias=neg, scale=-1.0)
            w = TOK + (NEW if n % TILES == TILES - 1 else 0)
            nc.scalar.activation(SS[:, m, 0:w], ps[:, 4 + m, 0:w], ACT.Exp, bias=neg,
                                 accum_out=stat[:, 6 + m:7 + m]).then_inc(ss_exp, 1)

        act.wait_ge(av_ready, PAIRS * QB)
        load_tile(act, 2, (3,))
        load_tile(act, 3, (3,))
        for n in range(LAST + 3):
            if n <= LAST:
                latents_out(act, nc.scalar.copy, n, 0)
            if n >= 2:
                probs_out(n - 2)
            if n <= LAST:
                latents_out(act, nc.scalar.copy, n, 2)
            if BUFS <= n + 2 <= LAST:
                load_tile(act, n + 2, (3,))
            if 1 <= n <= LAST + 1:
                sample_exp(n - 1)
        act.wait_ge(av_ready, PAIRS * QB + 1)
        nc.scalar.activation(n_hi[:, 0:PAIRS, SEQ:ROWS], ps[:, 6, 0:PAIRS * NEW].rearrange("p (a n) -> p a n", a=PAIRS),
                             ACT.Copy).then_inc(av_hi, 1)

        def wo_high(o):
            high(N_WO + o, (N_WO + o) % RING)

        wo_high(0)
        wo_high(1)
        act.wait_ge(out_state, 16 * (3 + CC))
        for r in range(NRB):
            act.wait_ge(ln_cent, r + 1)
            nc.scalar.activation(lnsq[:, r, :, :], cacc[:, :, rows(r)], ACT.Square).then_inc(ln_sq, 1)
        wo_high(2)
        for r in range(NRB):
            act.wait_ge(ln_sum, NRB + r + 1)
            nc.scalar.activation(sqs[:, r, :], ps[:, (NRB + r) % 4, 0:RB], ACT.Sqrt, scale=1.0 / CONV_CH,
                                 bias=stat[:, 23:24]).then_inc(ln_root, 1)
        wo_high(3)
        for r in range(NRB):
            act.wait_ge(ln_scaled, r + 1)
            for c in range(CC):
                nc.scalar.activation(cacc[:, c, rows(r)], cacc[:, c, rows(r)], ACT.Silu,
                                     scale=gain[:, G_CN + c:G_CN + c + 1], bias=gain[:, B_CN + c:B_CN + c + 1])\
                    .then_inc(ln_act, 1)
            act.wait_ge(ln_act, CC * (r + 1))
            nc.scalar.activation(n_hi[:, CC:KC, rows(r)], cacc[:, :, rows(r)], ACT.Copy).then_inc(ln_hi, 1)
            if r:
                wo_high(3 + r)

        for o in range(RING, KC):
            act.wait_ge(one_ready, Y_WO + WO_ORDER.index((o - RING, NRB - 1)) + 1)
            wo_high(o)

        def wo_y(tile):
            return Y_WO + WO_ORDER.index(tile)

        squares(2, 0, one_free, 4 + wo_y((7, 0)) + 1)
        norm_root(2, 0, wo_y("sum0"))
        squares(2, 1, one_free, 4 + wo_y((7, 1)) + 1)
        for s in range(4):
            act.wait_ge(one_ready, wo_y((2 + s, 2)) + 1)
            high(N_FF2 + s, (FF2_RING + s) % RING)
            if s == 2:
                norm_root(2, 1, wo_y("sum1"))
        squares(2, 2, one_free, 4 + wo_y((7, 2)) + 1)
        ffn(N_FF2, T_FF2, Y_FF2, 2, FF2_RING, [(N_PLE + x, PLE_RING[PLE_ORDER[x]]) for x in range(4)])

        act.wait_ge(one_ready, Y_PLE - 1)

        def embed_high(r):
            n = N_PLE + PLE_ORDER.index("p0") + r
            act.wait_ge(raw_in[n % RAW], 16 * (n // RAW + 1))
            nc.scalar.activation(hid_hi[:, :, rows(r)], raw[n % RAW][:, 0:VC * RB].rearrange("p (c n) -> p c n", c=VC),
                                 ACT.Copy).then_inc(w_hi, 1)

        embed_high(0)
        embed_high(1)
        squares(3, 2, one_free, 4 + Y_PLE - 1)
        for i, (o, r) in enumerate(PLE_TILES):
            t = T_PLE + i
            act.wait_ge(pair_ready, t + 1)
            act.wait_ge(pair_free, t + 1)
            nc.scalar.activation(gact[:, t % 2, :], ps[:, 2 * (t % 2), 0:RB], ACT.Sigmoid,
                                 bias=gain[:, B_PG + o:B_PG + o + 1]).then_inc(act_gate, 1)
            if i == 0:
                norm_high(3, 1)
                embed_high(2)
            if i in (1, 2):
                x = ("g3", "pp1")[i - 1]
                high(N_PLE + PLE_ORDER.index(x), PLE_RING[x])
            if i == 3:
                norm_root(3, 2, Y_PLE - 1, then_high=False)
            if i == 5:
                norm_high(3, 2)
            if 8 <= i < 12:
                x = f"g{i - 4}"
                high(N_PLE + PLE_ORDER.index(x), PLE_RING[x])
            if i in (15, 19):
                squares(4, (i - 15) // 4, ple_added, i + 1)
            if i in (17, 21):
                norm_root(4, (i - 17) // 4, Y_PLE + (i - 17) // 4)
        squares(4, 2, ple_added, 24)
        norm_root(4, 2, Y_PLE + 2)

    @block.vector
    def _(ve):
        step = Tally(ve, dve_step)

        def low(n, ring, add=0):
            ve.wait_ge(w_hi, n + 1 + add)
            nc.vector.tensor_tensor(wlo[ring][:, :], raw[n % RAW][:, :], whi[ring][:, :].bitcast(f32), ALU.subtract)\
                .then_inc(w_split, 1)

        def norm_sum(norm, r, y):
            ve.wait_ge(sq_ready, NRB * norm + r + 1)
            if y is not None:
                ve.wait_ge(one_ready, y + 1)
            nc.vector.tensor_reduce(red[:, :], sq[:, :, :].rearrange("p c n -> p n c"), AX.X, ALU.add)\
                .then_inc(sq_summed, 1)

        def norm_recip(norm, r):
            ve.wait_ge(root, NRB * norm + r + 1)
            nc.vector.reciprocal(rstd[:, :], rstd[:, :]).then_inc(one_free, 1)

        def norm_scale(norm, r, y, g0):
            if norm == 4 and r:
                ve.wait_ge(y_out, 16 * r)
            ve.wait_ge(one_free, 4 + y + 1)
            for c in range(KC):
                last = nc.vector.scalar_tensor_tensor(out=n32[:, c, :], in0=h[:, c, rows(r)],
                                                      scalar=gain[:, g0 + c:g0 + c + 1], in1=rstd[:, :],
                                                      op0=ALU.mult, op1=ALU.mult)
            last.then_inc(n32_ready, 1)

        def norm_low(norm, r):
            ve.wait_ge(n_high, NRB * norm + r + 1)
            nc.vector.tensor_tensor(n_lo[:, :, rows(r)], n32[:, :, :], n_hi[:, :, rows(r)].bitcast(f32),
                                    ALU.subtract).then_inc(n_ready, 1)

        def norm_apply(norm, r, y, g0):
            norm_recip(norm, r)
            norm_scale(norm, r, y, g0)
            if norm < 4:
                norm_low(norm, r)

        def add_tile(o, r, y, factor, base=0):
            ve.wait_ge(one_ready, base + (y + 1))
            nc.vector.scalar_tensor_tensor(out=h[:, o, rows(r)], in0=ps[:, 4 + y % 4, 0:RB], scalar=factor,
                                           in1=h[:, o, rows(r)], op0=ALU.mult, op1=ALU.add).then_inc(one_free, 1)

        def ffn(n0, t0, y0, norm, ring0, nexts, g_this, g_next):
            t0h = t0 - (CC * NRB if t0 else 0)

            def body(g, first, last):
                def hidden(t):
                    r, f = divmod(t, 2)
                    ve.wait_ge(act_gate, 6 * g + (t0 + t + 1))
                    nc.vector.tensor_tensor(prod[:, t % 2, :], gact[:, t % 2, :],
                                            ps[:, 2 * ((t0 + t) % 2) + 1, 0:RB], ALU.mult).then_inc(pair_free, 1)
                    ve.wait_ge(hid_high, 6 * g + (t0h + t + 1))
                    nc.vector.tensor_tensor(hid_lo[:, f, rows(r)], prod[:, t % 2, :],
                                            hid_hi[:, f, rows(r)].bitcast(f32), ALU.subtract).then_inc(hid_ready, 1)

                def next_low(i):
                    if not last:
                        low(n0 + 6 + i, (ring0 + i) % RING, 6 * g)
                    elif i < len(nexts):
                        low(*nexts[i])

                def adds(r, lo, hi):
                    for o in range(lo, hi):
                        sums = (r > 0) + (r == NRB - 1 and o >= 4) if last else 0
                        add_tile(o, r, y0 + KC * r + sums + o, 0.5, DOWN * g)

                yl = y0 + DOWN * g
                hidden(0)
                low(n0 + 4, (ring0 + 4) % RING, 6 * g)
                if first:
                    norm_recip(norm, 2)
                    low(n0 + 5, (ring0 + 5) % RING)
                    norm_scale(norm, 2, y0 - 1, g_this)
                hidden(1)
                if first:
                    norm_low(norm, 2)
                else:
                    low(n0 + 5, (ring0 + 5) % RING, 6 * g)
                hidden(2)
                adds(0, 0, KC)
                if last:
                    norm_sum(norm + 1, 0, None)
                hidden(3)
                if last:
                    norm_recip(norm + 1, 0)
                    norm_scale(norm + 1, 0, yl + KC, g_next)
                hidden(4)
                if not last:
                    next_low(0)
                adds(1, 0, 4)
                if last:
                    norm_low(norm + 1, 0)
                    next_low(0)
                next_low(1)
                adds(1, 4, KC)
                if last:
                    norm_sum(norm + 1, 1, yl + KC)
                hidden(5)
                adds(2, 0, 4)
                if last:
                    norm_recip(norm + 1, 1)
                next_low(2)
                adds(2, 4, KC)
                next_low(3)

            body(0, True, False)
            with ve.Fori(1, GROUPS - 1) as g:
                body(g, False, False)
            body(GROUPS - 1, False, True)

        norm_sum(0, 0, None)
        low(N_FF1, 0)
        low(N_FF1 + 1, 1)
        ve.wait_ge(const_in, 5 * 16)
        norm_recip(0, 0)
        norm_scale(0, 0, Y_NORM1, G_FF1)
        norm_sum(0, 1, Y_NORM1)
        norm_low(0, 0)
        low(N_FF1 + 2, 2)
        low(N_FF1 + 3, 3)
        norm_apply(0, 1, Y_NORM1 + 1, G_FF1)
        norm_sum(0, 2, Y_NORM1 + 1)
        ffn(N_FF1, T_FF1, Y_FF1, 0, 0, [(N_WIN + j, j) for j in range(4)], G_FF1, G_MIX)

        norm_scale(1, 1, Y_WIN - 5, G_MIX)
        norm_low(1, 1)
        norm_sum(1, 2, Y_WIN - 5)
        for j in (4, 5):
            low(N_WIN + j, j)

        def take(j, r):
            yy = Y_WIN + WIN_SINGLES.index((j, r))
            ve.wait_ge(one_ready, yy + 1)
            dst = (cq[:, j, rows(r)] if j < QC else ckv[:, j - QC, rows(r)] if j < QC + VC else kpe[:, rows(r)])
            src = ps[:, 4 + yy % 4, 0:RB] if j < QC + VC else ps[0:ROPE, 4 + yy % 4, 0:RB]
            nc.vector.tensor_copy(dst, src).then_inc(one_free, 1)

        def lat_sum(m, r):
            ve.wait_ge(lat_sq, NRB * m + r + 1)
            for x in range(1, (QC, VC)[m]):
                last = nc.vector.tensor_tensor(sqs[:, 0, :], sqs[:, 0, :], sqs[:, x, :], ALU.add)
                if x < (QC, VC)[m] - 1:
                    step.hit(last)
                    step.sync()
            last.then_inc(lat_red, 1)

        def lat_apply(m, r):
            src, c, g0 = ((cq, QC, G_Q), (ckv, VC, G_KV))[m]
            yy = Y_LAT + NRB * m + r
            ve.wait_ge(lat_root, NRB * m + r + 1)
            nc.vector.reciprocal(sqs[:, 1, :], sqs[:, 1, :]).then_inc(one_free, 1)
            ve.wait_ge(one_free, 4 + yy + 1)
            for x in range(c):
                last = nc.vector.scalar_tensor_tensor(out=src[:, x, rows(r)], in0=src[:, x, rows(r)],
                                                      scalar=gain[:, g0 + x:g0 + x + 1], in1=sqs[:, 1, :],
                                                      op0=ALU.mult, op1=ALU.mult)
            last.then_inc(lat_norm, 1)

        def glu(c, r):
            t = T_WIN + c * NRB + r
            ve.wait_ge(act_gate, t + 1)
            b = 2 * (t % 2)
            if r < NRB - 1:
                v = vext[:, c, HIST + r * RB:HIST + (r + 1) * RB]
                nc.vector.tensor_tensor(v, v, ps[:, b, 0:RB], ALU.mult).then_inc(pair_free, 1)
            else:
                v = vext[:, c, HIST + r * RB:HIST + SEQ]
                nc.vector.tensor_tensor(v, v, ps[:, b, 0:SEQ - r * RB], ALU.mult)
                v = vs[:, c, :, HIST:HIST + DEC_T]
                nc.vector.tensor_tensor(v, v, ps[:, b, SEQ - r * RB:RB].rearrange("p (b t) -> p b t", b=DEC_B),
                                        ALU.mult).then_inc(pair_free, 1)

        for tile in WIN_SINGLES:
            if tile == "sum":
                norm_apply(1, 2, Y_WIN + 4, G_MIX)
                continue
            take(*tile)
            if tile[0] == 4:
                low(N_WIN + 6 + tile[1], tile[1])
        for j in range(9, 12):
            low(N_WIN + j, j % RING)
        lat_sum(0, 0)
        for x in range(CC * NRB):
            glu(*divmod(x, NRB))
            if x == 2:
                for j in (12, 13):
                    low(N_WIN + j, j % RING)
            if 0 <= x - 2 < 2 * NRB:
                lat_apply(*divmod(x - 2, NRB))
                if x - 1 < 2 * NRB:
                    lat_sum(*divmod(x - 1, NRB))

        swap = [(i + ROPE // 2) % ROPE for i in range(ROPE)]
        ksw = sqs[0:ROPE, :, :].rearrange("p c n -> p (c n)")
        ve.wait_ge(trig_in, 16)
        ve.wait_ge(lat_norm, 2 * NRB)
        step.hit(nc.vector.stream_shuffle(ksw, kpe[:, :], swap))
        step.sync()
        step.hit(nc.vector.tensor_tensor(kpe[:, :], kpe[:, :], cs[0:ROPE, 0, :], ALU.mult))
        step.hit(nc.vector.tensor_tensor(ksw, ksw, cs[0:ROPE, 1, :], ALU.mult))
        step.sync()
        step.hit(nc.vector.tensor_tensor(kpe[:, :], kpe[:, :], ksw, ALU.add))
        step.sync()
        S0, S1 = ckv[:, 0, SEQ:ROWS], ckv[:, 1, SEQ:ROWS]
        for dst, src in ((newT[:, 0, :], S0[0:K96]), (newT[0:32, 1, :], S0[K96:P]), (newT[32:64, 1, :], S1[0:32]),
                         (newT[64:K96, 1, :], S1[32:64]), (newT[0:64, 2, :], S1[64:P]),
                         (newT[64:K96, 2, :], kpe[:, SEQ:ROWS])):
            nc.vector.tensor_copy(dst, src)
        nc.vector.tensor_copy(k[NOPE:NOPE + ROPE, 0, :], kpe[:, 0:SEQ])
        nc.vector.tensor_copy(k[NOPE:NOPE + ROPE, 1, :], kpe[:, 0:SEQ]).then_inc(kpe_ready, 1)
        ve.wait_ge(ready0, 3)
        ve.wait_ge(hist_in, 16 * CC)

        per_pair = 3 + 2 + 2 * PAIR_TAPS + 16 * 2
        for c in (0, 1):
            both, w, b = tap_operands(c, 0)
            for acc, src, _ in both:
                step.hit(nc.vector.tensor_scalar(acc, src, w, b, ALU.mult, ALU.add))
        done_before = step.n
        with ve.Fori(0, PAIRS) as p:
            step.off = per_pair * p

            def pair_taps(first, n):
                for t in range(first, first + n):
                    c, x = t % 2, t // 2 + 1
                    if t >= 2:
                        ve.wait_ge(dve_step, step.off + tap_at[c])
                    w = gain[:, bass.ds(PAIR_TAPS * p + (W_CONV + c * TAPS + x), 1)]
                    out_s = cacc[:, c, SEQ:ROWS].rearrange("p (b t) -> p b t", b=DEC_B)
                    nc.vector.scalar_tensor_tensor(out=cacc[:, c, 0:SEQ], in0=vext[:, c, bass.ds(PAIR_TAPS * p + x, SEQ)],
                                                   scalar=w, in1=cacc[:, c, 0:SEQ], op0=ALU.mult, op1=ALU.add)
                    step.hit(nc.vector.scalar_tensor_tensor(out=out_s, in0=vs[:, c, :, bass.ds(PAIR_TAPS * p + x, DEC_T)],
                                                            scalar=w, in1=out_s, op0=ALU.mult, op1=ALU.add))
                    tap_at[c] = step.n

            tap_at = {}
            ve.wait_ge(dve_step, step.off + done_before)
            pair_taps(0, PAIR_TAPS)
            ve.wait_ge(proj_free, Z_PROJ * p + (4 + 3))
            nc.vector.memset(stat[:, 22:23], 0.0)
            step.hit(nc.vector.stream_shuffle(qsw[:, :], qraw[:, :], swap))
            step.sync()
            step.hit(nc.vector.tensor_tensor(qraw[:, :], qraw[:, :], cs[:, 0, :], ALU.mult))
            step.hit(nc.vector.tensor_tensor(qsw[:, :], qsw[:, :], cs[:, 1, :], ALU.mult))
            step.sync()
            nc.vector.tensor_tensor(q[NOPE:NOPE + ROPE, 0, :], qraw[0:ROPE, :], qsw[0:ROPE, :], ALU.add)
            nc.vector.tensor_tensor(q[NOPE:NOPE + ROPE, 1, :], qraw[ROPE:2 * ROPE, :], qsw[ROPE:2 * ROPE, :],
                                    ALU.add).then_inc(rope_done, 1)
            ve.wait_ge(rope_done, p + 1)
            for hh in range(2):
                step.hit(nc.vector.tensor_copy(qabs[NOPE:K96, 2, :, bass.ds(8 * p + 4 * hh, 4)],
                                               q[NOPE:NOPE + ROPE, hh, SEQ:ROWS].rearrange("p (b t) -> p b t", b=DEC_B)))
            pair_taps(PAIR_TAPS, PAIR_TAPS)

            def untile(i):
                for x in range(1 if i < 4 else 2):
                    ve.wait_ge(t5_ready, 12 * p + (kap(i) + x + 1))
                    if i < 4:
                        nc.vector.tensor_copy(PT[:, i % 2, 1, 0:(i + 1) * P], ps[:, 5, 0:(i + 1) * P])\
                            .then_inc(t5_done, 1)
                    else:
                        nc.vector.tensor_copy(PT[:, i % 2, x, 512:(i + 1) * P], ps[:, 5, 0:(i - 3) * P])\
                            .then_inc(t5_done, 1)

            def low_av(i):
                ve.wait_ge(av_hi, QB * p + (i + 1))
                nc.vector.tensor_tensor(n_lo[:, p, i * P:(i + 1) * P], ps[:, 6 + i % 2, 0:P],
                                        n_hi[:, p, i * P:(i + 1) * P].bitcast(f32), ALU.subtract).then_inc(av_lo, 1)

            for i in range(QB):
                for hh in range(2):
                    u = 2 * i + hh
                    ve.wait_ge(s_ready, 2 * QB * p + (u + 1))
                    diag = psf[:, 1024 * hh + i * P:1024 * hh + (i + 1) * P]
                    step.hit(nc.vector.tensor_tensor(diag, diag, tri[:, :], ALU.add))
                    step.sync()
                    nc.vector.reduce_max(stat[:, 4 + u % 4:5 + u % 4], psf[:, 1024 * hh:1024 * hh + (i + 1) * P], AX.X,
                                         negate=True).then_inc(s_max, 1)
                if i:
                    untile(i - 1)
                for hh in range(2):
                    u = 2 * i + hh
                    ve.wait_ge(s_free, 2 * QB * p + (2 + u + 1))
                    step.hit(nc.vector.reciprocal(stat[:, 12 + u % 4:13 + u % 4], stat[:, 8 + u % 4:9 + u % 4]))
                    step.sync()
                    w = (i + 1) * P
                    nc.vector.tensor_scalar(pr[:, i % 2, hh, 0:w], pr[:, i % 2, hh, 0:w],
                                            stat[:, 12 + u % 4:13 + u % 4], None, ALU.mult).then_inc(p_norm, 1)
                if i >= 2:
                    low_av(i - 2)
            untile(QB - 1)
            low_av(QB - 2)
            low_av(QB - 1)
            assert step.n - done_before == per_pair, (step.n - done_before, per_pair)
        step.off = 0
        step.n = done_before + per_pair * PAIRS
        step.sync()

        taps = [(c, x) for x in range(1 + PAIR_TAPS * PAIRS, TAPS) for c in (0, 1)]
        taps += [(2, x) for x in range(POOL_FIRST, TAPS)]
        written = [0, 0, 0]

        def convolve(n):
            for c, x in taps[:n]:
                if written[c]:
                    ve.wait_ge(dve_step, written[c])
                elif c == 2:
                    ve.wait_ge(pool_tap, 2 * POOL_FIRST - 1)
                both, w, b = tap_operands(c, x)
                for acc, src, _ in both:
                    last = nc.vector.scalar_tensor_tensor(out=acc, in0=src, scalar=w, in1=acc, op0=ALU.mult,
                                                          op1=ALU.add)
                step.hit(last)
                written[c] = step.n
            del taps[:n]

        def sample_max(n):
            m, e = n % 2, (n - 1) % 2
            ve.wait_ge(ss_ready, n + 1)
            bank = ps[:, 4 + m, :]
            w = TOK
            if n % TILES == TILES - 1:
                w += NEW
                step.hit(nc.vector.tensor_tensor(bank[:, TOK:w], bank[:, TOK:w], smask[:, n // TILES, :], ALU.add))
                step.sync()
            if n >= 1:
                ve.wait_ge(ss_exp, n)
            if n % TILES:
                step.hit(nc.vector.reduce_max(stat[:, 10:11], bank[:, 0:w], AX.X, negate=True))
                step.sync()
                nc.vector.tensor_tensor(stat[:, m:m + 1], stat[:, 10:11], stat[:, e:e + 1], ALU.min).then_inc(ss_max, 1)
            else:
                nc.vector.reduce_max(stat[:, m:m + 1], bank[:, 0:w], AX.X, negate=True).then_inc(ss_max, 1)

        def accumulate(n):
            m, e = n % 2, (n - 1) % 2
            ve.wait_ge(c_used, n + 1)
            alpha, total, before = (stat[:, x:x + 1] for x in (4 + m, 8 + m, 8 + e))
            if n % TILES:
                step.hit(nc.vector.scalar_tensor_tensor(out=total, in0=before, scalar=alpha,
                                                        in1=stat[:, 6 + m:7 + m], op0=ALU.mult, op1=ALU.add))
                nc.vector.scalar_tensor_tensor(out=olat[:, :], in0=olat[:, :], scalar=alpha, in1=ps[:, 7, 0:KV_RANK],
                                               op0=ALU.mult, op1=ALU.add).then_inc(acc_done, 1)
            else:
                step.hit(nc.vector.tensor_copy(total, stat[:, 6 + m:7 + m]))
                nc.vector.tensor_copy(olat[:, :], ps[:, 7, 0:KV_RANK]).then_inc(acc_done, 1)
            ve.wait_ge(acc_done, n + 1)
            if n % TILES == TILES - 1:
                step.sync()
                step.hit(nc.vector.reciprocal(stat[:, 12:13], total))
                step.sync()
                nc.vector.tensor_scalar(olat[:, :], olat[:, :], stat[:, 12:13], None, ALU.mult).then_inc(olat_ready, 1)

        def take_outputs(grp):
            ve.wait_ge(ot_ready, grp + 2)
            nc.vector.tensor_copy(olatT[:, :, grp, :], ps[:, 7, KV_RANK:2 * KV_RANK].rearrange("p (c n) -> p c n", c=VC))\
                .then_inc(ot_done, 1)

        ve.wait_ge(ot_ready, 1)
        nc.vector.tensor_copy(ckvnew[:, :], ps[0:NEW, 7, KV_RANK:2 * KV_RANK]).then_inc(ot_done, 1)
        for n in range(LAST + 3):
            if n <= LAST:
                latents_out(ve, nc.vector.tensor_copy, n, 1)
            convolve(1)
            if n == TILES + 2:
                take_outputs(0)
            if n >= 2:
                accumulate(n - 2)
            if n <= LAST:
                latents_out(ve, nc.vector.tensor_copy, n, 3)
            if 1 <= n <= LAST + 1:
                sample_max(n - 1)
            convolve(1 + (n % 4 == 3))
        take_outputs(1)
        convolve(len(taps))
        ve.wait_ge(av_hi, PAIRS * QB + 1)
        nc.vector.tensor_tensor(n_lo[:, 0:PAIRS, SEQ:ROWS], ps[:, 6, 0:PAIRS * NEW].rearrange("p (a n) -> p a n", a=PAIRS),
                                n_hi[:, 0:PAIRS, SEQ:ROWS].bitcast(f32), ALU.subtract).then_inc(av_lo, 1)

        def wo_low(o):
            low(N_WO + o, (N_WO + o) % RING)

        def centre(r):
            c = cacc[:, :, rows(r)]
            ve.wait_ge(ln_sum, r + 1)
            nc.vector.scalar_tensor_tensor(out=c, in0=ps[:, r:r + 1, 0:RB].broadcast_to([P, CC, RB]),
                                           scalar=-1.0 / CONV_CH, in1=c, op0=ALU.mult, op1=ALU.add).then_inc(ln_cent, 1)

        def scale_rows(r):
            c = cacc[:, :, rows(r)]
            ve.wait_ge(ln_root, r + 1)
            nc.vector.reciprocal(sqs[:, r, :], sqs[:, r, :]).then_inc(ln_recip, 1)
            ve.wait_ge(ln_recip, r + 1)
            nc.vector.tensor_tensor(c, c, sqs[:, r:r + 1, :].broadcast_to([P, CC, RB]), ALU.mult).then_inc(ln_scaled, 1)

        def conv_low(r):
            ve.wait_ge(ln_hi, r + 1)
            nc.vector.tensor_tensor(n_lo[:, CC:KC, rows(r)], cacc[:, :, rows(r)],
                                    n_hi[:, CC:KC, rows(r)].bitcast(f32), ALU.subtract).then_inc(ln_lo, 1)

        step.sync()
        ve.wait_ge(pool_tap, 2 * POOL_FIRST - 1 + 2 * TAPS - 1)
        nc.vector.memset(stat[:, 22:23], 0.0).then_inc(conv_done, 1)
        wo_low(0)
        wo_low(1)
        for r in range(NRB):
            centre(r)
        scale_rows(0)
        wo_low(2)
        scale_rows(1)
        conv_low(0)
        scale_rows(2)
        wo_low(3)
        conv_low(1)
        wo_low(4)
        conv_low(2)
        wo_low(5)


        def wo_y(tile):
            return Y_WO + WO_ORDER.index(tile)

        for tile in WO_ORDER:
            if tile == "sum0":
                norm_apply(2, 0, wo_y("sum0"), G_FF2)
                continue
            if tile == "sum1":
                norm_apply(2, 1, wo_y("sum1"), G_FF2)
                continue
            add_tile(*tile, wo_y(tile), 1.0)
            if tile in ((0, 2), (1, 2)):
                low(N_WO + RING + tile[0], (N_WO + tile[0]) % RING)
            if tile == (7, 0):
                norm_sum(2, 0, None)
            if tile == (7, 1):
                norm_sum(2, 1, wo_y("sum0"))
            if tile in ((3, 2), (4, 2), (5, 2), (6, 2)):
                s = tile[0] - 3
                low(N_FF2 + s, (FF2_RING + s) % RING)
        norm_sum(2, 2, wo_y("sum1"))
        ffn(N_FF2, T_FF2, Y_FF2, 2, FF2_RING, [(N_PLE + x, PLE_RING[PLE_ORDER[x]]) for x in range(4)], G_FF2, G_PLE)

        def embed_low(r):
            n = N_PLE + PLE_ORDER.index("p0") + r
            ve.wait_ge(w_hi, n + 1)
            nc.vector.tensor_tensor(hid_lo[:, :, rows(r)], raw[n % RAW][:, 0:VC * RB].rearrange("p (c n) -> p c n", c=VC),
                                    hid_hi[:, :, rows(r)].bitcast(f32), ALU.subtract).then_inc(w_split, 1)

        embed_low(0)
        embed_low(1)
        norm_scale(3, 1, Y_PLE - 6, G_PLE)
        for i, (o, r) in enumerate(PLE_TILES):
            t = T_PLE + i
            ve.wait_ge(act_gate, t + 1)
            nc.vector.tensor_tensor(prod[:, t % 2, :], gact[:, t % 2, :], ps[:, 2 * (t % 2) + 1, 0:RB], ALU.mult)\
                .then_inc(pair_free, 1)
            ve.wait_ge(pair_free, 2 + t + 1)
            nc.vector.tensor_tensor(h[:, o, rows(r)], h[:, o, rows(r)], prod[:, t % 2, :], ALU.add)\
                .then_inc(ple_added, 1)
            if i == 0:
                embed_low(2)
                norm_low(3, 1)
            if i in (1, 2):
                x = ("g3", "pp1")[i - 1]
                low(N_PLE + PLE_ORDER.index(x), PLE_RING[x])
            if i == 2:
                norm_sum(3, 2, Y_PLE - 6)
            if i == 3:
                norm_recip(3, 2)
            if i == 4:
                norm_scale(3, 2, Y_PLE - 1, G_PLE)
            if i == 6:
                norm_low(3, 2)
            if 8 <= i < 12:
                x = f"g{i - 4}"
                low(N_PLE + PLE_ORDER.index(x), PLE_RING[x])
            if i in (15, 19):
                norm_sum(4, (i - 15) // 4, None if i == 15 else Y_PLE)
            if i in (17, 21):
                norm_recip(4, (i - 17) // 4)
            if i in (18, 22):
                norm_scale(4, (i - 18) // 4, Y_PLE + (i - 18) // 4, G_FIN)
        norm_sum(4, 2, Y_PLE + 1)
        norm_apply(4, 2, Y_PLE + 2, G_FIN)

    ctx.close()


def kernel(x_prompt, x_sample, cache_ckv, cache_kpe, state_conv, page_table, p_prompt, p_sample,
           g_ff1, w1_gate, w1_up, w1_down, g_mix, w_in, g_q, w_q_up, g_kv, w_uk, w_uv,
           conv_w, conv_b, g_cn, b_cn, w_o, g_ff2, w2_gate, w2_up, w2_down,
           g_ple, w_pg, b_pg, w_pp, g_final):
    import numpy as np
    import concourse.bacc as bacc
    from concourse.bass_utils import run_bass_kernel_spmd

    f = np.float32

    def A(x):
        return np.asarray(x)

    def by_chunk(v):
        return A(v).reshape(-1, P).T

    def cols(w):
        w = A(w)
        kk, nn = w.shape[0] // P, w.shape[1] // P
        return w.reshape(kk, P, nn, P).transpose(2, 1, 0, 3).reshape(nn, P, kk * P)

    def ffn_slots(wg, wu, wd):
        g, u, d = cols(wg[0]), cols(wu[0]), A(wd[0]).reshape(-1, P, D_MODEL)
        s = np.stack([g[0::2], u[0::2], g[1::2], u[1::2], d[0::2], d[1::2]], axis=1)
        return s.reshape(-1, P, 1024)

    wi = A(w_in[0])
    o3 = Q_RANK + KV_RANK + ROPE
    lat = np.concatenate([wi[:, :o3], np.zeros((D_MODEL, 6 * P - o3), f)], axis=1)
    ca, cb = cols(wi[:, o3:o3 + CONV_CH]), cols(wi[:, o3 + CONV_CH:])
    win = np.concatenate([cols(lat), np.stack([ca, cb], axis=1).reshape(-1, P, 1024)])
    pT = np.concatenate([A(p_prompt[0, 0]), A(p_sample[0]).reshape(NEW, -1)]).T
    pT = pT.reshape(VC, P, NRB, RB).transpose(2, 1, 0, 3).reshape(NRB, P, VC * RB)
    pT = np.concatenate([pT, np.zeros((NRB, P, 1024 - VC * RB), f)], axis=2)
    wg, wp = cols(w_pg[0]), cols(w_pp[0])
    wp = wp.reshape(2, 4, P, VC * P).transpose(0, 2, 1, 3).reshape(2, P, 1024)
    named = {f"g{i}": wg[i] for i in range(KC)}
    named.update({f"p{i}": pT[i] for i in range(NRB)})
    named.update({f"pp{i}": wp[i] for i in range(2)})
    stream = np.concatenate([ffn_slots(w1_gate, w1_up, w1_down), win, cols(w_o[0]),
                             ffn_slots(w2_gate, w2_up, w2_down), np.stack([named[x] for x in PLE_ORDER])])

    wq = A(w_q_up[0]).reshape(QC, P, PAIRS, 2, NOPE + ROPE)
    pe = wq[..., NOPE:].transpose(2, 1, 0, 3, 4).reshape(PAIRS, P, -1)
    nope = wq[..., :NOPE].transpose(2, 1, 0, 3, 4).reshape(PAIRS, P, -1)
    uk = A(w_uk[0]).reshape(VC, P, PAIRS, 2 * NOPE).transpose(2, 1, 0, 3).reshape(PAIRS, P, -1)
    uv = A(w_uv[0]).reshape(VC, P, PAIRS, 2 * VH).transpose(2, 1, 0, 3).reshape(PAIRS, P, -1)
    ukT = A(w_uk[0]).reshape(KV_RANK, PAIRS, 2, NOPE).transpose(1, 3, 2, 0).reshape(PAIRS, NOPE, -1)
    ukT = np.concatenate([ukT, np.zeros((PAIRS, P - NOPE, ukT.shape[2]), f)], axis=1)
    pairw = np.concatenate([pe, nope, uk, uv, ukT], axis=2)

    xT = np.concatenate([A(x_prompt[0]), A(x_sample).reshape(NEW, -1)]).T
    xT = xT.reshape(KC, P, ROWS).transpose(1, 0, 2)
    hist = A(state_conv[0]).transpose(2, 0, 1).reshape(CC, P, DEC_B, HIST).transpose(1, 0, 2, 3)
    cw = A(conv_w[0]).T.reshape(CC, P, TAPS).transpose(1, 0, 2).reshape(P, -1)
    gains = np.concatenate([by_chunk(g_ff1), by_chunk(g_mix), by_chunk(g_ff2), by_chunk(g_ple), by_chunk(g_final),
                            by_chunk(g_q), by_chunk(g_kv), by_chunk(g_cn), by_chunk(b_cn), by_chunk(conv_b),
                            by_chunk(b_pg), cw], axis=1)

    half = ROPE // 2
    inv = (f(10000.0) ** (-np.arange(half, dtype=f) / f(half))).astype(f)
    pos = np.concatenate([np.arange(SEQ), np.tile(PAST + np.arange(DEC_T), DEC_B)]).astype(f)
    ang = (pos[:, None] * inv[None, :]).astype(f).T
    cos, sin = np.cos(ang), np.sin(ang)
    trig = np.stack([np.tile(np.concatenate([cos, cos]), (2, 1)), np.tile(np.concatenate([-sin, sin]), (2, 1))], axis=1)
    tri = np.where(np.arange(P)[:, None] >= np.arange(P)[None, :], 0.0, -1e30).astype(f)
    row = np.arange(P)
    smask = np.full((P, 2, NEW), -1e30, f)
    for grp in range(2):
        for c in range(NEW):
            ok = (4 * grp + row // TH == c // DEC_T) & (row % DEC_T >= c % DEC_T)
            smask[ok, grp, c] = 0.0

    cache = np.concatenate([A(cache_ckv[0]), A(cache_kpe[0])], axis=2)
    wuv = A(w_uv[0]).reshape(VC, P, -1).transpose(1, 0, 2)

    ins = dict(wstream=stream, pairw=pairw, xT=xT, hist=hist, gains=gains, trig=trig.astype(f),
               ident=np.eye(P, dtype=f), tri=tri, smask=smask, cache=cache, wuv=wuv,
               ptab=A(page_table).reshape(1, -1))
    outs = dict(yT=(P, KC, ROWS), ckvT=(P, VC, ROWS), kpeT=(ROPE, ROWS), convp=(P, CC, HIST),
                convs=(P, CC, DEC_B, HIST))
    nc = bacc.Bacc("TRN2", target_bir_lowering=False, num_devices=1)
    arrays, args = {}, []
    for name, a in ins.items():
        a = np.ascontiguousarray(a)
        arrays[f"in_{name}"] = a
        args.append(nc.dram_tensor(f"in_{name}", a.shape, mybir.dt.from_np(a.dtype), kind="ExternalInput").ap())
    for name, shape in outs.items():
        args.append(nc.dram_tensor(f"out_{name}", shape, mybir.dt.float32, kind="ExternalOutput").ap())
    program(nc, *args)
    r = run_bass_kernel_spmd(nc, [arrays], core_ids=[0]).results[0]

    def rowsT(a):
        return a.transpose(2, 1, 0).reshape(ROWS, -1)

    y, c_, kp = rowsT(r["out_yT"]), rowsT(r["out_ckvT"]), r["out_kpeT"].T
    cp = r["out_convp"].transpose(2, 1, 0).reshape(1, 1, HIST, CONV_CH)
    cs_ = r["out_convs"].transpose(2, 3, 1, 0).reshape(1, DEC_B, HIST, CONV_CH)
    return (y[:SEQ].reshape(1, SEQ, D_MODEL), y[SEQ:].reshape(DEC_B, DEC_T, D_MODEL),
            c_[:SEQ].reshape(1, 1, SEQ, KV_RANK), kp[:SEQ].reshape(1, 1, SEQ, ROPE), cp,
            c_[SEQ:].reshape(1, DEC_B, DEC_T, KV_RANK), kp[SEQ:].reshape(1, DEC_B, DEC_T, ROPE), cs_)
```
